# Optimizing a Trainium2 kernel written in Bass

```python
import jax, jax.numpy as jnp
from jax import lax
import numpy as np

D_MODEL = 2048
BATCH = 1
SEQ = 256
DEPTH = 2

CHUNK = 64
HEAD_DIM = 64
N_Q_HEADS = 16
N_KV_HEADS = 2
GQA_GROUP = N_Q_HEADS // N_KV_HEADS
ATTN_WIDTH = N_Q_HEADS * HEAD_DIM
KV_WIDTH = N_KV_HEADS * HEAD_DIM
WINDOW = 128
WINDOW_CHUNKS = WINDOW // CHUNK
CONV_CH = D_MODEL - ATTN_WIDTH
CONV_WIDTH = 31
SHORT_CONV_WIDTH = 3
SHORT_CONV_CH = D_MODEL
EVEN_IN = 2 * CONV_CH + ATTN_WIDTH + 2 * KV_WIDTH
ODD_IN = 3 * SHORT_CONV_CH
D_FF = -(-8 * D_MODEL // (3 * 256)) * 256
N_EVEN = (DEPTH + 1) // 2
N_ODD = DEPTH // 2
RMS_EPS = 1e-6
LN_EPS = 1e-5
MASK_VALUE = -1e30

kernel_name = 'hybrid_conformer_swa_shortconv_encoder'

def rms_norm(x, g):
    x32 = x.astype(jnp.float32)
    y = x32 * lax.rsqrt(jnp.mean(x32 * x32, axis=-1, keepdims=True) + RMS_EPS)
    return (y * g.astype(jnp.float32)).astype(x.dtype)

def layer_norm(x, g, b):
    x32 = x.astype(jnp.float32)
    mu = jnp.mean(x32, axis=-1, keepdims=True)
    xc = x32 - mu
    var = jnp.mean(xc * xc, axis=-1, keepdims=True)
    y = xc * lax.rsqrt(var + LN_EPS) * g.astype(jnp.float32) + b.astype(jnp.float32)
    return y.astype(x.dtype)

def causal_depthwise_conv(x, w):
    k, c = w.shape
    return lax.conv_general_dilated(
        x, w[:, None, :].astype(x.dtype), window_strides=(1,), padding=[(k - 1, 0)],
        dimension_numbers=('NWC', 'WIO', 'NWC'), feature_group_count=c)

def alibi_slopes():
    return jnp.exp2(-8.0 * jnp.arange(1, N_Q_HEADS + 1, dtype=jnp.float32) / N_Q_HEADS)

def banded_sink_attention(q, k, v, sinks):
    b, t = q.shape[0], q.shape[1]
    nc = t // CHUNK
    pad = WINDOW - CHUNK
    qc = q.reshape(b, nc, CHUNK, N_KV_HEADS, GQA_GROUP, HEAD_DIM)
    kp = jnp.pad(k, ((0, 0), (pad, 0), (0, 0), (0, 0))).reshape(b, nc + WINDOW_CHUNKS - 1, CHUNK, N_KV_HEADS, HEAD_DIM)
    vp = jnp.pad(v, ((0, 0), (pad, 0), (0, 0), (0, 0))).reshape(b, nc + WINDOW_CHUNKS - 1, CHUNK, N_KV_HEADS, HEAD_DIM)
    kb = jnp.concatenate([kp[:, i:i + nc] for i in range(WINDOW_CHUNKS)], axis=2)
    vb = jnp.concatenate([vp[:, i:i + nc] for i in range(WINDOW_CHUNKS)], axis=2)
    scale = HEAD_DIM ** -0.5
    scores = jnp.einsum('bcqkgd,bcskd->bckgqs', qc, kb).astype(jnp.float32) * scale
    dist = jnp.abs(pad + jnp.arange(CHUNK)[:, None] - jnp.arange(WINDOW)[None, :]).astype(jnp.float32)
    alibi = (-alibi_slopes()[:, None, None] * dist[None]).reshape(N_KV_HEADS, GQA_GROUP, CHUNK, WINDOW)
    key_pos = jnp.arange(nc)[:, None] * CHUNK - pad + jnp.arange(WINDOW)[None, :]
    valid = (key_pos >= 0)[None, :, None, None, None, :]
    scores = jnp.where(valid, scores + alibi, MASK_VALUE)
    sink = sinks.astype(jnp.float32).reshape(N_KV_HEADS, GQA_GROUP)[None, None, :, :, None, None]
    sink_col = jnp.broadcast_to(sink, scores.shape[:-1] + (1,))
    probs = jax.nn.softmax(jnp.concatenate([scores, sink_col], axis=-1), axis=-1)[..., :-1]
    out = jnp.einsum('bckgqs,bcskd->bcqkgd', probs.astype(v.dtype), vb)
    return out.reshape(b, t, ATTN_WIDTH)

def conv_attention_mixer(h, w_in, w_out, dw_w, dw_b, ln_g, ln_b, qn_g, kn_g, sinks):
    b, t, _ = h.shape
    z = h @ w_in
    s1 = CONV_CH
    s2 = 2 * CONV_CH
    s3 = s2 + ATTN_WIDTH
    s4 = s3 + KV_WIDTH
    a, gate, q, k, v = jnp.split(z, [s1, s2, s3, s4], axis=-1)
    u = a * jax.nn.sigmoid(gate)
    u = causal_depthwise_conv(u, dw_w) + dw_b
    u = jax.nn.silu(layer_norm(u, ln_g, ln_b))
    q = rms_norm(q.reshape(b, t, N_Q_HEADS, HEAD_DIM), qn_g)
    k = rms_norm(k.reshape(b, t, N_KV_HEADS, HEAD_DIM), kn_g)
    v = v.reshape(b, t, N_KV_HEADS, HEAD_DIM)
    o = banded_sink_attention(q, k, v, sinks)
    return jnp.concatenate([u, o], axis=-1) @ w_out

def short_conv_mixer(h, w_in, conv_w, w_out):
    bg, cg, u = jnp.split(h @ w_in, 3, axis=-1)
    y = bg * causal_depthwise_conv(cg * u, conv_w)
    return y @ w_out

def swiglu_ffn(h, w_gate, w_up, w_down):
    return (jax.nn.silu(h @ w_gate) * (h @ w_up)) @ w_down

def setup_inputs(seed: int = 0) -> dict:
    key = jax.random.key(seed)
    ks = jax.random.split(key, 20)
    f32 = jnp.float32
    res_scale = (2.0 * DEPTH) ** -0.5

    def nrm(k, shape, s):
        return jax.random.normal(k, shape, f32) * s

    return {
        'x': jax.random.normal(ks[0], (BATCH, SEQ, D_MODEL), f32),
        'mix_norm_g': 1.0 + nrm(ks[1], (DEPTH, D_MODEL), 0.02),
        'ffn_norm_g': 1.0 + nrm(ks[2], (DEPTH, D_MODEL), 0.02),
        'hy_w_in': nrm(ks[3], (N_EVEN, D_MODEL, EVEN_IN), D_MODEL ** -0.5),
        'hy_w_out': nrm(ks[4], (N_EVEN, D_MODEL, D_MODEL), D_MODEL ** -0.5 * res_scale),
        'conv_dw_w': nrm(ks[5], (N_EVEN, CONV_WIDTH, CONV_CH), CONV_WIDTH ** -0.5),
        'conv_dw_b': nrm(ks[6], (N_EVEN, CONV_CH), 0.02),
        'conv_ln_g': 1.0 + nrm(ks[7], (N_EVEN, CONV_CH), 0.02),
        'conv_ln_b': nrm(ks[8], (N_EVEN, CONV_CH), 0.02),
        'q_norm_g': 1.0 + nrm(ks[9], (N_EVEN, HEAD_DIM), 0.02),
        'k_norm_g': 1.0 + nrm(ks[10], (N_EVEN, HEAD_DIM), 0.02),
        'attn_sinks': nrm(ks[11], (N_EVEN, N_Q_HEADS), 1.0),
        'sc_w_in': nrm(ks[12], (N_ODD, D_MODEL, ODD_IN), D_MODEL ** -0.5),
        'sc_conv_w': nrm(ks[13], (N_ODD, SHORT_CONV_WIDTH, SHORT_CONV_CH), SHORT_CONV_WIDTH ** -0.5),
        'sc_w_out': nrm(ks[14], (N_ODD, SHORT_CONV_CH, D_MODEL), SHORT_CONV_CH ** -0.5 * res_scale),
        'ffn_w_gate': nrm(ks[15], (DEPTH, D_MODEL, D_FF), D_MODEL ** -0.5),
        'ffn_w_up': nrm(ks[16], (DEPTH, D_MODEL, D_FF), D_MODEL ** -0.5),
        'ffn_w_down': nrm(ks[17], (DEPTH, D_FF, D_MODEL), D_FF ** -0.5 * res_scale),
    }

def reference(x, mix_norm_g, ffn_norm_g, hy_w_in, hy_w_out, conv_dw_w, conv_dw_b, conv_ln_g,
              conv_ln_b, q_norm_g, k_norm_g, attn_sinks, sc_w_in, sc_conv_w, sc_w_out,
              ffn_w_gate, ffn_w_up, ffn_w_down):
    for layer in range(DEPTH):
        h = rms_norm(x, mix_norm_g[layer])
        i = layer // 2
        if layer % 2 == 0:
            x = x + conv_attention_mixer(h, hy_w_in[i], hy_w_out[i], conv_dw_w[i], conv_dw_b[i],
                                         conv_ln_g[i], conv_ln_b[i], q_norm_g[i], k_norm_g[i],
                                         attn_sinks[i])
        else:
            x = x + short_conv_mixer(h, sc_w_in[i], sc_conv_w[i], sc_w_out[i])
        h = rms_norm(x, ffn_norm_g[layer])
        x = x + swiglu_ffn(h, ffn_w_gate[layer], ffn_w_up[layer], ffn_w_down[layer])
    return x


_drawn_inputs = setup_inputs


def setup_inputs(seed=0):
    import zlib

    import numpy as np

    out = dict(_drawn_inputs(seed))
    spreads = {}
    factors = {'mix_norm_g': 3.378,
     'ffn_norm_g': 4.727,
     'conv_dw_b': 4.867,
     'conv_ln_g': 8.0,
     'conv_ln_b': 8.0,
     'q_norm_g': 8.0,
     'k_norm_g': 8.0,
     'attn_sinks': 3.106}
    for name, (base, spread) in spreads.items():
        noise = np.random.default_rng([zlib.crc32(name.encode()), seed]).standard_normal(out[name].shape)
        drawn = base * np.exp(spread * noise) if base else spread * noise
        out[name] = __import__('jax').numpy.asarray(drawn.astype(out[name].dtype))
    for name, factor in factors.items():
        out[name] = (out[name] * factor).astype(out[name].dtype)
    return out
```

```python
from contextlib import ExitStack

import concourse.bass as bass
from concourse import mybir

F32 = mybir.dt.float32
F32R = mybir.dt.float32r
ALU = mybir.AluOpType
ACT = mybir.ActivationFunctionType
AX_X = mybir.AxisListType.X

P = 128
NB = 512
RING = 4
SLOT_K = 2
RMS_EPS = 1e-6
LN_EPS = 1e-5


def ds(start, size):
    return bass.ds(start, size)


class Plan:

    def __init__(self):
        self.slots = 0
        self.pair_uses = [0, 0, 0]
        self.jobs = {}
        self.groups = {}
        self.bank_uses = [0, 0]
        self.highs = {}
        self.lows = {}

    def job(self, name, pair, k_tiles):
        self.jobs[name] = (self.slots, pair, self.pair_uses[pair])
        self.slots += k_tiles // SLOT_K
        self.pair_uses[pair] += 1

    def group(self, name, high=False, low=False):
        n = len(self.groups)
        self.groups[name] = (n, n % 2, self.bank_uses[n % 2])
        self.bank_uses[n % 2] += 1
        if high:
            self.split(name, low)

    def split(self, name, low=True):
        self.highs[name] = len(self.highs)
        if low:
            self.lows[name] = len(self.lows)


def encoder_kernel(nc, x_in, w_in, w_out, sc_in, sc_out, w_gate, w_up, w_down, cols_in, tables_in, out):
    SEQ, D = x_in.shape
    FF = w_gate.shape[2]
    DEPTH = w_gate.shape[0]
    TT = SEQ // P
    KD = D // P
    KF = FF // P
    NJ = D // NB
    NF = FF // NB
    BK = NB // P
    CHUNK, HD, HQ, HKV = 64, 64, 16, 2
    GQ = HQ // HKV
    AW = HQ * HD
    CC = D - AW
    KC = CC // P
    TAPS = 31
    PAD = TAPS - 1
    KVW = HKV * HD
    assert TT == 2 and DEPTH == 2 and KVW == P and CC == 2 * NB and AW == 2 * NB
    SD = KD // SLOT_K
    SF = KF // SLOT_K
    SH = SD // 2

    MIXG, FFNG = 0, DEPTH * KD
    DWW = FFNG + DEPTH * KD
    DWB = DWW + KC * TAPS
    LNG = DWB + KC
    LNB = LNG + KC
    SCW = LNB + KC
    QG = SCW + 3 * KD
    KG = QG + HD
    SINK = KG + HD
    NCOLS = SINK + HQ

    plan = Plan()
    for b in range(NJ):
        for t in range(TT):
            plan.group(("x", 0, b, t), high=True, low=True)
    for n, name in enumerate(("g0", "a0", "g1", "a1", "q0", "q1", "kv")):
        plan.job(name, n % 2, KD)
    for c in range(2):
        for t in range(TT):
            plan.group(("u", c, t))
    for t in range(TT):
        for half in range(2):
            plan.group(("qT", t, half))
    plan.group("kT")

    def plan_scores(hh):
        for r in range(4):
            plan.group(("sc", hh, r))

    def plan_probs(hh):
        for r in range(2 * (1 + hh // 2)):
            plan.group(("p", hh, r))

    def plan_heads_out(t):
        for r in range(2):
            plan.group(("o", t, r), high=True)

    plan_scores(0), plan_scores(1), plan_probs(0), plan_scores(2), plan_probs(1), plan_heads_out(0)
    plan_scores(3), plan_probs(2), plan_probs(3), plan_heads_out(1)
    for nb in range(NJ):
        plan.job(("attn_out", nb), nb % 2, KD // 2)
    plan.group("mean")
    plan.group("var")
    for q in range(KC // 2):
        plan.split(("ln", q))
    for nb in range(NJ):
        plan.job(("conv_out", nb), nb % 2, KD // 2)
    for b in range(NJ):
        for t in range(TT):
            plan.group(("x", 1, b, t), high=True, low=True)

    def plan_ffn(layer, norm_after):
        for i in range(NF):
            plan.job(("gate", layer, i), 0, KD)
            plan.job(("up", layer, i), 1, KD)
            for t in range(TT):
                plan.group(("y", layer, i, t), high=True)
        for nb in range(NJ):
            plan.job(("down", layer, nb), nb % 2, KF)
        if norm_after is not None:
            for b in range(NJ):
                for t in range(TT):
                    plan.group(("x", norm_after, b, t), high=True, low=True)

    plan_ffn(0, 2)
    for j in range(NJ):
        plan.job(("cg", j), 0, KD)
        plan.job(("cu", j), 1, KD)
        plan.job(("bg", j), 2, KD)
        for t in range(TT):
            plan.group(("c", j, t))
        for t in range(TT):
            plan.group(("z", j, t), high=True, low=True)
    for nb in range(NJ):
        plan.job(("sc_out", nb), nb % 2, KD)
    for b in range(NJ):
        for t in range(TT):
            plan.group(("x", 3, b, t), high=True, low=True)
    plan_ffn(1, None)
    JOB, GROUP, HIGH, LOW, SLOTS = plan.jobs, plan.groups, plan.highs, plan.lows, plan.slots
    assert SLOTS % RING == 0
    assert all(JOB[("gate", la, 0)][0] % RING == 0 for la in range(DEPTH)) and JOB[("cg", 0)][0] % RING == 0

    with ExitStack() as ctx:
        def sb(name, shape, dt=F32, stack=ctx):
            return stack.enter_context(nc.sbuf_tensor(name, shape, dt))

        def sem(name):
            return ctx.enter_context(nc.semaphore(name))

        xs = sb("xs", [P, TT, D])
        xT_hi = sb("xT_hi", [P, KD, SEQ], F32R)
        xT_lo = sb("xT_lo", [P, KD, SEQ], F32R)
        w_raw = sb("w_raw", [P, RING, SLOT_K, NB])
        w_hi = sb("w_hi", [P, RING, SLOT_K, NB], F32R)
        w_lo = sb("w_lo", [P, RING, SLOT_K, NB], F32R)
        cols = sb("cols", [P, NCOLS])
        tables = sb("tables", [P, P + P + SEQ])
        ident = tables[:, 0:P]
        dist = [tables[:, P:2 * P], tables[:, 2 * P:2 * P + SEQ]]
        mixed = sb("mixed", [P, TT, NB])
        gated = sb("gated", [P, TT, NB])
        scaled = sb("scaled", [P, TT, BK, P])
        junk = sb("junk", [P, NB])
        sumsq = sb("sumsq", [P, TT, NJ])
        meansq = sb("meansq", [P, TT])
        root = sb("root", [P, TT])
        newton = sb("newton", [P, TT])
        rstd = sb("rstd", [P, TT])

        with ExitStack() as early:
            mT_hi = sb("mT_hi", [P, KD, SEQ], F32R, early)
            mT_lo = sb("mT_lo", [P, KD, SEQ], F32R, early)
            uT = sb("uT", [P, KC, PAD + SEQ], F32, early)
            cv = sb("cv", [P, KC, SEQ], F32, early)
            qT = sb("qT", [P, GQ, SEQ], F32, early)
            kT = sb("kT", [P, SEQ], F32, early)
            kv_tok = sb("kv_tok", [P, TT, 2 * KVW], F32, early)
            q_tok = sb("q_tok", [P, TT, AW], F32, early)
            s_tok = sb("s_tok", [P, TT, AW], F32, early)
            ln_v = sb("ln_v", [P, SEQ], F32, early)
            ln_r = sb("ln_r", [P, SEQ], F32, early)
            ln_t = sb("ln_t", [P, SEQ], F32, early)
            ones = sb("ones", [P, P], F32, early)
            NH = HQ + HKV
            qk_ss = sb("qk_ss", [P, TT, NH], F32, early)
            qk_root = sb("qk_root", [P, TT, NH], F32, early)
            qk_r = sb("qk_r", [P, TT, NH], F32, early)
            qk_t = sb("qk_t", [P, TT, NH], F32, early)
            top = sb("top", [P, 2, 8], F32, early)
            neg_top = sb("neg_top", [P, 2, 8], F32, early)
            sink_d = sb("sink_d", [P, 2, 8], F32, early)
            sink_e = sb("sink_e", [P, 2, 8], F32, early)
            den = sb("den", [P, 2, 8], F32, early)
            rden = sb("rden", [P, 2, 8], F32, early)
        with ExitStack() as late:
            yT_hi = sb("yT_hi", [P, KF, SEQ], F32R, late)
            yT_lo = sb("yT_lo", [P, KF, SEQ], F32R, late)
        with ExitStack() as late:
            zT_hi = sb("zT_hi", [P, KD, SEQ], F32R, late)
            zT_lo = sb("zT_lo", [P, KD, SEQ], F32R, late)
            bg_tok = sb("bg_tok", [P, TT, NB], F32, late)
            cT = sb("cT", [P, BK, 2 + SEQ], F32, late)
            zc = sb("zc", [P, BK, SEQ], F32, late)
        scores = [s_tok[:, :, :].rearrange("p t (h k) -> p (t h) k", k=SEQ),
                  q_tok[:, :, :].rearrange("p t (h k) -> p (t h) k", k=SEQ)]
        ln_sq = q_tok[:, :, :].rearrange("p t (c k) -> p (t c) k", k=SEQ)
        o_tok = mixed[:, :, :].rearrange("p t n -> p (t n)")

        pairs = [[ctx.enter_context(nc.psum_tensor(f"pair{p}_{t}", [P, NB], F32)) for t in range(TT)]
                 for p in range(3)]
        tbank = [ctx.enter_context(nc.psum_tensor(f"tbank{b}", [P, NB], F32)) for b in range(2)]
        conv_acc = pairs[2][0]
        heads_acc = pairs[2][1]

        x_loaded = [sem(f"x_loaded{b}") for b in range(NJ)]
        cols_loaded = sem("cols_loaded")
        tables_loaded = sem("tables_loaded")
        w_loaded = [sem(f"w_loaded{r}") for r in range(RING)]
        w_hi_ready = sem("w_hi_ready")
        w_lo_even = sem("w_lo_even")
        w_lo_odd = sem("w_lo_odd")
        w_used = sem("w_used")
        pair_read = [sem(f"pair_read{p}") for p in range(3)]
        t_ready = sem("t_ready")
        t_read = [sem(f"t_read{b}") for b in range(2)]
        hi_ready = sem("hi_ready")
        lo_ready = sem("lo_ready")
        sumsq_ready = sem("sumsq_ready")
        meansq_ready = sem("meansq_ready")
        root_ready = sem("root_ready")
        rstd_ready = sem("rstd_ready")
        pad_ready = sem("pad_ready")
        ones_ready = sem("ones_ready")
        qk_ss_ready = sem("qk_ss_ready")
        qk_root_ready = sem("qk_root_ready")
        qn_ready = sem("qn_ready")
        top_ready = sem("top_ready")
        p_ready = sem("p_ready")
        pv_done = sem("pv_done")
        o_ready = sem("o_ready")
        tap_done = sem("tap_done")
        cv_centered = sem("cv_centered")
        ln_sq_ready = sem("ln_sq_ready")
        ln_v_ready = sem("ln_v_ready")
        ln_root_ready = sem("ln_root_ready")
        ln_scaled = sem("ln_scaled")
        silu_done = sem("silu_done")
        c3_done = sem("c3_done")
        dve_step = sem("dve_step")
        act_step = sem("act_step")
        stored = sem("stored")

        def col(c, n=1):
            return cols[:, c:c + n]

        def tok(t):
            return slice(t * P, (t + 1) * P)

        def blk(b):
            return slice(b * NB, (b + 1) * NB)

        def bank4(b):
            return tbank[b][:, :].rearrange("p (k n) -> p k n", n=P)

        block = ctx.enter_context(nc.Block())

        @block.sync
        def _(sp):
            def place_free(s, per=0, rep=0):
                if s >= RING:
                    sp.wait_ge(w_lo_odd if s % 2 else w_lo_even, (s - RING) // 2 + 1 + (per // 2) * rep)

            def load_slot(s, source, cols_n=NB):
                r = s % RING
                sp.dma_start(w_raw[:, r, :, 0:cols_n], source).then_inc(w_loaded[r], 16)

            def load_job(s0, w, k0, slots, start, per=0, rep=0, cols_n=NB, swap=False):
                view = w.rearrange("(k p) n -> p k n", p=P)[:, :, ds(start, cols_n)]
                for q in ([1, 0] if swap else [0, 1]) + list(range(2, slots)):
                    k = k0 + SLOT_K * q
                    if swap and q == 1:
                        place_free(s0, per, rep)
                    if not (swap and q == 0):
                        place_free(s0 + q, per, rep)
                    load_slot(s0 + q, view[:, k:k + SLOT_K, :], cols_n)

            for b in range(NJ):
                sp.dma_start(xs[:, :, blk(b)],
                             x_in.rearrange("(t p) n -> p t n", p=P)[:, :, blk(b)]).then_inc(x_loaded[b], 16)
            starts = {"g0": CC, "a0": 0, "g1": CC + NB, "a1": NB, "q0": 2 * CC, "q1": 2 * CC + NB,
                      "kv": 2 * CC + AW}
            for name, start in starts.items():
                load_job(JOB[name][0], w_in, 0, SD, start, cols_n=2 * KVW if name == "kv" else NB)
            for nb in range(NJ):
                load_job(JOB[("attn_out", nb)][0], w_out, KC, SH, nb * NB)
            for nb in range(NJ):
                load_job(JOB[("conv_out", nb)][0], w_out, 0, SH, nb * NB)

            def ffn(layer):
                s0 = JOB[("gate", layer, 0)][0]
                with sp.Fori(1, NF + 1) as n:
                    i = n - 1
                    load_job(s0, w_gate[layer], 0, SD, i * NB, 2 * SD, i)
                    load_job(s0 + SD, w_up[layer], 0, SD, i * NB, 2 * SD, i)
                for nb in range(NJ):
                    load_job(JOB[("down", layer, nb)][0], w_down[layer], 0, SF, nb * NB)

            ffn(0)
            s0 = JOB[("cg", 0)][0]
            with sp.Fori(1, NJ + 1) as n:
                j = n - 1
                load_job(s0, sc_in, 0, SD, j * NB + D, 3 * SD, j)
                load_job(s0 + SD, sc_in, 0, SD, j * NB + 2 * D, 3 * SD, j)
                load_job(s0 + 2 * SD, sc_in, 0, SD, j * NB, 3 * SD, j, swap=True)
            for nb in range(NJ):
                load_job(JOB[("sc_out", nb)][0], sc_out, 0, SD, nb * NB)
            ffn(1)
            for nb in range(NJ):
                _, pair, uses = JOB[("down", 1, nb)]
                sp.wait_ge(pair_read[pair], uses + 1)
                sp.dma_start(out.rearrange("(t p) n -> p t n", p=P)[:, :, blk(nb)],
                             xs[:, :, blk(nb)]).then_inc(stored, 16)
            sp.wait_ge(stored, 16 * NJ)

        @block.gpsimd
        def _(pool):
            nc.gpsimd.memset(ones[:, :], 1.0 / CC).then_inc(ones_ready, 1)
            with pool.Fori(0, SLOTS // RING) as i:
                for r in range(1, RING, 2):
                    pool.wait_ge(w_hi_ready, RING * i + r + 1)
                    nc.gpsimd.tensor_tensor(w_lo[:, r, :, :], w_raw[:, r, :, :],
                                            w_hi[:, r, :, :].bitcast(F32), ALU.subtract).then_inc(w_lo_odd, 1)

        @block.tensor
        def _(pe):
            def slots(job, q0, q1, hi, lo, k0=0, per=0, rep=0, pair_per=0, n=NB, last=None):
                s0, pair, uses = JOB[job]
                last = q1 if last is None else last
                if q0 == 0 and (uses or pair_per):
                    pe.wait_ge(pair_read[pair], uses + pair_per * rep)
                for q in range(q0, q1):
                    s = s0 + q
                    r = s % RING
                    pe.wait_ge(w_lo_odd if s % 2 else w_lo_even, s // 2 + 1 + (per // 2) * rep)
                    for kk in range(SLOT_K):
                        k = k0 + SLOT_K * q + kk
                        first, end = (q == 0 and kk == 0), (q == last - 1 and kk == SLOT_K - 1)
                        for t in range(TT):
                            o = pairs[pair][t][:, 0:n]
                            nc.tensor.matmul(o, hi[:, k, tok(t)], w_hi[:, r, kk, 0:n], start=first, stop=False)
                            nc.tensor.matmul(o, hi[:, k, tok(t)], w_lo[:, r, kk, 0:n], start=False, stop=False)
                            mm = nc.tensor.matmul(o, lo[:, k, tok(t)], w_hi[:, r, kk, 0:n], start=False, stop=end)
                    mm.then_inc(w_used, 1)

            def bank_free(group, per=0, rep=0):
                _, b, uses = GROUP[group]
                if uses:
                    pe.wait_ge(t_read[b], uses + per * rep)
                return b

            def transposes(group, sources, per=0, rep=0):
                b = bank_free(group, per, rep)
                for n, source in enumerate(sources):
                    mm = nc.tensor.transpose(tbank[b][:, n * P:(n + 1) * P], source, ident)
                mm.then_inc(t_ready, 1)

            def x_transposes(norm, b):
                for t in range(TT):
                    transposes(("x", norm, b, t),
                               [xs[:, t, b * NB + k * P:b * NB + (k + 1) * P] for k in range(BK)])

            def x_split(norm, b):
                pe.wait_ge(lo_ready, LOW[("x", norm, b, TT - 1)] + 1)

            def read_out(job, per=0, rep=0):
                _, pair, uses = JOB[job]
                pe.wait_ge(pair_read[pair], uses + 1 + per * rep)

            def block_transposes(name, source, per=0, rep=0):
                for t in range(TT):
                    transposes(name + (t,), [source[:, t, k * P:(k + 1) * P] for k in range(BK)], per, rep)

            pe.wait_ge(tables_loaded, 16)
            for b in range(NJ):
                pe.wait_ge(x_loaded[b], 16)
                x_transposes(0, b)

            for b in range(NJ):
                x_split(0, b)
                slots("g0", 2 * b, 2 * b + 2, xT_hi, xT_lo, last=SD)
            slots("a0", 0, SD, xT_hi, xT_lo)
            slots("g1", 0, 4, xT_hi, xT_lo, last=SD)
            read_out("a0")
            block_transposes(("u", 0), mixed)
            slots("g1", 4, SD, xT_hi, xT_lo)
            slots("a1", 0, SD, xT_hi, xT_lo)
            slots("q0", 0, 4, xT_hi, xT_lo, last=SD)
            read_out("a1")
            block_transposes(("u", 1), mixed)
            slots("q0", 4, SD, xT_hi, xT_lo)
            slots("q1", 0, SD, xT_hi, xT_lo)
            slots("kv", 0, SD, xT_hi, xT_lo, n=2 * KVW)

            for t in range(TT):
                pe.wait_ge(qn_ready, t + 1)
                for half in range(2):
                    transposes(("qT", t, half),
                               [s_tok[:, t, (4 * half + j) * P:(4 * half + j + 1) * P] for j in range(4)])
            transposes("kT", [kv_tok[:, t, 0:P] for t in range(TT)])

            def keys_of(t):
                return P if t == 0 else SEQ

            def score_products(hh):
                t, half = hh // 2, hh % 2
                for r in range(4):
                    b = bank_free(("sc", hh, r))
                    g = r % 2
                    for m in range(2):
                        j = 4 * half + 2 * (r // 2) + m
                        mm = nc.tensor.matmul(tbank[b][:, m * SEQ:m * SEQ + keys_of(t)],
                                              qT[g * HD:(g + 1) * HD, j, tok(t)],
                                              kT[g * HD:(g + 1) * HD, 0:keys_of(t)], start=True, stop=True)
                    mm.then_inc(t_ready, 1)

            def prob_transposes(hh, r):
                kb = 1 + hh // 2
                per = 4 // kb
                transposes(("p", hh, r), [scores[hh % 2][:, per * r + m, c * P:(c + 1) * P]
                                          for m in range(per) for c in range(kb)])

            def value_products(hh, r, n):
                kb = 1 + hh // 2
                per = 4 // kb
                _, b, uses = GROUP[("p", hh, r)]
                pe.wait_ge(t_read[b], uses + 1)
                for m in range(per):
                    idx = per * r + m
                    g = idx // 4
                    for c in range(kb):
                        at = (m * kb + c) * P
                        mm = nc.tensor.matmul(heads_acc[:, idx * HD:(idx + 1) * HD],
                                              gated[:, n % 2, at:at + P],
                                              kv_tok[:, c, KVW + g * HD:KVW + (g + 1) * HD],
                                              start=(c == 0), stop=(c == kb - 1))
                mm.then_inc(pv_done, 1)

            def attend(hh, n0):
                pe.wait_ge(p_ready, hh + 1)
                groups = 2 * (1 + hh // 2)
                prob_transposes(hh, 0)
                for r in range(groups):
                    if r + 1 < groups:
                        prob_transposes(hh, r + 1)
                    if r == 0 and hh:
                        pe.wait_ge(o_ready, hh)
                    value_products(hh, r, n0 + r)

            def heads_transposes(t):
                pe.wait_ge(o_ready, 2 * t + 2)
                for r in range(2):
                    transposes(("o", t, r), [o_tok[:, (4 * r + k) * P:(4 * r + k + 1) * P] for k in range(4)])

            _, b, uses = GROUP["kT"]
            pe.wait_ge(t_read[b], uses + 1)
            score_products(0)
            score_products(1)
            attend(0, 0)
            score_products(2)
            attend(1, 2)
            heads_transposes(0)
            score_products(3)
            attend(2, 4)
            attend(3, 8)
            heads_transposes(1)

            for r in range(2):
                _, b, uses = GROUP[("o", 1, r)]
                pe.wait_ge(t_read[b], uses + 1)
            for nb in range(NJ):
                slots(("attn_out", nb), 0, SH, mT_hi, mT_lo, k0=KC)

            pe.wait_ge(ones_ready, 1)
            pe.wait_ge(tap_done, KC * TAPS)
            b = bank_free("mean")
            for c in range(KC):
                mm = nc.tensor.matmul(tbank[b][:, 0:SEQ], ones[:, :], cv[:, c, :], start=(c == 0), stop=(c == KC - 1))
            mm.then_inc(t_ready, 1)
            pe.wait_ge(ln_sq_ready, 1)
            b = bank_free("var")
            for c in range(KC):
                mm = nc.tensor.matmul(tbank[b][:, 0:SEQ], ones[:, :], ln_sq[:, c, :], start=(c == 0), stop=(c == KC - 1))
            mm.then_inc(t_ready, 1)

            for nb in range(NJ):
                job = ("conv_out", nb)
                if nb == 0:
                    for q in range(SH):
                        pe.wait_ge(lo_ready, LOW[("ln", q)] + 1)
                        slots(job, q, q + 1, mT_hi, mT_lo, last=SH)
                else:
                    slots(job, 0, 2, mT_hi, mT_lo, last=SH)
                    read_out(("conv_out", nb - 1))
                    x_transposes(1, nb - 1)
                    slots(job, 2, SH, mT_hi, mT_lo)

            def first_block(job, norm, last_out, last=SD):
                for b in range(2):
                    x_split(norm, b)
                    slots(job, 2 * b, 2 * b + 2, xT_hi, xT_lo, last=last)
                read_out(last_out)
                x_transposes(norm, NJ - 1)
                x_split(norm, 2)
                slots(job, 4, 6, xT_hi, xT_lo, last=last)
                x_split(norm, 3)
                slots(job, 6, SD, xT_hi, xT_lo)

            def ffn(layer, norm, last_out, norm_after):
                first_block(("gate", layer, 0), norm, last_out)
                slots(("up", layer, 0), 0, SD, xT_hi, xT_lo)
                with pe.Fori(1, NF) as i:
                    args = dict(per=2 * SD, rep=i, pair_per=1)
                    slots(("gate", layer, 0), 0, 4, xT_hi, xT_lo, last=SD, **args)
                    read_out(("up", layer, 0), 1, i - 1)
                    block_transposes(("y", layer, 0), mixed, 1, i - 1)
                    slots(("gate", layer, 0), 4, SD, xT_hi, xT_lo, **args)
                    slots(("up", layer, 0), 0, SD, xT_hi, xT_lo, **args)
                for nb in range(NJ):
                    job = ("down", layer, nb)
                    slots(job, 0, 4, yT_hi, yT_lo, last=SF)
                    if nb == 0:
                        read_out(("up", layer, NF - 1))
                        block_transposes(("y", layer, NF - 1), mixed)
                    elif norm_after is not None:
                        read_out(("down", layer, nb - 1))
                        x_transposes(norm_after, nb - 1)
                    slots(job, 4, SF - 2, yT_hi, yT_lo, last=SF)
                    if nb == 0:
                        for t in range(TT):
                            _, b, uses = GROUP[("y", layer, NF - 1, t)]
                            pe.wait_ge(t_read[b], uses + 1)
                    slots(job, SF - 2, SF, yT_hi, yT_lo)

            ffn(0, 1, ("conv_out", NJ - 1), 2)

            first_block(("cg", 0), 2, ("down", 0, NJ - 1))
            slots(("cu", 0), 0, SD, xT_hi, xT_lo)
            slots(("bg", 0), 0, 4, xT_hi, xT_lo, last=SD)
            read_out(("cu", 0))
            block_transposes(("c", 0), mixed)
            slots(("bg", 0), 4, SD, xT_hi, xT_lo)
            with pe.Fori(1, NJ) as j:
                args = dict(per=3 * SD, rep=j, pair_per=1)
                slots(("cg", 0), 0, 4, xT_hi, xT_lo, last=SD, **args)
                read_out(("bg", 0), 1, j - 1)
                block_transposes(("z", 0), bg_tok, 2, j - 1)
                slots(("cg", 0), 4, SD, xT_hi, xT_lo, **args)
                slots(("cu", 0), 0, SD, xT_hi, xT_lo, **args)
                slots(("bg", 0), 0, 4, xT_hi, xT_lo, last=SD, **args)
                read_out(("cu", 0), 1, j)
                block_transposes(("c", 0), mixed, 2, j)
                slots(("bg", 0), 4, SD, xT_hi, xT_lo, **args)
            for nb in range(NJ):
                job = ("sc_out", nb)
                if nb == 0:
                    pe.wait_ge(lo_ready, LOW[("z", NJ - 2, TT - 1)] + 1)
                slots(job, 0, 4, zT_hi, zT_lo, last=SD)
                if nb == 0:
                    read_out(("bg", NJ - 1))
                    block_transposes(("z", NJ - 1), bg_tok)
                    slots(job, 4, 6, zT_hi, zT_lo, last=SD)
                    pe.wait_ge(lo_ready, LOW[("z", NJ - 1, TT - 1)] + 1)
                    slots(job, 6, SD, zT_hi, zT_lo)
                else:
                    read_out(("sc_out", nb - 1))
                    x_transposes(3, nb - 1)
                    slots(job, 4, SD, zT_hi, zT_lo)

            ffn(1, 3, ("sc_out", NJ - 1), None)

        @block.scalar
        def _(act):
            steps = [0]

            def link(ins):
                steps[0] += 1
                ins.then_inc(act_step, 1)
                act.wait_ge(act_step, steps[0])

            def highs(s_from, s_to, per=0, rep=0):
                for s in range(s_from, min(s_to, SLOTS)):
                    r = s % RING
                    act.wait_ge(w_loaded[r], 16 * (s // RING + 1) + (16 * per // RING) * rep)
                    if s >= RING:
                        act.wait_ge(w_used, s - RING + 1 + per * rep)
                    nc.scalar.activation(w_hi[:, r, :, :], w_raw[:, r, :, :], ACT.Copy).then_inc(w_hi_ready, 1)

            def job_done(job, per=0, rep=0, slots=SD):
                s0, pair, _ = JOB[job]
                act.wait_ge(w_used, s0 + slots + per * rep)
                return pair

            def high_of_scaled(name, dest, k, t, per=0, rep=0, bank_per=0, scaled_t=None):
                _, b, uses = GROUP[name]
                act.wait_ge(t_read[b], uses + 1 + bank_per * rep)
                nc.scalar.activation(dest[:, k, tok(t)], scaled[:, t, :, :], ACT.Copy).then_inc(hi_ready, 1)

            def x_highs(norm, b):
                for t in range(TT):
                    high_of_scaled(("x", norm, b, t), xT_hi, slice(BK * b, BK * (b + 1)), t)

            def high_of_group(name, dest, k, t, per=0, rep=0):
                n, b, _ = GROUP[name]
                act.wait_ge(t_ready, n + 1 + per * rep)
                nc.scalar.activation(dest[:, k, tok(t)], bank4(b), ACT.Copy).then_inc(hi_ready, 1)

            def copy_group(name, dest, width=NB):
                n, b, _ = GROUP[name]
                act.wait_ge(t_ready, n + 1)
                src = tbank[b][:, 0:width]
                if len(dest.shape) == 3:
                    src = src.rearrange("p (k n) -> p k n", n=dest.shape[2])
                nc.scalar.activation(dest, src, ACT.Copy).then_inc(t_read[b], 1)

            def x_squares(b, count):
                for t in range(TT):
                    link(nc.scalar.activation(junk[:, :], xs[:, t, blk(b)], ACT.Square,
                                              accum_out=sumsq[:, t, b:b + 1]))
                if b == NJ - 1:
                    nc.scalar.activation(junk[:, :], xs[:, 0, blk(b)], ACT.Copy).then_inc(sumsq_ready, 1)

            def norm_root(norm):
                act.wait_ge(meansq_ready, norm + 1)
                nc.scalar.activation(root[:, :], meansq[:, :], ACT.Sqrt).then_inc(root_ready, 1)

            def read_pair(job, func, dest, width=NB, per=0, rep=0):
                pair = job_done(job, per, rep)
                for t in range(TT):
                    ins = nc.scalar.activation(dest[:, t, 0:width], pairs[pair][t][:, 0:width], func,
                                               scale=rstd[:, t:t + 1])
                ins.then_inc(pair_read[pair], 1)

            act.dma_start(tables[:, :], tables_in).then_inc(tables_loaded, 16)
            act.dma_start(cols[:, :], cols_in).then_inc(cols_loaded, 16)
            for b in range(NJ):
                x_highs(0, b)
                highs(b, b + 1)
            for b in range(NJ):
                act.wait_ge(x_loaded[b], 16)
                x_squares(b, 0)
            norm_root(0)

            highs(4, 11)
            act.wait_ge(rstd_ready, 1)
            read_pair("g0", ACT.Sigmoid, gated)
            highs(11, JOB["g1"][0] + 7)
            act.wait_ge(pad_ready, 1)
            for t in range(TT):
                copy_group(("u", 0, t), uT[:, 0:BK, PAD + t * P:PAD + (t + 1) * P])
            highs(JOB["g1"][0] + 7, JOB["a1"][0] + 3)
            act.wait_ge(pair_read[1], JOB["a0"][2] + 1)
            read_pair("g1", ACT.Sigmoid, gated)
            highs(JOB["a1"][0] + 3, JOB["q0"][0] + 7)
            for t in range(TT):
                copy_group(("u", 1, t), uT[:, BK:2 * BK, PAD + t * P:PAD + (t + 1) * P])
            highs(JOB["q0"][0] + 7, JOB["q1"][0] + 3)
            read_pair("q0", ACT.Copy, q_tok[:, :, 0:NB])
            highs(JOB["q1"][0] + 3, JOB["kv"][0] + 3)
            read_pair("q1", ACT.Copy, q_tok[:, :, NB:2 * NB])
            highs(JOB["kv"][0] + 3, JOB["kv"][0] + SD + 3)
            read_pair("kv", ACT.Copy, kv_tok, 2 * KVW)
            highs(JOB["kv"][0] + SD + 3, JOB["kv"][0] + SD + 4)

            act.wait_ge(qk_ss_ready, 1)
            nc.scalar.activation(qk_root[:, :, :], qk_ss[:, :, :], ACT.Sqrt).then_inc(qk_root_ready, 1)
            for t in range(TT):
                for half in range(2):
                    copy_group(("qT", t, half), qT[:, 4 * half:4 * half + 4, tok(t)])
            copy_group("kT", kT[:, :], SEQ)

            def exps(hh):
                keys = P if hh < 2 else SEQ
                act.wait_ge(top_ready, hh + 1)
                for idx in range(8):
                    s = scores[hh % 2][:, idx, 0:keys]
                    nc.scalar.activation(s, s, ACT.Exp, bias=neg_top[:, hh % 2, idx:idx + 1],
                                         accum_out=den[:, hh % 2, idx:idx + 1])
                nc.scalar.activation(sink_e[:, hh % 2, :], sink_d[:, hh % 2, :], ACT.Exp).then_inc(p_ready, 1)

            def prob_copies(hh, n0):
                for r in range(2 * (1 + hh // 2)):
                    n = n0 + r
                    if n >= 2:
                        act.wait_ge(pv_done, n - 1)
                    copy_group(("p", hh, r), gated[:, n % 2, :])

            def heads_highs(t):
                for r in range(2):
                    high_of_group(("o", t, r), mT_hi, slice(KC + 4 * r, KC + 4 * r + 4), t)

            exps(0)
            exps(1)
            prob_copies(0, 0)
            exps(2)
            prob_copies(1, 2)
            heads_highs(0)
            exps(3)
            prob_copies(2, 4)
            prob_copies(3, 8)
            heads_highs(1)

            s0 = JOB[("conv_out", 0)][0]
            highs(JOB[("attn_out", 0)][0] + 4, s0 + 3)
            act.wait_ge(cv_centered, 1)
            nc.scalar.activation(ln_sq, cv[:, :, :], ACT.Square).then_inc(ln_sq_ready, 1)
            act.wait_ge(ln_v_ready, 1)
            nc.scalar.activation(ln_r[:, :], ln_v[:, :], ACT.Sqrt).then_inc(ln_root_ready, 1)
            highs(s0 + 3, s0 + 4)
            for q in range(KC // 2):
                act.wait_ge(ln_scaled, q + 1)
                for c in range(2 * q, 2 * q + 2):
                    ins = nc.scalar.activation(cv[:, c, :], cv[:, c, :], ACT.Silu,
                                               bias=col(LNB + c), scale=col(LNG + c))
                ins.then_inc(silu_done, 1)
                act.wait_ge(silu_done, q + 1)
                nc.scalar.activation(mT_hi[:, 2 * q:2 * q + 2, :], cv[:, 2 * q:2 * q + 2, :],
                                     ACT.Copy).then_inc(hi_ready, 1)
            at = s0 + 4
            for nb in range(1, NJ):
                after = s0 + SH * nb + 2
                highs(at, after + 3)
                at = after + 3
                x_highs(1, nb - 1)
                x_squares(nb - 1, 0)

            def first_block(s0, at, norm):
                highs(at, s0 + 7)
                x_highs(norm, NJ - 1)
                x_squares(NJ - 1, 0)
                norm_root(norm)
                highs(s0 + 7, s0 + SD + 3)
                act.wait_ge(rstd_ready, norm + 1)

            def ffn(layer, norm, at, norm_after):
                s0 = JOB[("gate", layer, 0)][0]
                first_block(s0, at, norm)
                read_pair(("gate", layer, 0), ACT.Silu, gated)
                highs(s0 + SD + 3, s0 + 2 * SD + 4)
                with act.Fori(1, NF) as i:
                    highs(s0 + 4, s0 + 7, 2 * SD, i)
                    for t in range(TT):
                        high_of_group(("y", layer, 0, t), yT_hi, ds(BK * (i - 1), BK), t, TT, i - 1)
                    highs(s0 + 7, s0 + SD + 3, 2 * SD, i)
                    act.wait_ge(pair_read[1], JOB[("up", layer, 0)][2] + i)
                    read_pair(("gate", layer, 0), ACT.Silu, gated, NB, 2 * SD, i)
                    highs(s0 + SD + 3, s0 + 2 * SD + 4, 2 * SD, i)
                at = s0 + 2 * SD * NF + 4
                for nb in range(NJ):
                    after = JOB[("down", layer, nb)][0] + 4
                    highs(at, after + 3)
                    at = after + 3
                    if nb == 0:
                        for t in range(TT):
                            high_of_group(("y", layer, NF - 1, t), yT_hi, slice(KF - BK, KF), t)
                    elif norm_after is not None:
                        x_highs(norm_after, nb - 1)
                        x_squares(nb - 1, 0)
                return at

            at = ffn(0, 1, at, 2)

            s0 = JOB[("cg", 0)][0]

            def mixer_block(rep, from_c):
                per = 3 * SD
                if from_c:
                    act.wait_ge(pair_read[1], JOB[("cu", 0)][2] + rep)
                read_pair(("cg", 0), ACT.Copy, gated, NB, per, rep)
                highs(s0 + SD + 3, s0 + 2 * SD + 7, per, rep)
                if from_c:
                    act.wait_ge(c3_done, 3 * BK * rep)
                for t in range(TT):
                    n, b, _ = GROUP[("c", 0, t)]
                    act.wait_ge(t_ready, n + 1 + 2 * TT * rep)
                    nc.scalar.activation(cT[:, :, 2 + t * P:2 + (t + 1) * P], bank4(b),
                                         ACT.Copy).then_inc(t_read[b], 1)
                highs(s0 + 2 * SD + 7, s0 + 3 * SD + 3, per, rep)
                pair = JOB[("bg", 0)][1]
                act.wait_ge(w_used, s0 + 3 * SD + per * rep)
                for t in range(TT):
                    ins = nc.scalar.activation(bg_tok[:, t, :], pairs[pair][t][:, :], ACT.Copy,
                                               scale=rstd[:, t:t + 1])
                ins.then_inc(pair_read[pair], 1)
                highs(s0 + 3 * SD + 3, s0 + 3 * SD + 4, per, rep)

            first_block(s0, at, 2)
            mixer_block(0, False)
            with act.Fori(1, NJ) as j:
                highs(s0 + 4, s0 + 7, 3 * SD, j)
                for t in range(TT):
                    high_of_scaled(("z", 0, t), zT_hi, ds(BK * (j - 1), BK), t, rep=j - 1, bank_per=2)
                highs(s0 + 7, s0 + SD + 3, 3 * SD, j)
                mixer_block(j, True)
            at = s0 + 3 * SD * NJ + 4
            for nb in range(NJ):
                after = JOB[("sc_out", nb)][0] + 4
                highs(at, after + 3)
                at = after + 3
                if nb == 0:
                    for t in range(TT):
                        high_of_scaled(("z", NJ - 1, t), zT_hi, slice(KD - BK, KD), t)
                else:
                    x_highs(3, nb - 1)
                    x_squares(nb - 1, 0)
            at = ffn(1, 3, at, None)
            highs(at, SLOTS)

        @block.vector
        def _(dve):
            steps = [0]

            def link(ins):
                steps[0] += 1
                ins.then_inc(dve_step, 1)
                dve.wait_ge(dve_step, steps[0])

            def lows(s_from, s_to, per=0, rep=0):
                for s in range(s_from + s_from % 2, min(s_to, SLOTS), 2):
                    r = s % RING
                    dve.wait_ge(w_hi_ready, s + 1 + per * rep)
                    nc.vector.tensor_tensor(w_lo[:, r, :, :], w_raw[:, r, :, :],
                                            w_hi[:, r, :, :].bitcast(F32), ALU.subtract).then_inc(w_lo_even, 1)

            def gain(norm, b):
                base = (MIXG if norm % 2 == 0 else FFNG) + (norm // 2) * KD
                return col(base + BK * b, BK).unsqueeze(2).to_broadcast([P, BK, P])

            def x_split(norm, b):
                for t in range(TT):
                    n, bank, _ = GROUP[("x", norm, b, t)]
                    dve.wait_ge(t_ready, n + 1)
                    if LOW[("x", norm, b, t)] >= TT:
                        dve.wait_ge(lo_ready, LOW[("x", norm, b, t)] - TT + 1)
                    nc.vector.tensor_tensor(scaled[:, t, :, :], bank4(bank), gain(norm, b),
                                            ALU.mult).then_inc(t_read[bank], 1)
                for t in range(TT):
                    k = slice(BK * b, BK * (b + 1))
                    dve.wait_ge(hi_ready, HIGH[("x", norm, b, t)] + 1)
                    nc.vector.tensor_tensor(xT_lo[:, k, tok(t)], scaled[:, t, :, :],
                                            xT_hi[:, k, tok(t)].bitcast(F32), ALU.subtract).then_inc(lo_ready, 1)

            def low_of_group(name, hi, lo, k, t, per=0, rep=0, bank_per=0):
                _, b, _ = GROUP[name]
                dve.wait_ge(hi_ready, HIGH[name] + 1 + per * rep)
                nc.vector.tensor_tensor(lo[:, k, tok(t)], bank4(b), hi[:, k, tok(t)].bitcast(F32),
                                        ALU.subtract).then_inc(t_read[b], 1)

            def newton_root(value, r, tmp):
                link(nc.vector.reciprocal(r, r))
                link(nc.vector.tensor_tensor(tmp, r, r, ALU.mult))
                link(nc.vector.tensor_tensor(tmp, tmp, value, ALU.mult))
                link(nc.vector.tensor_scalar(tmp, tmp, -0.5, 1.5, ALU.mult, ALU.add))

            def norm_stats(norm):
                dve.wait_ge(sumsq_ready, norm + 1)
                link(nc.vector.reduce_sum(meansq[:, :], sumsq[:, :, :], AX_X))
                nc.vector.tensor_scalar(meansq[:, :], meansq[:, :], 1.0 / D, RMS_EPS, ALU.mult,
                                        ALU.add).then_inc(meansq_ready, 1)
                dve.wait_ge(root_ready, norm + 1)
                newton_root(meansq[:, :], root[:, :], newton[:, :])
                nc.vector.tensor_tensor(rstd[:, :], root[:, :], newton[:, :], ALU.mult).then_inc(rstd_ready, 1)
                dve.wait_ge(rstd_ready, norm + 1)

            def multiply_pair(job, per=0, rep=0, bank_per=0):
                s0, pair, _ = JOB[job]
                dve.wait_ge(w_used, s0 + SD + per * rep)
                for t in range(TT):
                    ins = nc.vector.scalar_tensor_tensor(mixed[:, t, :], pairs[pair][t][:, :], rstd[:, t:t + 1],
                                                         gated[:, t, :], ALU.mult, ALU.mult)
                ins.then_inc(pair_read[pair], 1)

            def add_pair(job, nb, slots):
                s0, pair, _ = JOB[job]
                dve.wait_ge(w_used, s0 + slots)
                for t in range(TT):
                    ins = nc.vector.tensor_tensor(xs[:, t, blk(nb)], pairs[pair][t][:, :], xs[:, t, blk(nb)], ALU.add)
                ins.then_inc(pair_read[pair], 1)

            def conv_taps(a, b):
                for n in range(a, min(b, KC * TAPS)):
                    two, rest = n // (2 * TAPS), n % (2 * TAPS)
                    k, m = rest // 2, rest % 2
                    c = 2 * two + m
                    w = col(DWW + c * TAPS + k)
                    acc = conv_acc[:, m * SEQ:(m + 1) * SEQ]
                    u = uT[:, c, k:k + SEQ]
                    if k == 0:
                        if n >= 2:
                            dve.wait_ge(tap_done, n - 1)
                        nc.vector.tensor_scalar(acc, u, w, col(DWB + c), ALU.mult, ALU.add).then_inc(tap_done, 1)
                    else:
                        dve.wait_ge(tap_done, n - 1)
                        dest = cv[:, c, :] if k == TAPS - 1 else acc
                        nc.vector.scalar_tensor_tensor(dest, u, w, acc, ALU.mult, ALU.add).then_inc(tap_done, 1)

            link(nc.vector.memset(uT[:, :, 0:PAD], 0.0))
            nc.vector.memset(junk[:, 0:2], 0.0).then_inc(pad_ready, 1)
            dve.wait_ge(cols_loaded, 16)
            for b in range(NJ):
                x_split(0, b)
                lows(b, b + 1)
            norm_stats(0)

            lows(4, JOB["g1"][0] + 4)
            dve.wait_ge(pair_read[0], JOB["g0"][2] + 1)
            multiply_pair("a0")
            lows(JOB["g1"][0] + 4, JOB["g1"][0] + 8)
            taps = 0
            for t in range(TT):
                _, b, uses = GROUP[("u", 0, t)]
                dve.wait_ge(t_read[b], uses + 1)
            for s in range(JOB["a1"][0], JOB["q0"][0] + 4, 2):
                lows(s, s + 2)
                conv_taps(taps, taps + 8)
                taps += 8
            dve.wait_ge(pair_read[0], JOB["g1"][2] + 1)
            multiply_pair("a1")
            for s in range(JOB["q0"][0] + 4, JOB["kv"][0] + SD + 4, 2):
                lows(s, s + 2)
                conv_taps(taps, min(taps + 8, KC * TAPS // 2))
                taps = min(taps + 8, KC * TAPS // 2)

            _, pair, uses = JOB["kv"]
            dve.wait_ge(pair_read[pair], uses + 1)
            k_sq = mixed[:, :, 0:KVW]
            dve.wait_ge(t_ready, GROUP[("u", 1, TT - 1)][0] + 1)
            link(nc.vector.tensor_tensor(k_sq, kv_tok[:, :, 0:KVW], kv_tok[:, :, 0:KVW], ALU.mult))
            nc.vector.tensor_tensor(s_tok[:, 0, :], q_tok[:, 0, :], q_tok[:, 0, :], ALU.mult)
            link(nc.vector.tensor_tensor(s_tok[:, 1, :], q_tok[:, 1, :], q_tok[:, 1, :], ALU.mult))
            for t in range(TT):
                nc.vector.reduce_sum(qk_ss[:, t, 0:HQ], s_tok[:, t, :].rearrange("p (h d) -> p h d", d=HD), AX_X)
                ins = nc.vector.reduce_sum(qk_ss[:, t, HQ:NH], k_sq[:, t, :].rearrange("p (h d) -> p h d", d=HD), AX_X)
            link(ins)
            nc.vector.tensor_scalar(qk_ss[:, :, :], qk_ss[:, :, :], 1.0 / HD, RMS_EPS, ALU.mult,
                                    ALU.add).then_inc(qk_ss_ready, 1)
            dve.wait_ge(qk_root_ready, 1)
            newton_root(qk_ss[:, :, :], qk_root[:, :, :], qk_t[:, :, :])
            link(nc.vector.tensor_tensor(qk_r[:, :, :], qk_root[:, :, :], qk_t[:, :, :], ALU.mult))
            link(nc.vector.tensor_scalar(qk_r[:, :, 0:HQ], qk_r[:, :, 0:HQ], HD ** -0.5, None, ALU.mult))
            for t in range(TT):
                q3 = q_tok[:, t, :].rearrange("p (h d) -> p h d", d=HD)
                k3 = kv_tok[:, t, 0:KVW].rearrange("p (h d) -> p h d", d=HD)
                nc.vector.tensor_tensor(q3, q3, qk_r[:, t, 0:HQ].unsqueeze(2).to_broadcast([P, HQ, HD]), ALU.mult)
                link(nc.vector.tensor_tensor(k3, k3, qk_r[:, t, HQ:NH].unsqueeze(2).to_broadcast([P, HKV, HD]),
                                             ALU.mult))
                for g in range(HKV):
                    nc.vector.tensor_tensor(
                        s_tok[:, t, :].rearrange("p (j g d) -> p j g d", g=HKV, d=HD)[:, :, g, :],
                        q_tok[:, t, g * GQ * HD:(g + 1) * GQ * HD].rearrange("p (j d) -> p j d", d=HD),
                        col(QG, HD).unsqueeze(1).to_broadcast([P, GQ, HD]), ALU.mult)
                nc.vector.tensor_tensor(k3, k3, col(KG, HD).unsqueeze(1).to_broadcast([P, HKV, HD]),
                                        ALU.mult).then_inc(qn_ready, 1)

            def score_rows(hh):
                t, half, sl = hh // 2, hh % 2, hh % 2
                keys = P if t == 0 else SEQ
                if hh < 2:
                    dve.wait_ge(t_ready, GROUP["kT"][0] + 1)
                else:
                    dve.wait_ge(t_ready, GROUP[("p", hh - 2, 1)][0] + 1)
                for r in range(4):
                    n, b, _ = GROUP[("sc", hh, r)]
                    dve.wait_ge(t_ready, n + 1)
                    g = r % 2
                    for m in range(2):
                        j = 4 * half + 2 * (r // 2) + m
                        slope = 2.0 ** (-8.0 * (g * GQ + j + 1) / HQ)
                        ins = nc.vector.scalar_tensor_tensor(
                            scores[sl][:, 4 * g + 2 * (r // 2) + m, 0:keys], dist[t], -slope,
                            tbank[b][:, m * SEQ:m * SEQ + keys], ALU.mult, ALU.add)
                    ins.then_inc(t_read[b], 1)
                for r in range(2):
                    n, b, uses = GROUP[("sc", hh, 2 + r)]
                    dve.wait_ge(t_read[b], uses + 1)
                top3 = top[:, sl, :].rearrange("p (g j) -> p g j", g=HKV)
                sink3 = col(SINK, HQ).rearrange("p (g j) -> p g j", g=HKV)[:, :, 4 * half:4 * half + 4]
                link(nc.vector.reduce_max(top[:, sl, :], scores[sl][:, :, 0:keys], AX_X))
                link(nc.vector.tensor_tensor(top3, top3, sink3, ALU.max))
                link(nc.vector.tensor_scalar(neg_top[:, sl, :], top[:, sl, :], -1.0, None, ALU.mult))
                nc.vector.tensor_tensor(sink_d[:, sl, :].rearrange("p (g j) -> p g j", g=HKV), sink3,
                                        neg_top[:, sl, :].rearrange("p (g j) -> p g j", g=HKV),
                                        ALU.add).then_inc(top_ready, 1)

            def heads_out(hh, groups_before):
                t, half, sl = hh // 2, hh % 2, hh % 2
                dve.wait_ge(p_ready, hh + 1)
                link(nc.vector.tensor_tensor(rden[:, sl, :], den[:, sl, :], sink_e[:, sl, :], ALU.add))
                link(nc.vector.reciprocal(rden[:, sl, :], rden[:, sl, :]))
                dve.wait_ge(pv_done, groups_before + 2 * (1 + t))
                if hh == 2:
                    dve.wait_ge(t_ready, GROUP[("o", 0, 1)][0] + 1)
                for g in range(HKV):
                    ins = nc.vector.tensor_tensor(
                        o_tok[:, (g * GQ + 4 * half) * HD:(g * GQ + 4 * half + 4) * HD]
                        .rearrange("p (j d) -> p j d", d=HD),
                        heads_acc[:, 4 * g * HD:4 * (g + 1) * HD].rearrange("p (j d) -> p j d", d=HD),
                        rden[:, sl, 4 * g:4 * g + 4].unsqueeze(2).to_broadcast([P, 4, HD]), ALU.mult)
                ins.then_inc(o_ready, 1)

            def heads_lows(t):
                for r in range(2):
                    low_of_group(("o", t, r), mT_hi, mT_lo, slice(KC + 4 * r, KC + 4 * r + 4), t)

            _, b, uses = GROUP[("qT", TT - 1, 1)]
            score_rows(0)
            score_rows(1)
            conv_taps(taps, taps + 8)
            heads_out(0, 0)
            score_rows(2)
            conv_taps(taps + 8, taps + 16)
            heads_out(1, 2)
            heads_lows(0)
            score_rows(3)
            conv_taps(taps + 16, taps + 24)
            heads_out(2, 4)
            conv_taps(taps + 24, taps + 32)
            taps += 32
            heads_out(3, 8)
            heads_lows(1)

            s0 = JOB[("attn_out", 0)][0]
            for nb in range(NJ):
                for s in range(s0 + SH * (nb + 1), s0 + SH * (nb + 2), 2):
                    lows(s, s + 2)
                    if s == s0 + SH * (nb + 1):
                        conv_taps(taps, taps + 8)
                        taps += 8
                add_pair(("attn_out", nb), nb, SH)
                conv_taps(taps, taps + 5)
                taps += 5
            conv_taps(taps, KC * TAPS)

            n, b, _ = GROUP["mean"]
            dve.wait_ge(tap_done, KC * TAPS)
            dve.wait_ge(t_ready, n + 1)
            nc.vector.tensor_tensor(cv[:, :, :], cv[:, :, :],
                                    tbank[b][:, 0:SEQ].unsqueeze(1).to_broadcast([P, KC, SEQ]),
                                    ALU.subtract).then_inc(cv_centered, 1)
            n, b2, _ = GROUP["var"]
            dve.wait_ge(cv_centered, 1)
            nc.vector.memset(junk[:, 0:2], 0.0).then_inc(t_read[b], 1)
            dve.wait_ge(t_ready, n + 1)
            nc.vector.tensor_scalar(ln_v[:, :], tbank[b2][:, 0:SEQ], LN_EPS, None, ALU.add).then_inc(t_read[b2], 1)
            dve.wait_ge(t_read[b2], GROUP["var"][2] + 1)
            nc.vector.memset(junk[:, 2:4], 0.0).then_inc(ln_v_ready, 1)
            dve.wait_ge(ln_root_ready, 1)
            newton_root(ln_v[:, :], ln_r[:, :], ln_t[:, :])
            link(nc.vector.tensor_tensor(ln_r[:, :], ln_r[:, :], ln_t[:, :], ALU.mult))
            for q in range(KC // 2):
                part = cv[:, 2 * q:2 * q + 2, :]
                nc.vector.tensor_tensor(part, part, ln_r[:, :].unsqueeze(1).to_broadcast([P, 2, SEQ]),
                                        ALU.mult).then_inc(ln_scaled, 1)
            for q in range(KC // 2):
                dve.wait_ge(hi_ready, HIGH[("ln", q)] + 1)
                nc.vector.tensor_tensor(mT_lo[:, 2 * q:2 * q + 2, :], cv[:, 2 * q:2 * q + 2, :],
                                        mT_hi[:, 2 * q:2 * q + 2, :].bitcast(F32), ALU.subtract).then_inc(lo_ready, 1)

            s0 = JOB[("conv_out", 0)][0]
            at = s0 + SH
            for nb in range(NJ):
                done = s0 + SH * (nb + 1)
                lows(at, done + 3)
                add_pair(("conv_out", nb), nb, SH)
                at = done + 3
                if nb < NJ - 1:
                    lows(at, done + 5)
                    at = done + 5
                    x_split(1, nb)

            def first_block(s0, at, norm):
                lows(at, s0 + 7)
                x_split(norm, NJ - 1)
                norm_stats(norm)
                return s0 + 7

            def ffn(layer, norm, at, norm_after):
                s0 = JOB[("gate", layer, 0)][0]
                at = first_block(s0, at, norm)
                lows(at, s0 + 2 * SD + 3)
                dve.wait_ge(pair_read[0], JOB[("gate", layer, 0)][2] + 1)
                multiply_pair(("up", layer, 0))
                with dve.Fori(1, NF) as i:
                    lows(s0 + 4, s0 + 7, 2 * SD, i)
                    for t in range(TT):
                        low_of_group(("y", layer, 0, t), yT_hi, yT_lo, ds(BK * (i - 1), BK), t, TT, i - 1)
                    lows(s0 + 8, s0 + 2 * SD + 3, 2 * SD, i)
                    dve.wait_ge(pair_read[0], JOB[("gate", layer, 0)][2] + 1 + i)
                    multiply_pair(("up", layer, 0), 2 * SD, i)
                at = s0 + 2 * SD * NF + 4
                for nb in range(NJ):
                    d0 = JOB[("down", layer, nb)][0]
                    lows(at, d0 + 7)
                    at = d0 + 8
                    if nb == 0:
                        for t in range(TT):
                            low_of_group(("y", layer, NF - 1, t), yT_hi, yT_lo, slice(KF - BK, KF), t)
                    elif norm_after is not None:
                        x_split(norm_after, nb - 1)
                    lows(at, d0 + SF + 3)
                    at = d0 + SF + 3
                    add_pair(("down", layer, nb), nb, SF)
                return at

            at = ffn(0, 1, at, 2)

            s0 = JOB[("cg", 0)][0]
            at = first_block(s0, at, 2)
            nc.vector.memset(cT[:, :, 0:2], 0.0)

            def gate_block(j, rep, k):
                for t in range(TT):
                    n, b, _ = GROUP[("z", j, t)]
                    dve.wait_ge(t_ready, n + 1 + 2 * TT * rep)
                    nc.vector.tensor_tensor(scaled[:, t, :, :], bank4(b), zc[:, :, tok(t)],
                                            ALU.mult).then_inc(t_read[b], 1)
                for t in range(TT):
                    dve.wait_ge(hi_ready, HIGH[("z", j, t)] + 1 + TT * rep)
                    nc.vector.tensor_tensor(zT_lo[:, k, tok(t)], scaled[:, t, :, :],
                                            zT_hi[:, k, tok(t)].bitcast(F32), ALU.subtract).then_inc(lo_ready, 1)

            def mixer_block(rep):
                per = 3 * SD
                dve.wait_ge(pair_read[0], JOB[("cg", 0)][2] + 1 + rep)
                multiply_pair(("cu", 0), per, rep)
                lows(s0 + 2 * SD + 4, s0 + 2 * SD + 7, per, rep)
                for t in range(TT):
                    _, b, uses = GROUP[("c", 0, t)]
                    dve.wait_ge(t_read[b], uses + 1 + 2 * rep)
                for tap in range(3):
                    for k in range(BK):
                        w = cols[:, ds(SCW + k * 3 + tap + 3 * BK * rep, 1)]
                        src = cT[:, k, tap:tap + SEQ]
                        if tap:
                            dve.wait_ge(c3_done, BK * (tap - 1) + k + 1 + 3 * BK * rep)
                            ins = nc.vector.scalar_tensor_tensor(zc[:, k, :], src, w, zc[:, k, :], ALU.mult, ALU.add)
                        else:
                            ins = nc.vector.tensor_scalar(zc[:, k, :], src, w, None, ALU.mult)
                        ins.then_inc(c3_done, 1)
                lows(s0 + 2 * SD + 8, s0 + 3 * SD + 4, per, rep)

            lows(at, s0 + 2 * SD + 3)
            mixer_block(0)
            with dve.Fori(1, NJ) as j:
                lows(s0 + 4, s0 + 7, 3 * SD, j)
                dve.wait_ge(c3_done, 3 * BK * j)
                gate_block(0, j - 1, ds(BK * (j - 1), BK))
                lows(s0 + 8, s0 + 2 * SD + 3, 3 * SD, j)
                mixer_block(j)
            at = s0 + 3 * SD * NJ + 4
            for nb in range(NJ):
                o0 = JOB[("sc_out", nb)][0]
                lows(at, o0 + 7)
                at = o0 + 8
                if nb == 0:
                    dve.wait_ge(c3_done, 3 * BK * NJ)
                    gate_block(NJ - 1, 0, slice(KD - BK, KD))
                else:
                    x_split(3, nb - 1)
                lows(at, o0 + SD + 3)
                at = o0 + SD + 3
                add_pair(("sc_out", nb), nb, SD)
            ffn(1, 3, at, None)


def _columns(np, v):
    def feature_major(a):
        a = np.asarray(a)
        lead, feats = a.shape[:-1], a.shape[-1]
        return a.reshape(-1, feats // 128, 128)

    def plain(a):
        a = feature_major(a)
        return a.transpose(2, 0, 1).reshape(128, -1)

    def taps(a):
        a = feature_major(a)
        return a.transpose(2, 1, 0).reshape(128, -1)

    def shared(a):
        return np.broadcast_to(np.asarray(a).reshape(1, -1), (128, np.asarray(a).size))

    return np.ascontiguousarray(np.concatenate([
        plain(v["mix_norm_g"]), plain(v["ffn_norm_g"]), taps(v["conv_dw_w"][0]), plain(v["conv_dw_b"]),
        plain(v["conv_ln_g"]), plain(v["conv_ln_b"]), taps(v["sc_conv_w"][0]),
        shared(v["q_norm_g"]), shared(v["k_norm_g"]), shared(v["attn_sinks"])], axis=1))


def _tables(np):
    chunk, far = 64, 1e33
    parts = [np.eye(128)]
    for q0, keys in ((0, 128), (128, 256)):
        q, k = np.arange(q0, q0 + 128)[:, None], np.arange(keys)[None, :]
        seen = (k // chunk == q // chunk) | (k // chunk == q // chunk - 1)
        parts.append(np.where(seen, np.abs(q - k), far))
    return np.concatenate(parts, axis=1).astype(np.float32)


def kernel(**inputs):
    import numpy as np
    import concourse.bacc as bacc
    from concourse import mybir as mb
    from concourse.bass_utils import run_bass_kernel_spmd

    v = {name: np.asarray(a) for name, a in inputs.items()}
    arrays = {
        "x": v["x"][0], "w_in": v["hy_w_in"][0], "w_out": v["hy_w_out"][0], "sc_in": v["sc_w_in"][0],
        "sc_out": v["sc_w_out"][0], "w_gate": v["ffn_w_gate"], "w_up": v["ffn_w_up"],
        "w_down": v["ffn_w_down"], "cols": _columns(np, v), "tables": _tables(np),
    }
    arrays = {f"in_{name}": np.ascontiguousarray(a) for name, a in arrays.items()}
    nc = bacc.Bacc("TRN2", target_bir_lowering=False, num_devices=1)
    args = [nc.dram_tensor(name, a.shape, mb.dt.from_np(a.dtype), kind="ExternalInput").ap()
            for name, a in arrays.items()]
    shape = v["x"].shape
    out = nc.dram_tensor("out_y", shape[1:], mb.dt.float32, kind="ExternalOutput").ap()
    encoder_kernel(nc, *args, out)
    result = run_bass_kernel_spmd(nc, [arrays], core_ids=[0])
    return result.results[0]["out_y"].reshape(shape)
```

```python
from contextlib import ExitStack

import concourse.bass as bass
from concourse import mybir

F32 = mybir.dt.float32
F32R = mybir.dt.float32r
ALU = mybir.AluOpType
ACT = mybir.ActivationFunctionType
AX_X = mybir.AxisListType.X

P = 128
NB = 512
RING = 4
SLOT_K = 2
RMS_EPS = 1e-6
LN_EPS = 1e-5


def ds(start, size):
    return bass.ds(start, size)


class Plan:

    def __init__(self):
        self.slots = 0
        self.pair_uses = [0, 0, 0]
        self.jobs = {}
        self.groups = {}
        self.bank_uses = [0, 0]
        self.highs = {}
        self.lows = {}

    def job(self, name, pair, k_tiles, adds=False):
        if adds:
            self.pair_uses[pair] -= 1
        self.jobs[name] = (self.slots, pair, self.pair_uses[pair])
        self.slots += k_tiles // SLOT_K
        self.pair_uses[pair] += 1

    def group(self, name, high=False, low=False):
        n = len(self.groups)
        self.groups[name] = (n, n % 2, self.bank_uses[n % 2])
        self.bank_uses[n % 2] += 1
        if high:
            self.split(name, low)

    def split(self, name, low=True):
        self.highs[name] = len(self.highs)
        if low:
            self.lows[name] = len(self.lows)


def encoder_kernel(nc, x_in, w_in, w_out, sc_in, sc_out, w_gate, w_up, w_down, cols_in, tables_in, out):
    SEQ, D = x_in.shape
    FF = w_gate.shape[2]
    DEPTH = w_gate.shape[0]
    TT = SEQ // P
    KD = D // P
    KF = FF // P
    NJ = D // NB
    NF = FF // NB
    BK = NB // P
    CHUNK, HD, HQ, HKV = 64, 64, 16, 2
    GQ = HQ // HKV
    AW = HQ * HD
    CC = D - AW
    KC = CC // P
    TAPS = 31
    PAD = TAPS - 1
    KVW = HKV * HD
    assert TT == 2 and DEPTH == 2 and KVW == P and CC == 2 * NB and AW == 2 * NB
    SD = KD // SLOT_K
    SF = KF // SLOT_K
    SH = SD // 2

    MIXG, FFNG = 0, DEPTH * KD
    DWW = FFNG + DEPTH * KD
    DWB = DWW + KC * TAPS
    LNG = DWB + KC
    LNB = LNG + KC
    SCW = LNB + KC
    QG = SCW + 3 * KD
    KG = QG + HD
    SINK = KG + HD
    NCOLS = SINK + HQ

    plan = Plan()
    for b in range(NJ):
        for t in range(TT):
            plan.group(("x", 0, b, t), high=True, low=True)
    plan.job("g0", 1, KD)
    plan.job("a0", 0, KD)
    plan.job("kv", 1, KD)
    plan.group(("u", 0, 0)), plan.group(("u", 0, 1))
    plan.job("q0", 0, KD)
    plan.group("kT")
    plan.job("q1", 1, KD)
    plan.job("g1", 0, KD)
    plan.job("a1", 1, KD)
    OUT_ORDER = ((0, 0), (0, 1), (1, 0), (1, 1), (0, 2), (1, 2), (0, 3), (1, 3))
    for g, nb in OUT_ORDER:
        plan.job(("attn_out", g, nb), nb % 2, KC // 2, adds=(g == 1))
    P_GROUPS = (2, 4, 2, 4)
    P_BEFORE = (0, 2, 6, 8)
    def plan_queries(g):
        for t in range(TT):
            plan.group(("qT", g, t))

    def plan_scores(hh):
        for r in range(4):
            plan.group(("sc", hh, r))

    def plan_probs(hh):
        for r in range(P_GROUPS[hh]):
            plan.group(("p", hh, r))

    def plan_heads(g):
        for t in range(TT):
            plan.group(("o", g, t), high=True)

    plan_queries(0), plan_scores(0), plan_scores(1), plan_probs(0), plan_probs(1)
    plan_queries(1), plan_scores(2), plan_heads(0), plan_scores(3), plan_probs(2), plan_probs(3)
    plan.group(("u", 1, 0)), plan.group(("u", 1, 1))
    plan_heads(1)
    plan.group("mean")
    plan.group("var")
    for q in range(KC // 2):
        plan.split(("ln", q))
    for nb in range(NJ):
        plan.job(("conv_out", nb), nb % 2, KD // 2)
    for b in range(NJ):
        for t in range(TT):
            plan.group(("x", 1, b, t), high=True, low=True)

    def plan_ffn(layer, norm_after):
        for i in range(NF):
            plan.job(("gate", layer, i), 0, KD)
            plan.job(("up", layer, i), 1, KD)
            for t in range(TT):
                plan.group(("y", layer, i, t), high=True)
        for nb in range(NJ):
            plan.job(("down", layer, nb), nb % 2, KF)
        if norm_after is not None:
            for b in range(NJ):
                for t in range(TT):
                    plan.group(("x", norm_after, b, t), high=True, low=True)

    plan_ffn(0, 2)
    for j in range(NJ):
        plan.job(("cg", j), 0, KD)
        plan.job(("cu", j), 1, KD)
        plan.job(("bg", j), 2, KD)
        for t in range(TT):
            plan.group(("c", j, t))
        for t in range(TT):
            plan.group(("z", j, t), high=True, low=True)
    for nb in range(NJ):
        plan.job(("sc_out", nb), nb % 2, KD)
    for b in range(NJ):
        for t in range(TT):
            plan.group(("x", 3, b, t), high=True, low=True)
    plan_ffn(1, None)
    JOB, GROUP, HIGH, LOW, SLOTS = plan.jobs, plan.groups, plan.highs, plan.lows, plan.slots
    assert SLOTS % RING == 0
    assert all(JOB[("gate", la, 0)][0] % RING == 0 for la in range(DEPTH)) and JOB[("cg", 0)][0] % RING == 0

    with ExitStack() as ctx:
        def sb(name, shape, dt=F32, stack=ctx):
            return stack.enter_context(nc.sbuf_tensor(name, shape, dt))

        def sem(name):
            return ctx.enter_context(nc.semaphore(name))

        xs = sb("xs", [P, TT, D])
        xT_hi = sb("xT_hi", [P, KD, SEQ], F32R)
        xT_lo = sb("xT_lo", [P, KD, SEQ], F32R)
        w_raw = sb("w_raw", [P, RING, SLOT_K, NB])
        w_hi = sb("w_hi", [P, RING, SLOT_K, NB], F32R)
        w_lo = sb("w_lo", [P, RING, SLOT_K, NB], F32R)
        cols = sb("cols", [P, NCOLS])
        tables = sb("tables", [P, P + P + SEQ])
        ident = tables[:, 0:P]
        dist = [tables[:, P:2 * P], tables[:, 2 * P:2 * P + SEQ]]
        mixed = sb("mixed", [P, TT, NB])
        gated = sb("gated", [P, TT, NB])
        scaled = sb("scaled", [P, TT, BK, P])
        junk = sb("junk", [P, NB])
        sumsq = sb("sumsq", [P, TT, NJ])
        meansq = sb("meansq", [P, TT])
        root = sb("root", [P, TT])
        newton = sb("newton", [P, TT])
        rstd = sb("rstd", [P, TT])
        idle = sb("idle", [P, TT])

        with ExitStack() as early:
            mT_hi = sb("mT_hi", [P, KD, SEQ], F32R, early)
            mT_lo = sb("mT_lo", [P, KD, SEQ], F32R, early)
            uT = sb("uT", [P, KC, PAD + SEQ], F32, early)
            cv = sb("cv", [P, KC, SEQ], F32, early)
            products = sb("products", [P, 4, SEQ], F32, early)
            qT = sb("qT", [P, GQ, SEQ], F32, early)
            kT = sb("kT", [P, HKV, SEQ], F32, early)
            kv_tok = sb("kv_tok", [P, TT, 2 * KVW], F32, early)
            k_twice = sb("k_twice", [P, TT, HKV, 2, HD], F32, early)
            q_tok = sb("q_tok", [P, TT, AW], F32, early)
            scores = [sb("scores0", [P, GQ, P], F32, early), sb("scores1", [P, GQ, SEQ], F32, early)]
            ln_v = sb("ln_v", [P, SEQ], F32, early)
            ln_r = sb("ln_r", [P, SEQ], F32, early)
            ln_t = sb("ln_t", [P, SEQ], F32, early)
            ones = sb("ones", [P, P], F32, early)
            k_gain = sb("k_gain", [P, HD], F32, early)
            qk_ms = [sb(f"qk_ms{n}", [P, TT, HKV if n == 0 else GQ], F32, early) for n in range(3)]
            qk_r = [sb(f"qk_r{n}", [P, TT, HKV if n == 0 else GQ], F32, early) for n in range(3)]
            qk_t = [sb(f"qk_t{n}", [P, TT, HKV if n == 0 else GQ], F32, early) for n in range(3)]
            top = sb("top", [P, TT, GQ], F32, early)
            neg_top = sb("neg_top", [P, TT, GQ], F32, early)
            sink_d = sb("sink_d", [P, TT, GQ], F32, early)
            sink_e = sb("sink_e", [P, TT, GQ], F32, early)
            den = sb("den", [P, TT, GQ], F32, early)
            rden = sb("rden", [P, TT, GQ], F32, early)
        with ExitStack() as late:
            yT_hi = sb("yT_hi", [P, KF, SEQ], F32R, late)
            yT_lo = sb("yT_lo", [P, KF, SEQ], F32R, late)
        with ExitStack() as late:
            zT_hi = sb("zT_hi", [P, KD, SEQ], F32R, late)
            zT_lo = sb("zT_lo", [P, KD, SEQ], F32R, late)
            bg_tok = sb("bg_tok", [P, TT, NB], F32, late)
            cT = sb("cT", [P, BK, 2 + SEQ], F32, late)
            zc = sb("zc", [P, BK, SEQ], F32, late)
        ln_sq = q_tok[:, :, :].rearrange("p t (c k) -> p (t c) k", k=SEQ)
        probs = scaled[:, :, :, :].rearrange("p t k n -> p t (k n)")
        q_sq = mixed[:, :, :]

        pool_taps = [(c, k) for k in range(TAPS) for c in (0, 1)] + [(4, k) for k in range(TAPS)]
        dve_taps = [(c, k) for k in range(TAPS) for c in (2, 3)]
        EARLY_TAPS = len(dve_taps)
        dve_taps += [(c, k) for k in range(TAPS) for c in (5, 6)] + [(7, k) for k in range(TAPS)]
        acc_place = {2: 0, 3: 1, 5: 0, 6: 1, 7: 0}
        FIRST_TAP, SECOND_TAPS = JOB["kv"][0] + 7, JOB[("attn_out", 0, 0)][0] + 5

        def products_by(s):
            if s < SECOND_TAPS:
                return max(0, min(2 * (s - FIRST_TAP + 1), 2 * TAPS))
            return 2 * TAPS + min(3 * (s - SECOND_TAPS + 1), TAPS)

        def pool_adds(n):
            return sum(k > 0 for _, k in pool_taps[:n + 1])

        pairs = [[ctx.enter_context(nc.psum_tensor(f"pair{p}_{t}", [P, NB], F32)) for t in range(TT)]
                 for p in range(3)]
        tbank = [ctx.enter_context(nc.psum_tensor(f"tbank{b}", [P, NB], F32)) for b in range(2)]
        conv_acc = pairs[2][0]
        heads_acc = pairs[2][1]

        x_loaded = [sem(f"x_loaded{b}") for b in range(NJ)]
        cols_loaded = sem("cols_loaded")
        tables_loaded = sem("tables_loaded")
        w_loaded = [sem(f"w_loaded{r}") for r in range(RING)]
        w_hi_ready = sem("w_hi_ready")
        w_lo_even = sem("w_lo_even")
        w_lo_odd = sem("w_lo_odd")
        w_used = sem("w_used")
        pair_read = [sem(f"pair_read{p}") for p in range(3)]
        t_ready = sem("t_ready")
        t_read = [sem(f"t_read{b}") for b in range(2)]
        hi_ready = sem("hi_ready")
        lo_ready = sem("lo_ready")
        sumsq_ready = sem("sumsq_ready")
        meansq_ready = sem("meansq_ready")
        root_ready = sem("root_ready")
        rstd_ready = sem("rstd_ready")
        pad_ready = sem("pad_ready")
        ones_ready = sem("ones_ready")
        q_sq_ready = sem("q_sq_ready")
        qk_ms_ready = sem("qk_ms_ready")
        qk_root_ready = sem("qk_root_ready")
        qk_normed = sem("qk_normed")
        top_ready = sem("top_ready")
        p_ready = sem("p_ready")
        pv_done = sem("pv_done")
        o_ready = sem("o_ready")
        tap_done = sem("tap_done")
        product_ready = sem("product_ready")
        pool_tap_done = sem("pool_tap_done")
        cv_centered = sem("cv_centered")
        ln_sq_ready = sem("ln_sq_ready")
        ln_v_ready = sem("ln_v_ready")
        ln_root_ready = sem("ln_root_ready")
        ln_scaled = sem("ln_scaled")
        silu_done = sem("silu_done")
        c3_done = sem("c3_done")
        dve_step = sem("dve_step")
        act_step = sem("act_step")
        stored = sem("stored")

        def col(c, n=1):
            return cols[:, c:c + n]

        def tok(t):
            return slice(t * P, (t + 1) * P)

        def blk(b):
            return slice(b * NB, (b + 1) * NB)

        def bank4(b):
            return tbank[b][:, :].rearrange("p (k n) -> p k n", n=P)

        block = ctx.enter_context(nc.Block())

        @block.sync
        def _(sp):
            def place_free(s, per=0, rep=0):
                if s >= RING:
                    sp.wait_ge(w_lo_odd if s % 2 else w_lo_even, (s - RING) // 2 + 1 + (per // 2) * rep)

            def load_slot(s, source, cols_n=NB):
                r = s % RING
                sp.dma_start(w_raw[:, r, :, 0:cols_n], source).then_inc(w_loaded[r], 16)

            def load_job(s0, w, k0, slots, start, per=0, rep=0, cols_n=NB, swap=False):
                view = w.rearrange("(k p) n -> p k n", p=P)[:, :, ds(start, cols_n)]
                for q in ([1, 0] if swap else [0, 1]) + list(range(2, slots)):
                    k = k0 + SLOT_K * q
                    if swap and q == 1:
                        place_free(s0, per, rep)
                    if not (swap and q == 0):
                        place_free(s0 + q, per, rep)
                    load_slot(s0 + q, view[:, k:k + SLOT_K, :], cols_n)

            first = w_in.rearrange("(k p) n -> p k n", p=P)
            for b in range(NJ):
                sp.dma_start(xs[:, :, blk(b)],
                             x_in.rearrange("(t p) n -> p t n", p=P)[:, :, blk(b)]).then_inc(x_loaded[b], 16)
                load_slot(b, first[:, SLOT_K * b:SLOT_K * (b + 1), ds(CC, NB)])
            starts = {"g0": CC, "a0": 0, "kv": 2 * CC + AW, "q0": 2 * CC, "q1": 2 * CC + NB,
                      "g1": CC + NB, "a1": NB}
            for name, start in starts.items():
                s0, done = JOB[name][0], NJ if name == "g0" else 0
                load_job(s0 + done, w_in, SLOT_K * done, SD - done, start, cols_n=2 * KVW if name == "kv" else NB)
            for g, nb in OUT_ORDER:
                load_job(JOB[("attn_out", g, nb)][0], w_out, KC + KC // 2 * g, SH // 2, nb * NB)
            for nb in range(NJ):
                load_job(JOB[("conv_out", nb)][0], w_out, 0, SH, nb * NB)

            def ffn(layer):
                s0 = JOB[("gate", layer, 0)][0]
                with sp.Fori(1, NF + 1) as n:
                    i = n - 1
                    load_job(s0, w_gate[layer], 0, SD, i * NB, 2 * SD, i)
                    load_job(s0 + SD, w_up[layer], 0, SD, i * NB, 2 * SD, i)
                for nb in range(NJ):
                    load_job(JOB[("down", layer, nb)][0], w_down[layer], 0, SF, nb * NB)

            ffn(0)
            s0 = JOB[("cg", 0)][0]
            with sp.Fori(1, NJ + 1) as n:
                j = n - 1
                load_job(s0, sc_in, 0, SD, j * NB + D, 3 * SD, j)
                load_job(s0 + SD, sc_in, 0, SD, j * NB + 2 * D, 3 * SD, j)
                load_job(s0 + 2 * SD, sc_in, 0, SD, j * NB, 3 * SD, j, swap=True)
            for nb in range(NJ):
                load_job(JOB[("sc_out", nb)][0], sc_out, 0, SD, nb * NB)
            ffn(1)
            for nb in range(NJ):
                _, pair, uses = JOB[("down", 1, nb)]
                sp.wait_ge(pair_read[pair], uses + 1)
                sp.dma_start(out.rearrange("(t p) n -> p t n", p=P)[:, :, blk(nb)],
                             xs[:, :, blk(nb)]).then_inc(stored, 16)
            sp.wait_ge(stored, 16 * NJ)

        @block.gpsimd
        def _(pool):
            nc.gpsimd.memset(ones[:, :], 1.0 / CC).then_inc(ones_ready, 1)

            def low(s, place):
                pool.wait_ge(w_hi_ready, s + 1)
                nc.gpsimd.tensor_tensor(w_lo[:, place, :, :], w_raw[:, place, :, :],
                                        w_hi[:, place, :, :].bitcast(F32), ALU.subtract).then_inc(w_lo_odd, 1)

            def add_taps(a, b):
                for n in range(a, min(b, len(pool_taps))):
                    c, k = pool_taps[n]
                    if k == 0:
                        continue
                    pool.wait_ge(product_ready, n + 1)
                    if k > 1:
                        pool.wait_ge(pool_tap_done, pool_adds(pool_taps.index((c, k - 1))))
                    nc.gpsimd.tensor_tensor(cv[:, c, :], products[:, n % 4, :], cv[:, c, :],
                                            ALU.add).then_inc(pool_tap_done, 1)

            first_ffn = JOB[("gate", 0, 0)][0]
            for s in range(1, first_ffn, 2):
                low(s, s % RING)
                add_taps(products_by(s - 2), products_by(s))

            with pool.Fori(first_ffn // RING, SLOTS // RING) as i:
                for r in range(1, RING, 2):
                    low(RING * i + r, r)

        @block.tensor
        def _(pe):
            def slots(job, q0, q1, hi, lo, k0=0, per=0, rep=0, pair_per=0, n=NB, last=None, adds=False):
                s0, pair, uses = JOB[job]
                last = q1 if last is None else last
                if q0 == 0 and not adds and (uses or pair_per):
                    pe.wait_ge(pair_read[pair], uses + pair_per * rep)
                for q in range(q0, q1):
                    s = s0 + q
                    r = s % RING
                    pe.wait_ge(w_lo_odd if s % 2 else w_lo_even, s // 2 + 1 + (per // 2) * rep)
                    for kk in range(SLOT_K):
                        k = k0 + SLOT_K * q + kk
                        first, end = (q == 0 and kk == 0 and not adds), (q == last - 1 and kk == SLOT_K - 1)
                        for t in range(TT):
                            o = pairs[pair][t][:, 0:n]
                            nc.tensor.matmul(o, hi[:, k, tok(t)], w_hi[:, r, kk, 0:n], start=first, stop=False)
                            nc.tensor.matmul(o, hi[:, k, tok(t)], w_lo[:, r, kk, 0:n], start=False, stop=False)
                            mm = nc.tensor.matmul(o, lo[:, k, tok(t)], w_hi[:, r, kk, 0:n], start=False, stop=end)
                    mm.then_inc(w_used, 1)

            def bank_free(group, per=0, rep=0):
                _, b, uses = GROUP[group]
                if uses:
                    pe.wait_ge(t_read[b], uses + per * rep)
                return b

            def transposes(group, sources, per=0, rep=0):
                b = bank_free(group, per, rep)
                for n, source in enumerate(sources):
                    mm = nc.tensor.transpose(tbank[b][:, n * P:(n + 1) * P], source, ident)
                mm.then_inc(t_ready, 1)

            def x_transposes(norm, b):
                for t in range(TT):
                    transposes(("x", norm, b, t),
                               [xs[:, t, b * NB + k * P:b * NB + (k + 1) * P] for k in range(BK)])

            def x_split(norm, b):
                pe.wait_ge(lo_ready, LOW[("x", norm, b, TT - 1)] + 1)

            def read_out(job, per=0, rep=0):
                _, pair, uses = JOB[job]
                pe.wait_ge(pair_read[pair], uses + 1 + per * rep)

            def block_transposes(name, source, per=0, rep=0):
                for t in range(TT):
                    transposes(name + (t,), [source[:, t, k * P:(k + 1) * P] for k in range(BK)], per, rep)

            pe.wait_ge(tables_loaded, 16)
            def x_arrived(b):
                pe.wait_ge(x_loaded[b], 16)
                x_transposes(0, b)

            x_arrived(0)
            x_arrived(1)

            def keys_of(t):
                return P if t == 0 else SEQ

            def query_transposes(g):
                pe.wait_ge(qk_normed, 2 + g)
                for t in range(TT):
                    transposes(("qT", g, t), [q_tok[:, t, (4 * g + j) * P:(4 * g + j + 1) * P] for j in range(4)])

            def score_products(hh, r0, r1):
                g, t = hh // 2, hh % 2
                _, b, uses = GROUP[("qT", g, t)]
                pe.wait_ge(t_read[b], uses + 1)
                for r in range(r0, r1):
                    b = bank_free(("sc", hh, r))
                    e = r % 2
                    for m in range(2):
                        mm = nc.tensor.matmul(tbank[b][:, m * SEQ:m * SEQ + keys_of(t)],
                                              qT[e * HD:(e + 1) * HD, 4 * g + 2 * (r // 2) + m, tok(t)],
                                              kT[e * HD:(e + 1) * HD, g, 0:keys_of(t)], start=True, stop=True)
                    mm.then_inc(t_ready, 1)

            def prob_transposes(hh, r0, r1):
                kb = 1 + hh % 2
                per = 4 // kb
                if r0 == 0:
                    pe.wait_ge(p_ready, hh + 1)
                for r in range(r0, r1):
                    transposes(("p", hh, r), [scores[hh % 2][:, per * r + m, c * P:(c + 1) * P]
                                              for m in range(per) for c in range(kb)])

            def value_products(hh, r0, r1):
                kb = 1 + hh % 2
                per = 4 // kb
                g = hh // 2
                if r0 == 0 and hh:
                    pe.wait_ge(o_ready, hh)
                for r in range(r0, r1):
                    _, b, uses = GROUP[("p", hh, r)]
                    pe.wait_ge(t_read[b], uses + 1)
                    for m in range(per):
                        j = per * r + m
                        for c in range(kb):
                            at = (m * kb + c) * P
                            mm = nc.tensor.matmul(heads_acc[:, j * HD:(j + 1) * HD],
                                                  probs[:, (P_BEFORE[hh] + r) % 2, at:at + P],
                                                  kv_tok[:, c, KVW + g * HD:KVW + (g + 1) * HD],
                                                  start=(c == 0), stop=(c == kb - 1))
                    mm.then_inc(pv_done, 1)

            def heads_transposes(g):
                for t in range(TT):
                    pe.wait_ge(o_ready, 2 * g + t + 1)
                    transposes(("o", g, t), [q_tok[:, t, (4 * g + k) * P:(4 * g + k + 1) * P] for k in range(4)])

            for b in range(NJ):
                x_split(0, b)
                slots("g0", 2 * b, 2 * b + 2, xT_hi, xT_lo, last=SD)
                if b + 2 < NJ:
                    x_arrived(b + 2)
            slots("a0", 0, SD, xT_hi, xT_lo)
            slots("kv", 0, 4, xT_hi, xT_lo, n=2 * KVW, last=SD)
            read_out("a0")
            block_transposes(("u", 0), mixed)
            slots("kv", 4, SD, xT_hi, xT_lo, n=2 * KVW)
            slots("q0", 0, 6, xT_hi, xT_lo, last=SD)
            pe.wait_ge(qk_normed, 1)
            transposes("kT", [k_twice[:, t, g, :, :].rearrange("p w d -> p (w d)")
                              for g in range(HKV) for t in range(TT)])
            slots("q0", 6, SD, xT_hi, xT_lo)
            slots("q1", 0, 5, xT_hi, xT_lo, last=SD)
            query_transposes(0)
            slots("q1", 5, 6, xT_hi, xT_lo, last=SD)
            score_products(0, 0, 2)
            slots("q1", 6, 7, xT_hi, xT_lo, last=SD)
            score_products(0, 2, 4)
            slots("q1", 7, SD, xT_hi, xT_lo)
            score_products(1, 0, 2)
            slots("g1", 0, 1, xT_hi, xT_lo, last=SD)
            score_products(1, 2, 4)
            slots("g1", 1, 3, xT_hi, xT_lo, last=SD)
            prob_transposes(0, 0, 2)
            slots("g1", 3, 4, xT_hi, xT_lo, last=SD)
            value_products(0, 0, 2)
            slots("g1", 4, 5, xT_hi, xT_lo, last=SD)
            prob_transposes(1, 0, 2)
            slots("g1", 5, 6, xT_hi, xT_lo, last=SD)
            value_products(1, 0, 2)
            prob_transposes(1, 2, 4)
            slots("g1", 6, 7, xT_hi, xT_lo, last=SD)
            value_products(1, 2, 4)
            query_transposes(1)
            slots("g1", 7, SD, xT_hi, xT_lo)
            score_products(2, 0, 2)
            slots("a1", 0, 1, xT_hi, xT_lo, last=SD)
            score_products(2, 2, 4)
            heads_transposes(0)
            slots("a1", 1, 2, xT_hi, xT_lo, last=SD)
            score_products(3, 0, 2)
            slots("a1", 2, 3, xT_hi, xT_lo, last=SD)
            score_products(3, 2, 4)
            slots("a1", 3, 5, xT_hi, xT_lo, last=SD)
            prob_transposes(2, 0, 2)
            slots("a1", 5, 6, xT_hi, xT_lo, last=SD)
            value_products(2, 0, 2)
            slots("a1", 6, 7, xT_hi, xT_lo, last=SD)
            prob_transposes(3, 0, 2)
            slots("a1", 7, SD, xT_hi, xT_lo)

            def attn_out(n, q0, q1):
                g, nb = OUT_ORDER[n]
                slots(("attn_out", g, nb), q0, q1, mT_hi, mT_lo, k0=KC + KC // 2 * g, last=2 if g else SD,
                      adds=(g == 1))

            def heads_split(g):
                for t in range(TT):
                    _, b, uses = GROUP[("o", g, t)]
                    pe.wait_ge(t_read[b], uses + 1)

            heads_split(0)
            value_products(3, 0, 2)
            prob_transposes(3, 2, 4)
            attn_out(0, 0, 1)
            read_out("a1")
            block_transposes(("u", 1), mixed)
            value_products(3, 2, 4)
            attn_out(0, 1, 2)
            attn_out(1, 0, 1)
            heads_transposes(1)
            attn_out(1, 1, 2)
            heads_split(1)
            for n in range(2, len(OUT_ORDER)):
                attn_out(n, 0, 2)

            pe.wait_ge(ones_ready, 1)
            b = bank_free("mean")
            for c in range(KC):
                if (c, TAPS - 1) in dve_taps:
                    pe.wait_ge(tap_done, dve_taps.index((c, TAPS - 1)) + 1)
                else:
                    pe.wait_ge(pool_tap_done, pool_adds(pool_taps.index((c, TAPS - 1))))
                mm = nc.tensor.matmul(tbank[b][:, 0:SEQ], ones[:, :], cv[:, c, :], start=(c == 0), stop=(c == KC - 1))
            mm.then_inc(t_ready, 1)
            b = bank_free("var")
            for c in range(KC):
                if c % 2 == 0:
                    pe.wait_ge(ln_sq_ready, c // 2 + 1)
                mm = nc.tensor.matmul(tbank[b][:, 0:SEQ], ones[:, :], ln_sq[:, c, :], start=(c == 0), stop=(c == KC - 1))
            mm.then_inc(t_ready, 1)

            for nb in range(NJ):
                job = ("conv_out", nb)
                if nb == 0:
                    for q in range(SH):
                        pe.wait_ge(lo_ready, LOW[("ln", q)] + 1)
                        slots(job, q, q + 1, mT_hi, mT_lo, last=SH)
                else:
                    slots(job, 0, 2, mT_hi, mT_lo, last=SH)
                    read_out(("conv_out", nb - 1))
                    x_transposes(1, nb - 1)
                    slots(job, 2, SH, mT_hi, mT_lo)

            def first_block(job, norm, last_out, last=SD):
                for b in range(2):
                    x_split(norm, b)
                    slots(job, 2 * b, 2 * b + 2, xT_hi, xT_lo, last=last)
                read_out(last_out)
                x_transposes(norm, NJ - 1)
                x_split(norm, 2)
                slots(job, 4, 6, xT_hi, xT_lo, last=last)
                x_split(norm, 3)
                slots(job, 6, SD, xT_hi, xT_lo)

            def ffn(layer, norm, last_out, norm_after):
                first_block(("gate", layer, 0), norm, last_out)
                slots(("up", layer, 0), 0, SD, xT_hi, xT_lo)
                with pe.Fori(1, NF) as i:
                    args = dict(per=2 * SD, rep=i, pair_per=1)
                    slots(("gate", layer, 0), 0, 4, xT_hi, xT_lo, last=SD, **args)
                    read_out(("up", layer, 0), 1, i - 1)
                    block_transposes(("y", layer, 0), mixed, 1, i - 1)
                    slots(("gate", layer, 0), 4, SD, xT_hi, xT_lo, **args)
                    slots(("up", layer, 0), 0, SD, xT_hi, xT_lo, **args)
                for nb in range(NJ):
                    job = ("down", layer, nb)
                    slots(job, 0, 4, yT_hi, yT_lo, last=SF)
                    if nb == 0:
                        read_out(("up", layer, NF - 1))
                        block_transposes(("y", layer, NF - 1), mixed)
                    elif norm_after is not None:
                        read_out(("down", layer, nb - 1))
                        x_transposes(norm_after, nb - 1)
                    slots(job, 4, SF - 2, yT_hi, yT_lo, last=SF)
                    if nb == 0:
                        for t in range(TT):
                            _, b, uses = GROUP[("y", layer, NF - 1, t)]
                            pe.wait_ge(t_read[b], uses + 1)
                    slots(job, SF - 2, SF, yT_hi, yT_lo)

            ffn(0, 1, ("conv_out", NJ - 1), 2)

            first_block(("cg", 0), 2, ("down", 0, NJ - 1))
            slots(("cu", 0), 0, SD, xT_hi, xT_lo)
            slots(("bg", 0), 0, 4, xT_hi, xT_lo, last=SD)
            read_out(("cu", 0))
            block_transposes(("c", 0), mixed)
            slots(("bg", 0), 4, SD, xT_hi, xT_lo)
            with pe.Fori(1, NJ) as j:
                args = dict(per=3 * SD, rep=j, pair_per=1)
                slots(("cg", 0), 0, 4, xT_hi, xT_lo, last=SD, **args)
                read_out(("bg", 0), 1, j - 1)
                block_transposes(("z", 0), bg_tok, 2, j - 1)
                slots(("cg", 0), 4, SD, xT_hi, xT_lo, **args)
                slots(("cu", 0), 0, SD, xT_hi, xT_lo, **args)
                slots(("bg", 0), 0, 4, xT_hi, xT_lo, last=SD, **args)
                read_out(("cu", 0), 1, j)
                block_transposes(("c", 0), mixed, 2, j)
                slots(("bg", 0), 4, SD, xT_hi, xT_lo, **args)
            for nb in range(NJ):
                job = ("sc_out", nb)
                if nb == 0:
                    pe.wait_ge(lo_ready, LOW[("z", NJ - 2, TT - 1)] + 1)
                slots(job, 0, 4, zT_hi, zT_lo, last=SD)
                if nb == 0:
                    read_out(("bg", NJ - 1))
                    block_transposes(("z", NJ - 1), bg_tok)
                    slots(job, 4, 6, zT_hi, zT_lo, last=SD)
                    pe.wait_ge(lo_ready, LOW[("z", NJ - 1, TT - 1)] + 1)
                    slots(job, 6, SD, zT_hi, zT_lo)
                else:
                    read_out(("sc_out", nb - 1))
                    x_transposes(3, nb - 1)
                    slots(job, 4, SD, zT_hi, zT_lo)

            ffn(1, 3, ("sc_out", NJ - 1), None)

        @block.scalar
        def _(act):
            steps = [0]

            def link(ins):
                steps[0] += 1
                ins.then_inc(act_step, 1)
                act.wait_ge(act_step, steps[0])

            def highs(s_from, s_to, per=0, rep=0):
                for s in range(s_from, min(s_to, SLOTS)):
                    r = s % RING
                    act.wait_ge(w_loaded[r], 16 * (s // RING + 1) + (16 * per // RING) * rep)
                    if s >= RING:
                        act.wait_ge(w_used, s - RING + 1 + per * rep)
                    nc.scalar.activation(w_hi[:, r, :, :], w_raw[:, r, :, :], ACT.Copy).then_inc(w_hi_ready, 1)

            def job_done(job, per=0, rep=0, slots=SD):
                s0, pair, _ = JOB[job]
                act.wait_ge(w_used, s0 + slots + per * rep)
                return pair

            def high_of_scaled(name, dest, k, t, per=0, rep=0, bank_per=0, scaled_t=None):
                _, b, uses = GROUP[name]
                act.wait_ge(t_read[b], uses + 1 + bank_per * rep)
                nc.scalar.activation(dest[:, k, tok(t)], scaled[:, t, :, :], ACT.Copy).then_inc(hi_ready, 1)

            def x_highs(norm, b):
                for t in range(TT):
                    high_of_scaled(("x", norm, b, t), xT_hi, slice(BK * b, BK * (b + 1)), t)

            def high_of_group(name, dest, k, t, per=0, rep=0):
                n, b, _ = GROUP[name]
                act.wait_ge(t_ready, n + 1 + per * rep)
                nc.scalar.activation(dest[:, k, tok(t)], bank4(b), ACT.Copy).then_inc(hi_ready, 1)

            def copy_group(name, dest):
                n, b, _ = GROUP[name]
                act.wait_ge(t_ready, n + 1)
                src = tbank[b][:, :]
                if len(dest.shape) == 3:
                    src = src.rearrange("p (k n) -> p k n", n=dest.shape[2])
                nc.scalar.activation(dest, src, ACT.Copy).then_inc(t_read[b], 1)

            def x_squares(b):
                for t in range(TT):
                    link(nc.scalar.activation(junk[:, :], xs[:, t, blk(b)], ACT.Square,
                                              accum_out=sumsq[:, t, b:b + 1]))
                if b == NJ - 1:
                    nc.scalar.activation(junk[:, :], xs[:, 0, blk(b)], ACT.Copy).then_inc(sumsq_ready, 1)

            def norm_root(norm):
                act.wait_ge(meansq_ready, norm + 1)
                nc.scalar.activation(root[:, :], meansq[:, :], ACT.Sqrt).then_inc(root_ready, 1)

            def read_pair(job, func, dest, width=NB, per=0, rep=0):
                pair = job_done(job, per, rep)
                for t in range(TT):
                    ins = nc.scalar.activation(dest[:, t, 0:width], pairs[pair][t][:, 0:width], func,
                                               scale=rstd[:, t:t + 1])
                ins.then_inc(pair_read[pair], 1)

            act.dma_start(tables[:, :], tables_in).then_inc(tables_loaded, 16)
            act.dma_start(cols[:, :], cols_in).then_inc(cols_loaded, 16)
            highs(0, 1)
            for b in range(NJ):
                x_highs(0, b)
                highs(max(2 * b, 1), 2 * b + 2)
                x_squares(b)
            norm_root(0)

            def read_by_other(job):
                _, pair, uses = JOB[job]
                act.wait_ge(pair_read[pair], uses + 1)

            def tap_products(a, b):
                for n in range(a, min(b, len(pool_taps))):
                    c, k = pool_taps[n]
                    u, w = uT[:, c, k:k + SEQ], col(DWW + c * TAPS + k)
                    if k == 0:
                        nc.scalar.activation(cv[:, c, :], u, ACT.Identity, bias=col(DWB + c),
                                             scale=w).then_inc(product_ready, 1)
                        continue
                    if n >= 4 and pool_adds(n - 4):
                        act.wait_ge(pool_tap_done, pool_adds(n - 4))
                    nc.scalar.activation(products[:, n % 4, :], u, ACT.Copy, scale=w).then_inc(product_ready, 1)

            def highs_and_taps(s_from, s_to):
                for s in range(s_from, s_to):
                    highs(s, s + 1)
                    tap_products(products_by(s - 1), products_by(s))

            def root_of(n):
                act.wait_ge(qk_ms_ready, n + 1)
                nc.scalar.activation(qk_r[n][:, :, :], qk_ms[n][:, :, :], ACT.Sqrt).then_inc(qk_root_ready, 1)

            def query_squares(g):
                part = q_tok[:, :, g * NB:(g + 1) * NB]
                _, pair, uses = JOB[f"q{g}"]
                act.wait_ge(pair_read[pair], uses + 1)
                nc.scalar.activation(q_sq, part, ACT.Square).then_inc(q_sq_ready, 1)

            def exps(hh):
                t = hh % 2
                keys = P if t == 0 else SEQ
                act.wait_ge(top_ready, hh + 1)
                for j in range(GQ):
                    s = scores[t][:, j, 0:keys]
                    nc.scalar.activation(s, s, ACT.Exp, bias=neg_top[:, t, j:j + 1], accum_out=den[:, t, j:j + 1])
                nc.scalar.activation(sink_e[:, t, :], sink_d[:, t, :], ACT.Exp).then_inc(p_ready, 1)

            def prob_copies(hh, r0, r1):
                for r in range(r0, r1):
                    n = P_BEFORE[hh] + r
                    if n >= 2:
                        act.wait_ge(pv_done, n - 1)
                    copy_group(("p", hh, r), probs[:, n % 2, :])

            def heads_highs(g):
                for t in range(TT):
                    high_of_group(("o", g, t), mT_hi, slice(KC + 4 * g, KC + 4 * g + 4), t)

            def query_copies(g):
                for t in range(TT):
                    copy_group(("qT", g, t), qT[:, 4 * g:4 * g + 4, tok(t)])

            highs(8, 11)
            act.wait_ge(rstd_ready, 1)
            read_pair("g0", ACT.Sigmoid, gated)
            kv0, q00, q10, g10, a10 = (JOB[n][0] for n in ("kv", "q0", "q1", "g1", "a1"))
            ao0, co0 = JOB[("attn_out", 0, 0)][0], JOB[("conv_out", 0)][0]
            highs(11, kv0 + 7)
            act.wait_ge(pad_ready, 1)
            for t in range(TT):
                copy_group(("u", 0, t), uT[:, 0:BK, PAD + t * P:PAD + (t + 1) * P])
            for t in range(TT):
                _, b, uses = GROUP[("u", 0, t)]
                act.wait_ge(t_read[b], uses + 1)
            highs_and_taps(kv0 + 7, q00 + 3)
            read_pair("kv", ACT.Copy, kv_tok, 2 * KVW)
            highs_and_taps(q00 + 3, q00 + 6)
            root_of(0)
            highs_and_taps(q00 + 6, q10 + 1)
            copy_group("kT", kT[:, :, :].rearrange("p g n -> p (g n)"))
            highs_and_taps(q10 + 1, q10 + 3)
            read_pair("q0", ACT.Copy, q_tok[:, :, 0:NB])
            query_squares(0)
            highs_and_taps(q10 + 3, q10 + 5)
            root_of(1)
            highs_and_taps(q10 + 5, q10 + 8)
            query_copies(0)
            highs_and_taps(q10 + 8, g10 + 3)
            exps(0)
            read_pair("q1", ACT.Copy, q_tok[:, :, NB:2 * NB])
            query_squares(1)
            highs_and_taps(g10 + 3, g10 + 5)
            exps(1)
            prob_copies(0, 0, 2)
            highs_and_taps(g10 + 5, g10 + 6)
            root_of(2)
            highs_and_taps(g10 + 6, g10 + 8)
            prob_copies(1, 0, 2)
            highs_and_taps(g10 + 8, g10 + 9)
            prob_copies(1, 2, 4)
            highs_and_taps(g10 + 9, g10 + 10)
            query_copies(1)
            highs_and_taps(g10 + 10, a10 + 3)
            read_by_other("a0")
            read_pair("g1", ACT.Sigmoid, gated)
            highs_and_taps(a10 + 3, a10 + 4)
            heads_highs(0)
            highs_and_taps(a10 + 4, a10 + 5)
            exps(2)
            highs_and_taps(a10 + 5, a10 + 7)
            exps(3)
            highs_and_taps(a10 + 7, a10 + 8)
            prob_copies(2, 0, 2)
            highs_and_taps(a10 + 8, a10 + 10)
            prob_copies(3, 0, 2)
            highs_and_taps(a10 + 10, ao0 + 3)
            prob_copies(3, 2, 4)
            highs_and_taps(ao0 + 3, ao0 + 4)
            for t in range(TT):
                copy_group(("u", 1, t), uT[:, BK:2 * BK, PAD + t * P:PAD + (t + 1) * P])
            for t in range(TT):
                _, b, uses = GROUP[("u", 1, t)]
                act.wait_ge(t_read[b], uses + 1)
            highs_and_taps(ao0 + 4, ao0 + 6)
            heads_highs(1)
            highs_and_taps(ao0 + 6, co0 + 3)

            s0 = co0
            act.wait_ge(meansq_ready, 1)
            nc.scalar.activation(idle[:, :], meansq[:, :], ACT.Sqrt).then_inc(act_step, 1)
            for q in range(KC // 2):
                act.wait_ge(cv_centered, q + 1)
                nc.scalar.activation(ln_sq[:, 2 * q:2 * q + 2, :], cv[:, 2 * q:2 * q + 2, :],
                                     ACT.Square).then_inc(ln_sq_ready, 1)
            act.wait_ge(ln_v_ready, 1)
            nc.scalar.activation(ln_r[:, :], ln_v[:, :], ACT.Sqrt).then_inc(ln_root_ready, 1)
            steps[0] += 1
            act.wait_ge(act_step, steps[0])
            link(nc.scalar.activation(idle[:, :], meansq[:, :], ACT.Silu))
            highs(s0 + 3, s0 + 4)
            for q in range(KC // 2):
                act.wait_ge(ln_scaled, q + 1)
                for c in range(2 * q, 2 * q + 2):
                    ins = nc.scalar.activation(cv[:, c, :], cv[:, c, :], ACT.Silu,
                                               bias=col(LNB + c), scale=col(LNG + c))
                ins.then_inc(silu_done, 1)
                act.wait_ge(silu_done, q + 1)
                nc.scalar.activation(mT_hi[:, 2 * q:2 * q + 2, :], cv[:, 2 * q:2 * q + 2, :],
                                     ACT.Copy).then_inc(hi_ready, 1)
            at = s0 + 4
            for nb in range(1, NJ):
                after = s0 + SH * nb + 2
                highs(at, after + 3)
                at = after + 3
                x_highs(1, nb - 1)
                x_squares(nb - 1)

            def first_block(s0, at, norm):
                highs(at, s0 + 7)
                x_highs(norm, NJ - 1)
                x_squares(NJ - 1)
                norm_root(norm)
                highs(s0 + 7, s0 + SD + 3)
                act.wait_ge(rstd_ready, norm + 1)

            def ffn(layer, norm, at, norm_after):
                s0 = JOB[("gate", layer, 0)][0]
                first_block(s0, at, norm)
                read_pair(("gate", layer, 0), ACT.Silu, gated)
                highs(s0 + SD + 3, s0 + 2 * SD + 4)
                with act.Fori(1, NF) as i:
                    highs(s0 + 4, s0 + 7, 2 * SD, i)
                    for t in range(TT):
                        high_of_group(("y", layer, 0, t), yT_hi, ds(BK * (i - 1), BK), t, TT, i - 1)
                    highs(s0 + 7, s0 + SD + 3, 2 * SD, i)
                    act.wait_ge(pair_read[1], JOB[("up", layer, 0)][2] + i)
                    read_pair(("gate", layer, 0), ACT.Silu, gated, NB, 2 * SD, i)
                    highs(s0 + SD + 3, s0 + 2 * SD + 4, 2 * SD, i)
                at = s0 + 2 * SD * NF + 4
                for nb in range(NJ):
                    after = JOB[("down", layer, nb)][0] + 4
                    highs(at, after + 3)
                    at = after + 3
                    if nb == 0:
                        for t in range(TT):
                            high_of_group(("y", layer, NF - 1, t), yT_hi, slice(KF - BK, KF), t)
                    elif norm_after is not None:
                        x_highs(norm_after, nb - 1)
                        x_squares(nb - 1)
                return at

            at = ffn(0, 1, at, 2)

            s0 = JOB[("cg", 0)][0]

            def mixer_block(rep, from_c):
                per = 3 * SD
                if from_c:
                    act.wait_ge(pair_read[1], JOB[("cu", 0)][2] + rep)
                read_pair(("cg", 0), ACT.Copy, gated, NB, per, rep)
                highs(s0 + SD + 3, s0 + 2 * SD + 7, per, rep)
                if from_c:
                    act.wait_ge(c3_done, 3 * BK * rep)
                for t in range(TT):
                    n, b, _ = GROUP[("c", 0, t)]
                    act.wait_ge(t_ready, n + 1 + 2 * TT * rep)
                    nc.scalar.activation(cT[:, :, 2 + t * P:2 + (t + 1) * P], bank4(b),
                                         ACT.Copy).then_inc(t_read[b], 1)
                highs(s0 + 2 * SD + 7, s0 + 3 * SD + 3, per, rep)
                pair = JOB[("bg", 0)][1]
                act.wait_ge(w_used, s0 + 3 * SD + per * rep)
                for t in range(TT):
                    ins = nc.scalar.activation(bg_tok[:, t, :], pairs[pair][t][:, :], ACT.Copy,
                                               scale=rstd[:, t:t + 1])
                ins.then_inc(pair_read[pair], 1)
                highs(s0 + 3 * SD + 3, s0 + 3 * SD + 4, per, rep)

            first_block(s0, at, 2)
            mixer_block(0, False)
            with act.Fori(1, NJ) as j:
                highs(s0 + 4, s0 + 7, 3 * SD, j)
                for t in range(TT):
                    high_of_scaled(("z", 0, t), zT_hi, ds(BK * (j - 1), BK), t, rep=j - 1, bank_per=2)
                highs(s0 + 7, s0 + SD + 3, 3 * SD, j)
                mixer_block(j, True)
            at = s0 + 3 * SD * NJ + 4
            for nb in range(NJ):
                after = JOB[("sc_out", nb)][0] + 4
                highs(at, after + 3)
                at = after + 3
                if nb == 0:
                    for t in range(TT):
                        high_of_scaled(("z", NJ - 1, t), zT_hi, slice(KD - BK, KD), t)
                else:
                    x_highs(3, nb - 1)
                    x_squares(nb - 1)
            at = ffn(1, 3, at, None)
            highs(at, SLOTS)

        @block.vector
        def _(dve):
            steps = [0]

            def link(ins):
                steps[0] += 1
                ins.then_inc(dve_step, 1)
                dve.wait_ge(dve_step, steps[0])

            def lows(s_from, s_to, per=0, rep=0):
                for s in range(s_from + s_from % 2, min(s_to, SLOTS), 2):
                    r = s % RING
                    dve.wait_ge(w_hi_ready, s + 1 + per * rep)
                    nc.vector.tensor_tensor(w_lo[:, r, :, :], w_raw[:, r, :, :],
                                            w_hi[:, r, :, :].bitcast(F32), ALU.subtract).then_inc(w_lo_even, 1)

            def gain(norm, b):
                base = (MIXG if norm % 2 == 0 else FFNG) + (norm // 2) * KD
                return col(base + BK * b, BK).unsqueeze(2).to_broadcast([P, BK, P])

            def x_split(norm, b):
                for t in range(TT):
                    n, bank, _ = GROUP[("x", norm, b, t)]
                    dve.wait_ge(t_ready, n + 1)
                    if LOW[("x", norm, b, t)] >= TT:
                        dve.wait_ge(lo_ready, LOW[("x", norm, b, t)] - TT + 1)
                    nc.vector.tensor_tensor(scaled[:, t, :, :], bank4(bank), gain(norm, b),
                                            ALU.mult).then_inc(t_read[bank], 1)
                for t in range(TT):
                    k = slice(BK * b, BK * (b + 1))
                    dve.wait_ge(hi_ready, HIGH[("x", norm, b, t)] + 1)
                    nc.vector.tensor_tensor(xT_lo[:, k, tok(t)], scaled[:, t, :, :],
                                            xT_hi[:, k, tok(t)].bitcast(F32), ALU.subtract).then_inc(lo_ready, 1)

            def low_of_group(name, hi, lo, k, t, per=0, rep=0, bank_per=0):
                _, b, _ = GROUP[name]
                dve.wait_ge(hi_ready, HIGH[name] + 1 + per * rep)
                nc.vector.tensor_tensor(lo[:, k, tok(t)], bank4(b), hi[:, k, tok(t)].bitcast(F32),
                                        ALU.subtract).then_inc(t_read[b], 1)

            def newton_root(value, r, tmp):
                link(nc.vector.reciprocal(r, r))
                link(nc.vector.tensor_tensor(tmp, r, r, ALU.mult))
                link(nc.vector.scalar_tensor_tensor(tmp, tmp, -0.5, value, ALU.mult, ALU.mult))

            def newton_step(dest, r, tmp):
                return nc.vector.scalar_tensor_tensor(dest, tmp, 1.5, r, ALU.add, ALU.mult)

            def norm_stats(norm):
                dve.wait_ge(sumsq_ready, norm + 1)
                link(nc.vector.reduce_sum(meansq[:, :], sumsq[:, :, :], AX_X))
                nc.vector.tensor_scalar(meansq[:, :], meansq[:, :], 1.0 / D, RMS_EPS, ALU.mult,
                                        ALU.add).then_inc(meansq_ready, 1)
                dve.wait_ge(root_ready, norm + 1)
                newton_root(meansq[:, :], root[:, :], newton[:, :])
                newton_step(rstd[:, :], root[:, :], newton[:, :]).then_inc(rstd_ready, 1)
                dve.wait_ge(rstd_ready, norm + 1)

            def multiply_pair(job, per=0, rep=0, bank_per=0):
                s0, pair, _ = JOB[job]
                dve.wait_ge(w_used, s0 + SD + per * rep)
                for t in range(TT):
                    ins = nc.vector.scalar_tensor_tensor(mixed[:, t, :], pairs[pair][t][:, :], rstd[:, t:t + 1],
                                                         gated[:, t, :], ALU.mult, ALU.mult)
                ins.then_inc(pair_read[pair], 1)

            def add_pair(job, nb, slots):
                s0, pair, _ = JOB[job]
                dve.wait_ge(w_used, s0 + slots)
                for t in range(TT):
                    ins = nc.vector.tensor_tensor(xs[:, t, blk(nb)], pairs[pair][t][:, :], xs[:, t, blk(nb)], ALU.add)
                ins.then_inc(pair_read[pair], 1)

            before = {step: n for n, step in enumerate(dve_taps)}

            def conv_taps(a, b):
                b = min(b, len(dve_taps))
                for n in range(a, b):
                    c, k = dve_taps[n]
                    w = col(DWW + c * TAPS + k)
                    place = acc_place[c]
                    acc = conv_acc[:, place * SEQ:(place + 1) * SEQ]
                    u = uT[:, c, k:k + SEQ]
                    if k == 0:
                        if n >= 2:
                            dve.wait_ge(tap_done, n)
                        nc.vector.tensor_scalar(acc, u, w, col(DWB + c), ALU.mult, ALU.add).then_inc(tap_done, 1)
                    else:
                        dve.wait_ge(tap_done, before[(c, k - 1)] + 1)
                        dest = cv[:, c, :] if k == TAPS - 1 else acc
                        nc.vector.scalar_tensor_tensor(dest, u, w, acc, ALU.mult, ALU.add).then_inc(tap_done, 1)
                return b

            link(nc.vector.memset(uT[:, :, 0:PAD], 0.0))
            nc.vector.memset(junk[:, 0:2], 0.0).then_inc(pad_ready, 1)
            dve.wait_ge(cols_loaded, 16)
            lows(0, 1)
            for b in range(NJ):
                x_split(0, b)
                lows(max(2 * b, 1), 2 * b + 1)
            norm_stats(0)

            def read_by_other(job):
                _, pair, uses = JOB[job]
                dve.wait_ge(pair_read[pair], uses + 1)

            def heads_of(x):
                return x.rearrange("p (h d) -> p h d", d=HD)

            def inverse_roots(n):
                ms, r, tmp = (x[n][:, :, :] for x in (qk_ms, qk_r, qk_t))
                nc.vector.tensor_scalar(ms, ms, 1.0 / HD, RMS_EPS, ALU.mult, ALU.add).then_inc(qk_ms_ready, 1)
                dve.wait_ge(qk_root_ready, n + 1)
                newton_root(ms, r, tmp)
                link(newton_step(r, r, tmp))

            def key_norms():
                read_by_other("kv")
                sq = k_twice[:, :, :, 0, :]
                keys = kv_tok[:, :, 0:KVW].rearrange("p t (h d) -> p t h d", d=HD)
                link(nc.vector.tensor_tensor(sq, keys, keys, ALU.mult))
                link(nc.vector.reduce_sum(qk_ms[0][:, :, :], sq, AX_X))
                link(nc.vector.tensor_scalar(k_gain[:, :], col(KG, HD), HD ** -0.5, None, ALU.mult))
                link(nc.vector.tensor_tensor(k_gain[:, :], k_gain[:, :], col(QG, HD), ALU.mult))
                inverse_roots(0)
                for t in range(TT):
                    ins = nc.vector.tensor_tensor(keys[:, t, :, :], keys[:, t, :, :],
                                                  qk_r[0][:, t, :].unsqueeze(2).to_broadcast([P, HKV, HD]), ALU.mult)
                link(ins)
                for t in range(TT):
                    for w in range(2):
                        ins = nc.vector.tensor_tensor(k_twice[:, t, :, w, :], keys[:, t, :, :],
                                                      k_gain[:, :].unsqueeze(1).to_broadcast([P, HKV, HD]), ALU.mult)
                ins.then_inc(qk_normed, 1)

            def query_norms(g):
                dve.wait_ge(q_sq_ready, g + 1)
                for t in range(TT):
                    ins = nc.vector.reduce_sum(qk_ms[1 + g][:, t, :], heads_of(q_sq[:, t, :]), AX_X)
                link(ins)
                inverse_roots(1 + g)
                for t in range(TT):
                    q3 = heads_of(q_tok[:, t, g * NB:(g + 1) * NB])
                    ins = nc.vector.tensor_tensor(q3, q3, qk_r[1 + g][:, t, :].unsqueeze(2).to_broadcast([P, GQ, HD]),
                                                  ALU.mult)
                ins.then_inc(qk_normed, 1)

            def score_rows(hh):
                g, t = hh // 2, hh % 2
                keys = P if t == 0 else SEQ
                if hh >= 2:
                    dve.wait_ge(t_ready, GROUP[("p", hh - 2, P_GROUPS[hh - 2] - 1)][0] + 1)
                for r in range(4):
                    n, b, _ = GROUP[("sc", hh, r)]
                    dve.wait_ge(t_ready, n + 1)
                    for m in range(2):
                        j = 2 * (2 * (r // 2) + m) + r % 2
                        slope = 2.0 ** (-8.0 * (g * GQ + j + 1) / HQ)
                        ins = nc.vector.scalar_tensor_tensor(scores[t][:, j, 0:keys], dist[t], -slope,
                                                             tbank[b][:, m * SEQ:m * SEQ + keys], ALU.mult, ALU.add)
                    ins.then_inc(t_read[b], 1)
                for r in range(2, 4):
                    _, b, uses = GROUP[("sc", hh, r)]
                    dve.wait_ge(t_read[b], uses + 1)
                sink = col(SINK + g * GQ, GQ)
                link(nc.vector.reduce_max(top[:, t, :], scores[t][:, :, 0:keys], AX_X))
                link(nc.vector.tensor_tensor(top[:, t, :], top[:, t, :], sink, ALU.max))
                link(nc.vector.tensor_scalar(neg_top[:, t, :], top[:, t, :], -1.0, None, ALU.mult))
                nc.vector.tensor_tensor(sink_d[:, t, :], sink, neg_top[:, t, :], ALU.add).then_inc(top_ready, 1)

            def heads_out(hh):
                g, t = hh // 2, hh % 2
                dve.wait_ge(p_ready, hh + 1)
                link(nc.vector.tensor_tensor(rden[:, t, :], den[:, t, :], sink_e[:, t, :], ALU.add))
                link(nc.vector.reciprocal(rden[:, t, :], rden[:, t, :]))
                dve.wait_ge(pv_done, P_BEFORE[hh] + P_GROUPS[hh])
                nc.vector.tensor_tensor(heads_of(q_tok[:, t, g * NB:(g + 1) * NB]), heads_of(heads_acc[:, :]),
                                        rden[:, t, :].unsqueeze(2).to_broadcast([P, GQ, HD]),
                                        ALU.mult).then_inc(o_ready, 1)

            def heads_lows(g):
                for t in range(TT):
                    low_of_group(("o", g, t), mT_hi, mT_lo, slice(KC + 4 * g, KC + 4 * g + 4), t)

            def lows_and_taps(s_from, s_to, taps, each, end):
                for s in range(s_from + s_from % 2, s_to, 2):
                    lows(s, s + 1)
                    taps = conv_taps(taps, min(taps + each, end))
                return taps

            kv0, q00, q10, g10, a10 = (JOB[n][0] for n in ("kv", "q0", "q1", "g1", "a1"))
            ao0 = JOB[("attn_out", 0, 0)][0]
            lows(8, kv0 + 4)
            read_by_other("g0")
            multiply_pair("a0")
            lows(kv0 + 4, kv0 + 8)
            for t in range(TT):
                _, b, uses = GROUP[("u", 0, t)]
                dve.wait_ge(t_read[b], uses + 1)
            EARLY, LATE = EARLY_TAPS, len(dve_taps)
            taps = lows_and_taps(kv0 + 8, q00 + 4, 0, 4, EARLY)
            key_norms()
            taps = lows_and_taps(q00 + 4, q10 + 4, taps, 5, EARLY)
            query_norms(0)
            taps = lows_and_taps(q10 + 4, q10 + 10, taps, 6, EARLY)
            score_rows(0)
            taps = lows_and_taps(q10 + 10, q10 + 12, taps, 3, EARLY)
            score_rows(1)
            query_norms(1)
            taps = lows_and_taps(g10 + 4, g10 + 8, taps, 3, EARLY)
            heads_out(0)
            taps = lows_and_taps(g10 + 8, g10 + 11, taps, 5, EARLY)
            heads_out(1)
            taps = lows_and_taps(g10 + 11, a10 + 4, taps, 3, EARLY)
            score_rows(2)
            lows(a10 + 4, a10 + 5)
            heads_lows(0)
            score_rows(3)
            taps = lows_and_taps(a10 + 5, a10 + 9, taps, 4, EARLY)
            heads_out(2)
            taps = lows_and_taps(a10 + 9, ao0 + 3, taps, 4, EARLY)
            conv_taps(taps, EARLY)
            multiply_pair("a1")
            lows(ao0 + 3, ao0 + 5)
            heads_out(3)
            for t in range(TT):
                _, b, uses = GROUP[("u", 1, t)]
                dve.wait_ge(t_read[b], uses + 1)
            taps = lows_and_taps(ao0 + 5, ao0 + 7, EARLY, 5, LATE)
            heads_lows(1)
            taps = lows_and_taps(ao0 + 7, ao0 + 10, taps, 10, LATE)
            add_pair(("attn_out", 1, 0), 0, 2)
            taps = lows_and_taps(ao0 + 10, ao0 + 12, taps, 10, LATE)
            add_pair(("attn_out", 1, 1), 1, 2)
            taps = lows_and_taps(ao0 + 12, ao0 + 16, taps, 10, LATE)
            add_pair(("attn_out", 1, 2), 2, 2)
            taps = lows_and_taps(ao0 + 16, ao0 + 20, taps, 10, LATE)
            add_pair(("attn_out", 1, 3), 3, 2)
            conv_taps(taps, LATE)

            n, b, _ = GROUP["mean"]
            dve.wait_ge(tap_done, len(dve_taps))
            dve.wait_ge(pool_tap_done, pool_adds(len(pool_taps) - 1))
            dve.wait_ge(t_ready, n + 1)
            for q in range(KC // 2):
                part = cv[:, 2 * q:2 * q + 2, :]
                nc.vector.tensor_tensor(part, part, tbank[b][:, 0:SEQ].unsqueeze(1).to_broadcast([P, 2, SEQ]),
                                        ALU.subtract).then_inc(cv_centered, 1)
            dve.wait_ge(cv_centered, KC // 2)
            nc.vector.memset(junk[:, 0:2], 0.0).then_inc(t_read[b], 1)
            n, b2, _ = GROUP["var"]
            dve.wait_ge(t_ready, n + 1)
            nc.vector.tensor_scalar(ln_v[:, :], tbank[b2][:, 0:SEQ], LN_EPS, None, ALU.add).then_inc(t_read[b2], 1)
            dve.wait_ge(t_read[b2], GROUP["var"][2] + 1)
            nc.vector.memset(junk[:, 2:4], 0.0).then_inc(ln_v_ready, 1)
            dve.wait_ge(ln_root_ready, 1)
            newton_root(ln_v[:, :], ln_r[:, :], ln_t[:, :])
            link(newton_step(ln_r[:, :], ln_r[:, :], ln_t[:, :]))
            for q in range(KC // 2):
                part = cv[:, 2 * q:2 * q + 2, :]
                nc.vector.tensor_tensor(part, part, ln_r[:, :].unsqueeze(1).to_broadcast([P, 2, SEQ]),
                                        ALU.mult).then_inc(ln_scaled, 1)
            for q in range(KC // 2):
                dve.wait_ge(hi_ready, HIGH[("ln", q)] + 1)
                nc.vector.tensor_tensor(mT_lo[:, 2 * q:2 * q + 2, :], cv[:, 2 * q:2 * q + 2, :],
                                        mT_hi[:, 2 * q:2 * q + 2, :].bitcast(F32), ALU.subtract).then_inc(lo_ready, 1)

            s0 = JOB[("conv_out", 0)][0]
            at = s0 + 4
            for nb in range(NJ):
                done = s0 + SH * (nb + 1)
                lows(at, done + 3)
                add_pair(("conv_out", nb), nb, SH)
                at = done + 3
                if nb < NJ - 1:
                    lows(at, done + 5)
                    at = done + 5
                    x_split(1, nb)

            def first_block(s0, at, norm):
                lows(at, s0 + 7)
                x_split(norm, NJ - 1)
                norm_stats(norm)
                return s0 + 7

            def ffn(layer, norm, at, norm_after):
                s0 = JOB[("gate", layer, 0)][0]
                at = first_block(s0, at, norm)
                lows(at, s0 + 2 * SD + 3)
                dve.wait_ge(pair_read[0], JOB[("gate", layer, 0)][2] + 1)
                multiply_pair(("up", layer, 0))
                with dve.Fori(1, NF) as i:
                    lows(s0 + 4, s0 + 7, 2 * SD, i)
                    for t in range(TT):
                        low_of_group(("y", layer, 0, t), yT_hi, yT_lo, ds(BK * (i - 1), BK), t, TT, i - 1)
                    lows(s0 + 8, s0 + 2 * SD + 3, 2 * SD, i)
                    dve.wait_ge(pair_read[0], JOB[("gate", layer, 0)][2] + 1 + i)
                    multiply_pair(("up", layer, 0), 2 * SD, i)
                at = s0 + 2 * SD * NF + 4
                for nb in range(NJ):
                    d0 = JOB[("down", layer, nb)][0]
                    lows(at, d0 + 7)
                    at = d0 + 8
                    if nb == 0:
                        for t in range(TT):
                            low_of_group(("y", layer, NF - 1, t), yT_hi, yT_lo, slice(KF - BK, KF), t)
                    elif norm_after is not None:
                        x_split(norm_after, nb - 1)
                    lows(at, d0 + SF + 3)
                    at = d0 + SF + 3
                    add_pair(("down", layer, nb), nb, SF)
                return at

            at = ffn(0, 1, at, 2)

            s0 = JOB[("cg", 0)][0]
            at = first_block(s0, at, 2)
            nc.vector.memset(cT[:, :, 0:2], 0.0)

            def gate_block(j, rep, k):
                for t in range(TT):
                    n, b, _ = GROUP[("z", j, t)]
                    dve.wait_ge(t_ready, n + 1 + 2 * TT * rep)
                    nc.vector.tensor_tensor(scaled[:, t, :, :], bank4(b), zc[:, :, tok(t)],
                                            ALU.mult).then_inc(t_read[b], 1)
                for t in range(TT):
                    dve.wait_ge(hi_ready, HIGH[("z", j, t)] + 1 + TT * rep)
                    nc.vector.tensor_tensor(zT_lo[:, k, tok(t)], scaled[:, t, :, :],
                                            zT_hi[:, k, tok(t)].bitcast(F32), ALU.subtract).then_inc(lo_ready, 1)

            def mixer_block(rep):
                per = 3 * SD
                dve.wait_ge(pair_read[0], JOB[("cg", 0)][2] + 1 + rep)
                multiply_pair(("cu", 0), per, rep)
                lows(s0 + 2 * SD + 4, s0 + 2 * SD + 7, per, rep)
                for t in range(TT):
                    _, b, uses = GROUP[("c", 0, t)]
                    dve.wait_ge(t_read[b], uses + 1 + 2 * rep)
                for tap in range(3):
                    for k in range(BK):
                        w = cols[:, ds(SCW + k * 3 + tap + 3 * BK * rep, 1)]
                        src = cT[:, k, tap:tap + SEQ]
                        if tap:
                            dve.wait_ge(c3_done, BK * (tap - 1) + k + 1 + 3 * BK * rep)
                            ins = nc.vector.scalar_tensor_tensor(zc[:, k, :], src, w, zc[:, k, :], ALU.mult, ALU.add)
                        else:
                            ins = nc.vector.tensor_scalar(zc[:, k, :], src, w, None, ALU.mult)
                        ins.then_inc(c3_done, 1)
                lows(s0 + 2 * SD + 8, s0 + 3 * SD + 4, per, rep)

            lows(at, s0 + 2 * SD + 3)
            mixer_block(0)
            with dve.Fori(1, NJ) as j:
                lows(s0 + 4, s0 + 7, 3 * SD, j)
                dve.wait_ge(c3_done, 3 * BK * j)
                gate_block(0, j - 1, ds(BK * (j - 1), BK))
                lows(s0 + 8, s0 + 2 * SD + 3, 3 * SD, j)
                mixer_block(j)
            at = s0 + 3 * SD * NJ + 4
            for nb in range(NJ):
                o0 = JOB[("sc_out", nb)][0]
                lows(at, o0 + 7)
                at = o0 + 8
                if nb == 0:
                    dve.wait_ge(c3_done, 3 * BK * NJ)
                    gate_block(NJ - 1, 0, slice(KD - BK, KD))
                else:
                    x_split(3, nb - 1)
                lows(at, o0 + SD + 3)
                at = o0 + SD + 3
                add_pair(("sc_out", nb), nb, SD)
            ffn(1, 3, at, None)


def _columns(np, v):
    def feature_major(a):
        a = np.asarray(a)
        lead, feats = a.shape[:-1], a.shape[-1]
        return a.reshape(-1, feats // 128, 128)

    def plain(a):
        a = feature_major(a)
        return a.transpose(2, 0, 1).reshape(128, -1)

    def taps(a):
        a = feature_major(a)
        return a.transpose(2, 1, 0).reshape(128, -1)

    def shared(a):
        return np.broadcast_to(np.asarray(a).reshape(1, -1), (128, np.asarray(a).size))

    return np.ascontiguousarray(np.concatenate([
        plain(v["mix_norm_g"]), plain(v["ffn_norm_g"]), taps(v["conv_dw_w"][0]), plain(v["conv_dw_b"]),
        plain(v["conv_ln_g"]), plain(v["conv_ln_b"]), taps(v["sc_conv_w"][0]),
        shared(v["q_norm_g"]), shared(v["k_norm_g"]), shared(v["attn_sinks"])], axis=1))


def _tables(np):
    chunk, far = 64, 1e33
    parts = [np.eye(128)]
    for q0, keys in ((0, 128), (128, 256)):
        q, k = np.arange(q0, q0 + 128)[:, None], np.arange(keys)[None, :]
        seen = (k // chunk == q // chunk) | (k // chunk == q // chunk - 1)
        parts.append(np.where(seen, np.abs(q - k), far))
    return np.concatenate(parts, axis=1).astype(np.float32)


def kernel(**inputs):
    import numpy as np
    import concourse.bacc as bacc
    from concourse import mybir as mb
    from concourse.bass_utils import run_bass_kernel_spmd

    v = {name: np.asarray(a) for name, a in inputs.items()}
    arrays = {
        "x": v["x"][0], "w_in": v["hy_w_in"][0], "w_out": v["hy_w_out"][0], "sc_in": v["sc_w_in"][0],
        "sc_out": v["sc_w_out"][0], "w_gate": v["ffn_w_gate"], "w_up": v["ffn_w_up"],
        "w_down": v["ffn_w_down"], "cols": _columns(np, v), "tables": _tables(np),
    }
    arrays = {f"in_{name}": np.ascontiguousarray(a) for name, a in arrays.items()}
    nc = bacc.Bacc("TRN2", target_bir_lowering=False, num_devices=1)
    args = [nc.dram_tensor(name, a.shape, mb.dt.from_np(a.dtype), kind="ExternalInput").ap()
            for name, a in arrays.items()]
    shape = v["x"].shape
    out = nc.dram_tensor("out_y", shape[1:], mb.dt.float32, kind="ExternalOutput").ap()
    encoder_kernel(nc, *args, out)
    result = run_bass_kernel_spmd(nc, [arrays], core_ids=[0])
    return result.results[0]["out_y"].reshape(shape)
```

```python
from contextlib import ExitStack

import concourse.bass as bass
from concourse import mybir

F32 = mybir.dt.float32
F32R = mybir.dt.float32r
ALU = mybir.AluOpType
ACT = mybir.ActivationFunctionType
AX_X = mybir.AxisListType.X

P = 128
NB = 512
RING = 4
SLOT_K = 2
HB = NB // 2
HALF_K = 2 * SLOT_K
PRODUCTS = 8
RMS_EPS = 1e-6
LN_EPS = 1e-5


def ds(start, size):
    return bass.ds(start, size)


class Plan:

    def __init__(self):
        self.slots = 0
        self.pair_uses = [0, 0, 0]
        self.jobs = {}
        self.groups = {}
        self.bank_uses = [0, 0]
        self.highs = {}
        self.lows = {}

    def job(self, name, pair, k_tiles, adds=False, slot_k=SLOT_K):
        if adds:
            self.pair_uses[pair] -= 1
        self.jobs[name] = (self.slots, pair, self.pair_uses[pair])
        self.slots += k_tiles // slot_k
        self.pair_uses[pair] += 1

    def group(self, name, high=False, low=False):
        n = len(self.groups)
        self.groups[name] = (n, n % 2, self.bank_uses[n % 2])
        self.bank_uses[n % 2] += 1
        if high:
            self.split(name, low)

    def split(self, name, low=True):
        self.highs[name] = len(self.highs)
        if low:
            self.lows[name] = len(self.lows)


def encoder_kernel(nc, x_in, w_in, w_out, sc_in, sc_out, w_gate, w_up, w_down, cols_in, tables_in, out):
    SEQ, D = x_in.shape
    FF = w_gate.shape[2]
    DEPTH = w_gate.shape[0]
    TT = SEQ // P
    KD = D // P
    KF = FF // P
    NJ = D // NB
    NF = FF // NB
    BK = NB // P
    HD, HQ, HKV = 64, 16, 2
    GQ = HQ // HKV
    AW = HQ * HD
    CC = D - AW
    KC = CC // P
    TAPS = 31
    PAD = TAPS - 1
    KVW = HKV * HD
    assert TT == 2 and DEPTH == 2 and KVW == P and 2 * KVW == HB and CC == 2 * NB and AW == 2 * NB
    SD = KD // SLOT_K
    SN = KD // HALF_K
    SF = KF // SLOT_K
    SH = SD // 2

    MIXG, FFNG = 0, DEPTH * KD
    DWW = FFNG + DEPTH * KD
    DWB = DWW + KC * TAPS
    LNG = DWB + KC
    LNB = LNG + KC
    SCW = LNB + KC
    QG = SCW + 3 * KD
    KG = QG + HD
    SINK = KG + HD
    NCOLS = SINK + HQ

    plan = Plan()
    for b in range(NJ):
        for t in range(TT):
            plan.group(("x", 0, b, t), high=True, low=True)
    plan.job("g0", 1, KD)
    plan.job("a0", 0, KD)
    plan.job("kv", 1, KD, slot_k=HALF_K)
    plan.group(("u", 0, 0)), plan.group(("u", 0, 1))
    plan.job("q0", 0, KD)
    plan.group("kT")
    plan.job("q1", 1, KD)
    for h in range(2):
        plan.job(("g1", h), 0, KD, slot_k=HALF_K)
        plan.job(("a1", h), 1, KD, slot_k=HALF_K)
    OUT_ORDER = ((0, 0), (0, 1), (1, 0), (1, 1), (0, 2), (1, 2), (0, 3), (1, 3))
    for g, nb in OUT_ORDER:
        plan.job(("attn_out", g, nb), nb % 2, KC // 2, adds=(g == 1))
    P_GROUPS = (2, 4, 2, 4)
    P_BEFORE = (0, 2, 6, 8)
    def plan_queries(g):
        for t in range(TT):
            plan.group(("qT", g, t))

    def plan_scores(hh):
        for r in range(4):
            plan.group(("sc", hh, r))

    def plan_probs(hh):
        for r in range(P_GROUPS[hh]):
            plan.group(("p", hh, r))

    def plan_heads(g):
        for t in range(TT):
            plan.group(("o", g, t), high=True)

    plan_queries(0), plan_scores(0), plan_scores(1), plan_probs(0), plan_probs(1)
    plan_queries(1), plan_scores(2), plan_heads(0)
    plan.group(("u1", 0))
    plan_scores(3), plan_probs(2), plan_probs(3)
    plan.group(("u1", 1))
    plan_heads(1)
    plan.group("mean")
    plan.group("var")
    for q in range(KC // 2):
        plan.split(("ln", q))
    for nb in range(NJ):
        plan.job(("conv_out", nb), nb % 2, KD // 2)
    for b in range(NJ):
        for t in range(TT):
            plan.group(("x", 1, b, t), high=True, low=True)

    def plan_ffn(layer, norm_after):
        for i in range(NF):
            plan.job(("gate", layer, i), 0, KD)
            plan.job(("up", layer, i), 1, KD)
            for t in range(TT):
                plan.group(("y", layer, i, t), high=True)
        for nb in range(NJ):
            plan.job(("down", layer, nb), nb % 2, KF)
        if norm_after is not None:
            for b in range(NJ):
                for t in range(TT):
                    plan.group(("x", norm_after, b, t), high=True, low=True)

    plan_ffn(0, 2)
    for j in range(NJ):
        plan.job(("cg", j), 0, KD)
        plan.job(("cu", j), 1, KD)
        plan.job(("bg", j), 2, KD)
        for t in range(TT):
            plan.group(("c", j, t))
        for t in range(TT):
            plan.group(("z", j, t), high=True, low=True)
    for nb in range(NJ):
        plan.job(("sc_out", nb), nb % 2, KD)
    for b in range(NJ):
        for t in range(TT):
            plan.group(("x", 3, b, t), high=True, low=True)
    plan_ffn(1, None)
    JOB, GROUP, HIGH, LOW, SLOTS = plan.jobs, plan.groups, plan.highs, plan.lows, plan.slots
    assert SLOTS % RING == 0
    assert all(JOB[("gate", la, 0)][0] % RING == 0 for la in range(DEPTH)) and JOB[("cg", 0)][0] % RING == 0

    with ExitStack() as ctx:
        def sb(name, shape, dt=F32, stack=ctx):
            return stack.enter_context(nc.sbuf_tensor(name, shape, dt))

        def sem(name):
            return ctx.enter_context(nc.semaphore(name))

        xs = sb("xs", [P, TT, D])
        xT_hi = sb("xT_hi", [P, KD, SEQ], F32R)
        xT_lo = sb("xT_lo", [P, KD, SEQ], F32R)
        w_raw = sb("w_raw", [P, RING, SLOT_K, NB])
        w_hi = sb("w_hi", [P, RING, SLOT_K, NB], F32R)
        w_lo = sb("w_lo", [P, RING, SLOT_K, NB], F32R)
        cols = sb("cols", [P, NCOLS])
        tables = sb("tables", [P, P + P + SEQ])
        ident = tables[:, 0:P]
        dist = [tables[:, P:2 * P], tables[:, 2 * P:2 * P + SEQ]]
        mixed = sb("mixed", [P, TT, NB])
        gated = sb("gated", [P, TT, NB])
        scaled = sb("scaled", [P, TT, BK, P])
        junk = sb("junk", [P, NB])
        sumsq = sb("sumsq", [P, TT, NJ])
        meansq = sb("meansq", [P, TT])
        root = sb("root", [P, TT])
        newton = sb("newton", [P, TT])
        rstd = sb("rstd", [P, TT])
        idle = sb("idle", [P, TT])

        with ExitStack() as early:
            mT_hi = sb("mT_hi", [P, KD, SEQ], F32R, early)
            mT_lo = sb("mT_lo", [P, KD, SEQ], F32R, early)
            uT = sb("uT", [P, KC, PAD + SEQ], F32, early)
            cv = sb("cv", [P, KC, SEQ], F32, early)
            products = sb("products", [P, PRODUCTS, SEQ], F32, early)
            qT = sb("qT", [P, GQ, SEQ], F32, early)
            kT = sb("kT", [P, HKV, SEQ], F32, early)
            kv_tok = sb("kv_tok", [P, TT, 2 * KVW], F32, early)
            k_twice = sb("k_twice", [P, TT, HKV, 2, HD], F32, early)
            q_tok = sb("q_tok", [P, TT, AW], F32, early)
            scores = [sb("scores0", [P, GQ, P], F32, early), sb("scores1", [P, GQ, SEQ], F32, early)]
            ln_v = sb("ln_v", [P, SEQ], F32, early)
            ones = sb("ones", [P, P], F32, early)
            k_gain = sb("k_gain", [P, HD], F32, early)
            qk_ms = [sb(f"qk_ms{n}", [P, TT, HKV if n == 0 else GQ], F32, early) for n in range(3)]
            qk_r = [sb(f"qk_r{n}", [P, TT, HKV if n == 0 else GQ], F32, early) for n in range(3)]
            qk_t = [sb(f"qk_t{n}", [P, TT, HKV if n == 0 else GQ], F32, early) for n in range(3)]
            top = sb("top", [P, TT, GQ], F32, early)
            neg_top = sb("neg_top", [P, TT, GQ], F32, early)
            sink_d = sb("sink_d", [P, TT, GQ], F32, early)
            sink_e = sb("sink_e", [P, TT, GQ], F32, early)
            den = sb("den", [P, TT, GQ], F32, early)
            rden = sb("rden", [P, TT, GQ], F32, early)
        with ExitStack() as late:
            yT_hi = sb("yT_hi", [P, KF, SEQ], F32R, late)
            yT_lo = sb("yT_lo", [P, KF, SEQ], F32R, late)
        with ExitStack() as late:
            zT_hi = sb("zT_hi", [P, KD, SEQ], F32R, late)
            zT_lo = sb("zT_lo", [P, KD, SEQ], F32R, late)
            bg_tok = sb("bg_tok", [P, TT, NB], F32, late)
            cT = sb("cT", [P, BK, 2 + SEQ], F32, late)
            zc = sb("zc", [P, BK, SEQ], F32, late)
        ln_sq = q_tok[:, :, :].rearrange("p t (c k) -> p (t c) k", k=SEQ)
        probs = scaled[:, :, :, :].rearrange("p t k n -> p t (k n)")
        q_sq = mixed[:, :, :]
        ln_r, ln_t = junk[:, 0:SEQ], junk[:, SEQ:2 * SEQ]
        LATE_JOBS = [(name, h) for h in range(2) for name in ("g1", "a1")]

        SHARE = 24
        pool_taps = [(c, k) for k in range(TAPS) for c in (0, 1)] + [(4, k) for k in range(SHARE)]
        pool_taps += [(c, k) for k in range(SHARE, TAPS) for c in (4, KC - 1)]
        dve_taps = [(c, k) for k in range(TAPS) for c in (2, 3)]
        U0_TAPS = len(dve_taps)
        dve_taps += [(5, k) for k in range(TAPS)]
        U1_TAPS = len(dve_taps)
        dve_taps += [(c, k) for k in range(SHARE) for c in (6, 7)] + [(6, k) for k in range(SHARE, TAPS)]
        dve_taps += [(KC - 1, TAPS)]
        ALL_TAPS = len(dve_taps)
        acc_place = {2: 0, 3: 1, 5: 0, 6: 1, 7: 0}
        FIRST_TAP, SECOND_TAPS = JOB["kv"][0] + 5, JOB[("g1", 0)][0] + 13

        def products_by(s):
            first = max(0, min(2 * (s - FIRST_TAP + 1), 2 * TAPS))
            return first + max(0, min(2 * (s - SECOND_TAPS + 1), len(pool_taps) - 2 * TAPS))

        def starts_sum(c, k):
            return k == (SHARE if c == KC - 1 else 0)

        def pool_adds(n):
            return sum(not starts_sum(*step) for step in pool_taps[:n + 1])

        pairs = [[ctx.enter_context(nc.psum_tensor(f"pair{p}_{t}", [P, NB], F32)) for t in range(TT)]
                 for p in range(3)]
        tbank = [ctx.enter_context(nc.psum_tensor(f"tbank{b}", [P, NB], F32)) for b in range(2)]
        conv_acc = pairs[2][0]
        heads_acc = pairs[2][1]

        x_loaded = [sem(f"x_loaded{b}") for b in range(NJ)]
        cols_loaded = sem("cols_loaded")
        tables_loaded = sem("tables_loaded")
        w_loaded = [sem(f"w_loaded{r}") for r in range(RING)]
        w_hi_ready = sem("w_hi_ready")
        w_lo_even = sem("w_lo_even")
        w_lo_odd = sem("w_lo_odd")
        w_used = sem("w_used")
        pair_read = [sem(f"pair_read{p}") for p in range(3)]
        t_ready = sem("t_ready")
        t_read = [sem(f"t_read{b}") for b in range(2)]
        hi_ready = sem("hi_ready")
        lo_ready = sem("lo_ready")
        sumsq_ready = sem("sumsq_ready")
        meansq_ready = sem("meansq_ready")
        root_ready = sem("root_ready")
        rstd_ready = sem("rstd_ready")
        pad_ready = sem("pad_ready")
        ones_ready = sem("ones_ready")
        q_sq_ready = sem("q_sq_ready")
        qk_ms_ready = sem("qk_ms_ready")
        qk_root_ready = sem("qk_root_ready")
        qk_normed = sem("qk_normed")
        top_ready = sem("top_ready")
        p_ready = sem("p_ready")
        pv_done = sem("pv_done")
        o_ready = sem("o_ready")
        tap_done = sem("tap_done")
        product_ready = sem("product_ready")
        pool_tap_done = sem("pool_tap_done")
        cv_centered = sem("cv_centered")
        ln_sq_ready = sem("ln_sq_ready")
        ln_v_ready = sem("ln_v_ready")
        ln_root_ready = sem("ln_root_ready")
        ln_scaled = sem("ln_scaled")
        silu_done = sem("silu_done")
        c3_done = sem("c3_done")
        dve_step = sem("dve_step")
        act_step = sem("act_step")
        stored = sem("stored")

        def col(c, n=1):
            return cols[:, c:c + n]

        def tok(t):
            return slice(t * P, (t + 1) * P)

        def blk(b):
            return slice(b * NB, (b + 1) * NB)

        def bank4(b):
            return tbank[b][:, :].rearrange("p (k n) -> p k n", n=P)

        block = ctx.enter_context(nc.Block())

        @block.sync
        def _(sp):
            def place_free(s, per=0, rep=0):
                if s >= RING:
                    sp.wait_ge(w_lo_odd if s % 2 else w_lo_even, (s - RING) // 2 + 1 + (per // 2) * rep)

            def load_slot(s, source):
                r = s % RING
                sp.dma_start(w_raw[:, r, :, :], source).then_inc(w_loaded[r], 16)

            def load_narrow(s0, w, start):
                view = w.rearrange("(k p) n -> p k n", p=P)[:, :, ds(start, HB)]
                for q in range(SN):
                    place_free(s0 + q)
                    r = (s0 + q) % RING
                    sp.dma_start(w_raw[:, r, :, :].rearrange("p k (h n) -> p (k h) n", n=HB),
                                 view[:, HALF_K * q:HALF_K * (q + 1), :]).then_inc(w_loaded[r], 16)

            def load_job(s0, w, k0, slots, start, per=0, rep=0, swap=False):
                view = w.rearrange("(k p) n -> p k n", p=P)[:, :, ds(start, NB)]
                for q in ([1, 0] if swap else [0, 1]) + list(range(2, slots)):
                    k = k0 + SLOT_K * q
                    if swap and q == 1:
                        place_free(s0, per, rep)
                    if not (swap and q == 0):
                        place_free(s0 + q, per, rep)
                    load_slot(s0 + q, view[:, k:k + SLOT_K, :])

            first = w_in.rearrange("(k p) n -> p k n", p=P)
            for b in range(NJ):
                sp.dma_start(xs[:, :, blk(b)],
                             x_in.rearrange("(t p) n -> p t n", p=P)[:, :, blk(b)]).then_inc(x_loaded[b], 16)
                load_slot(b, first[:, SLOT_K * b:SLOT_K * (b + 1), ds(CC, NB)])
            load_job(JOB["g0"][0] + NJ, w_in, SLOT_K * NJ, SD - NJ, CC)
            load_job(JOB["a0"][0], w_in, 0, SD, 0)
            load_narrow(JOB["kv"][0], w_in, 2 * CC + AW)
            load_job(JOB["q0"][0], w_in, 0, SD, 2 * CC)
            load_job(JOB["q1"][0], w_in, 0, SD, 2 * CC + NB)
            for h in range(2):
                load_narrow(JOB[("g1", h)][0], w_in, CC + NB + h * HB)
                load_narrow(JOB[("a1", h)][0], w_in, NB + h * HB)
            for g, nb in OUT_ORDER:
                load_job(JOB[("attn_out", g, nb)][0], w_out, KC + KC // 2 * g, SH // 2, nb * NB)
            for nb in range(NJ):
                load_job(JOB[("conv_out", nb)][0], w_out, 0, SH, nb * NB)

            def ffn(layer):
                s0 = JOB[("gate", layer, 0)][0]
                with sp.Fori(1, NF + 1) as n:
                    i = n - 1
                    load_job(s0, w_gate[layer], 0, SD, i * NB, 2 * SD, i)
                    load_job(s0 + SD, w_up[layer], 0, SD, i * NB, 2 * SD, i)
                for nb in range(NJ):
                    load_job(JOB[("down", layer, nb)][0], w_down[layer], 0, SF, nb * NB)

            ffn(0)
            s0 = JOB[("cg", 0)][0]
            with sp.Fori(1, NJ + 1) as n:
                j = n - 1
                load_job(s0, sc_in, 0, SD, j * NB + D, 3 * SD, j)
                load_job(s0 + SD, sc_in, 0, SD, j * NB + 2 * D, 3 * SD, j)
                load_job(s0 + 2 * SD, sc_in, 0, SD, j * NB, 3 * SD, j, swap=True)
            for nb in range(NJ):
                load_job(JOB[("sc_out", nb)][0], sc_out, 0, SD, nb * NB)
            ffn(1)
            for nb in range(NJ):
                _, pair, uses = JOB[("down", 1, nb)]
                sp.wait_ge(pair_read[pair], uses + 1)
                sp.dma_start(out.rearrange("(t p) n -> p t n", p=P)[:, :, blk(nb)],
                             xs[:, :, blk(nb)]).then_inc(stored, 16)
            sp.wait_ge(stored, 16 * NJ)

        @block.gpsimd
        def _(pool):
            nc.gpsimd.memset(ones[:, :], 1.0 / CC).then_inc(ones_ready, 1)

            def low(s, place):
                pool.wait_ge(w_hi_ready, s + 1)
                nc.gpsimd.tensor_tensor(w_lo[:, place, :, :], w_raw[:, place, :, :],
                                        w_hi[:, place, :, :].bitcast(F32), ALU.subtract).then_inc(w_lo_odd, 1)

            def add_taps(a, b):
                for n in range(a, min(b, len(pool_taps))):
                    c, k = pool_taps[n]
                    if starts_sum(c, k):
                        continue
                    pool.wait_ge(product_ready, n + 1)
                    if not starts_sum(c, k - 1):
                        pool.wait_ge(pool_tap_done, pool_adds(pool_taps.index((c, k - 1))))
                    nc.gpsimd.tensor_tensor(cv[:, c, :], products[:, n % PRODUCTS, :], cv[:, c, :],
                                            ALU.add).then_inc(pool_tap_done, 1)

            first_ffn = JOB[("gate", 0, 0)][0]
            for s in range(1, first_ffn, 2):
                low(s, s % RING)
                add_taps(products_by(s - 2), products_by(s))

            with pool.Fori(first_ffn // RING, SLOTS // RING) as i:
                for r in range(1, RING, 2):
                    low(RING * i + r, r)

        @block.tensor
        def _(pe):
            def slots(job, q0, q1, hi, lo, k0=0, per=0, rep=0, pair_per=0, last=None, adds=False):
                s0, pair, uses = JOB[job]
                last = q1 if last is None else last
                if q0 == 0 and not adds and (uses or pair_per):
                    pe.wait_ge(pair_read[pair], uses + pair_per * rep)
                for q in range(q0, q1):
                    s = s0 + q
                    r = s % RING
                    pe.wait_ge(w_lo_odd if s % 2 else w_lo_even, s // 2 + 1 + (per // 2) * rep)
                    for kk in range(SLOT_K):
                        k = k0 + SLOT_K * q + kk
                        first, end = (q == 0 and kk == 0 and not adds), (q == last - 1 and kk == SLOT_K - 1)
                        for t in range(TT):
                            o = pairs[pair][t][:, :]
                            nc.tensor.matmul(o, hi[:, k, tok(t)], w_hi[:, r, kk, :], start=first, stop=False)
                            nc.tensor.matmul(o, hi[:, k, tok(t)], w_lo[:, r, kk, :], start=False, stop=False)
                            mm = nc.tensor.matmul(o, lo[:, k, tok(t)], w_hi[:, r, kk, :], start=False, stop=end)
                    mm.then_inc(w_used, 1)

            def narrow(job, q0, q1):
                s0, pair, uses = JOB[job]
                if q0 == 0:
                    pe.wait_ge(pair_read[pair], uses)
                for q in range(q0, q1):
                    s = s0 + q
                    r = s % RING
                    pe.wait_ge(w_lo_odd if s % 2 else w_lo_even, s // 2 + 1)
                    for kk in range(HALF_K):
                        k = HALF_K * q + kk
                        at, c = kk // 2, slice(kk % 2 * HB, (kk % 2 + 1) * HB)
                        for t in range(TT):
                            o = pairs[pair][t][:, 0:HB]
                            nc.tensor.matmul(o, xT_hi[:, k, tok(t)], w_hi[:, r, at, c], start=(k == 0), stop=False)
                            nc.tensor.matmul(o, xT_hi[:, k, tok(t)], w_lo[:, r, at, c], start=False, stop=False)
                            mm = nc.tensor.matmul(o, xT_lo[:, k, tok(t)], w_hi[:, r, at, c], start=False,
                                                  stop=(k == KD - 1))
                    mm.then_inc(w_used, 1)

            def bank_free(group, per=0, rep=0):
                _, b, uses = GROUP[group]
                if uses:
                    pe.wait_ge(t_read[b], uses + per * rep)
                return b

            def transposes(group, sources, per=0, rep=0):
                b = bank_free(group, per, rep)
                for n, source in enumerate(sources):
                    mm = nc.tensor.transpose(tbank[b][:, n * P:(n + 1) * P], source, ident)
                mm.then_inc(t_ready, 1)

            def x_transposes(norm, b):
                for t in range(TT):
                    transposes(("x", norm, b, t),
                               [xs[:, t, b * NB + k * P:b * NB + (k + 1) * P] for k in range(BK)])

            def x_split(norm, b):
                pe.wait_ge(lo_ready, LOW[("x", norm, b, TT - 1)] + 1)

            def read_out(job, per=0, rep=0):
                _, pair, uses = JOB[job]
                pe.wait_ge(pair_read[pair], uses + 1 + per * rep)

            def block_transposes(name, source, per=0, rep=0):
                for t in range(TT):
                    transposes(name + (t,), [source[:, t, k * P:(k + 1) * P] for k in range(BK)], per, rep)

            def x_arrived(b):
                pe.wait_ge(x_loaded[b], 16)
                x_transposes(0, b)

            pe.wait_ge(tables_loaded, 16)
            x_arrived(0)
            x_arrived(1)

            def keys_of(t):
                return P if t == 0 else SEQ

            def query_transposes(g):
                pe.wait_ge(qk_normed, 2 + g)
                for t in range(TT):
                    transposes(("qT", g, t), [q_tok[:, t, (4 * g + j) * P:(4 * g + j + 1) * P] for j in range(4)])

            def score_products(hh, r0, r1):
                g, t = hh // 2, hh % 2
                _, b, uses = GROUP[("qT", g, t)]
                pe.wait_ge(t_read[b], uses + 1)
                for r in range(r0, r1):
                    b = bank_free(("sc", hh, r))
                    e = r % 2
                    for m in range(2):
                        mm = nc.tensor.matmul(tbank[b][:, m * SEQ:m * SEQ + keys_of(t)],
                                              qT[e * HD:(e + 1) * HD, 4 * g + 2 * (r // 2) + m, tok(t)],
                                              kT[e * HD:(e + 1) * HD, g, 0:keys_of(t)], start=True, stop=True)
                    mm.then_inc(t_ready, 1)

            def prob_transposes(hh, r0, r1):
                kb = 1 + hh % 2
                per = 4 // kb
                if r0 == 0:
                    pe.wait_ge(p_ready, hh + 1)
                for r in range(r0, r1):
                    transposes(("p", hh, r), [scores[hh % 2][:, per * r + m, c * P:(c + 1) * P]
                                              for m in range(per) for c in range(kb)])

            def value_products(hh, r0, r1):
                kb = 1 + hh % 2
                per = 4 // kb
                g = hh // 2
                if r0 == 0 and hh:
                    pe.wait_ge(o_ready, hh)
                for r in range(r0, r1):
                    _, b, uses = GROUP[("p", hh, r)]
                    pe.wait_ge(t_read[b], uses + 1)
                    for m in range(per):
                        j = per * r + m
                        for c in range(kb):
                            at = (m * kb + c) * P
                            mm = nc.tensor.matmul(heads_acc[:, j * HD:(j + 1) * HD],
                                                  probs[:, (P_BEFORE[hh] + r) % 2, at:at + P],
                                                  kv_tok[:, c, KVW + g * HD:KVW + (g + 1) * HD],
                                                  start=(c == 0), stop=(c == kb - 1))
                    mm.then_inc(pv_done, 1)

            def heads_transposes(g):
                for t in range(TT):
                    pe.wait_ge(o_ready, 2 * g + t + 1)
                    transposes(("o", g, t), [q_tok[:, t, (4 * g + k) * P:(4 * g + k + 1) * P] for k in range(4)])

            for b in range(NJ):
                x_split(0, b)
                slots("g0", 2 * b, 2 * b + 2, xT_hi, xT_lo, last=SD)
                if b + 2 < NJ:
                    x_arrived(b + 2)
            slots("a0", 0, SD, xT_hi, xT_lo)
            narrow("kv", 0, 2)
            read_out("a0")
            block_transposes(("u", 0), mixed)
            narrow("kv", 2, SN)
            slots("q0", 0, 6, xT_hi, xT_lo, last=SD)
            pe.wait_ge(qk_normed, 1)
            transposes("kT", [k_twice[:, t, g, :, :].rearrange("p w d -> p (w d)")
                              for g in range(HKV) for t in range(TT)])
            slots("q0", 6, SD, xT_hi, xT_lo)
            slots("q1", 0, 5, xT_hi, xT_lo, last=SD)
            query_transposes(0)
            slots("q1", 5, 6, xT_hi, xT_lo, last=SD)
            score_products(0, 0, 2)
            slots("q1", 6, 7, xT_hi, xT_lo, last=SD)
            score_products(0, 2, 4)
            slots("q1", 7, SD, xT_hi, xT_lo)
            score_products(1, 0, 2)
            def late(q0, q1):
                for q in range(q0, q1):
                    narrow(LATE_JOBS[q // SN], q % SN, q % SN + 1)

            def u1_transposes(h):
                read_out(("a1", h))
                transposes(("u1", h), [mixed[:, t, h * HB + k * P:h * HB + (k + 1) * P]
                                       for k in range(BK // 2) for t in range(TT)])

            late(0, 1)
            score_products(1, 2, 4)
            late(1, 3)
            prob_transposes(0, 0, 2)
            late(3, 4)
            value_products(0, 0, 2)
            late(4, 5)
            prob_transposes(1, 0, 2)
            late(5, 6)
            value_products(1, 0, 2)
            prob_transposes(1, 2, 4)
            late(6, 7)
            value_products(1, 2, 4)
            query_transposes(1)
            late(7, 8)
            score_products(2, 0, 2)
            late(8, 9)
            score_products(2, 2, 4)
            heads_transposes(0)
            late(9, 10)
            u1_transposes(0)
            score_products(3, 0, 2)
            late(10, 11)
            score_products(3, 2, 4)
            late(11, 13)
            prob_transposes(2, 0, 2)
            late(13, 14)
            value_products(2, 0, 2)
            late(14, 15)
            prob_transposes(3, 0, 2)
            late(15, 16)

            def attn_out(n, q0, q1):
                g, nb = OUT_ORDER[n]
                slots(("attn_out", g, nb), q0, q1, mT_hi, mT_lo, k0=KC + KC // 2 * g, last=2 if g else SD,
                      adds=(g == 1))

            def heads_split(g):
                for t in range(TT):
                    _, b, uses = GROUP[("o", g, t)]
                    pe.wait_ge(t_read[b], uses + 1)

            heads_split(0)
            value_products(3, 0, 2)
            prob_transposes(3, 2, 4)
            attn_out(0, 0, 1)
            u1_transposes(1)
            value_products(3, 2, 4)
            attn_out(0, 1, 2)
            attn_out(1, 0, 1)
            heads_transposes(1)
            attn_out(1, 1, 2)
            heads_split(1)
            def channel_means():
                pe.wait_ge(ones_ready, 1)
                b = bank_free("mean")
                for c in range(KC):
                    last = (c, TAPS if c == KC - 1 else TAPS - 1)
                    if last in dve_taps:
                        pe.wait_ge(tap_done, dve_taps.index(last) + 1)
                    else:
                        pe.wait_ge(pool_tap_done, pool_adds(pool_taps.index((c, TAPS - 1))))
                    mm = nc.tensor.matmul(tbank[b][:, 0:SEQ], ones[:, :], cv[:, c, :], start=(c == 0), stop=(c == KC - 1))
                mm.then_inc(t_ready, 1)

            def channel_variances():
                b = bank_free("var")
                for c in range(KC):
                    if c % 2 == 0:
                        pe.wait_ge(ln_sq_ready, c // 2 + 1)
                    mm = nc.tensor.matmul(tbank[b][:, 0:SEQ], ones[:, :], ln_sq[:, c, :], start=(c == 0), stop=(c == KC - 1))
                mm.then_inc(t_ready, 1)

            for n in range(2, 7):
                attn_out(n, 0, 2)
            channel_means()
            attn_out(7, 0, 1)
            channel_variances()
            attn_out(7, 1, 2)

            for nb in range(NJ):
                job = ("conv_out", nb)
                if nb == 0:
                    for q in range(SH):
                        pe.wait_ge(lo_ready, LOW[("ln", q)] + 1)
                        slots(job, q, q + 1, mT_hi, mT_lo, last=SH)
                else:
                    slots(job, 0, 2, mT_hi, mT_lo, last=SH)
                    read_out(("conv_out", nb - 1))
                    x_transposes(1, nb - 1)
                    slots(job, 2, SH, mT_hi, mT_lo)

            def first_block(job, norm, last_out, last=SD):
                for b in range(2):
                    x_split(norm, b)
                    slots(job, 2 * b, 2 * b + 2, xT_hi, xT_lo, last=last)
                read_out(last_out)
                x_transposes(norm, NJ - 1)
                x_split(norm, 2)
                slots(job, 4, 6, xT_hi, xT_lo, last=last)
                x_split(norm, 3)
                slots(job, 6, SD, xT_hi, xT_lo)

            def ffn(layer, norm, last_out, norm_after):
                first_block(("gate", layer, 0), norm, last_out)
                slots(("up", layer, 0), 0, SD, xT_hi, xT_lo)
                with pe.Fori(1, NF) as i:
                    args = dict(per=2 * SD, rep=i, pair_per=1)
                    slots(("gate", layer, 0), 0, 4, xT_hi, xT_lo, last=SD, **args)
                    read_out(("up", layer, 0), 1, i - 1)
                    block_transposes(("y", layer, 0), mixed, 1, i - 1)
                    slots(("gate", layer, 0), 4, SD, xT_hi, xT_lo, **args)
                    slots(("up", layer, 0), 0, SD, xT_hi, xT_lo, **args)
                for nb in range(NJ):
                    job = ("down", layer, nb)
                    slots(job, 0, 4, yT_hi, yT_lo, last=SF)
                    if nb == 0:
                        read_out(("up", layer, NF - 1))
                        block_transposes(("y", layer, NF - 1), mixed)
                    elif norm_after is not None:
                        read_out(("down", layer, nb - 1))
                        x_transposes(norm_after, nb - 1)
                    slots(job, 4, SF - 2, yT_hi, yT_lo, last=SF)
                    if nb == 0:
                        for t in range(TT):
                            _, b, uses = GROUP[("y", layer, NF - 1, t)]
                            pe.wait_ge(t_read[b], uses + 1)
                    slots(job, SF - 2, SF, yT_hi, yT_lo)

            ffn(0, 1, ("conv_out", NJ - 1), 2)

            first_block(("cg", 0), 2, ("down", 0, NJ - 1))
            slots(("cu", 0), 0, SD, xT_hi, xT_lo)
            slots(("bg", 0), 0, 4, xT_hi, xT_lo, last=SD)
            read_out(("cu", 0))
            block_transposes(("c", 0), mixed)
            slots(("bg", 0), 4, SD, xT_hi, xT_lo)
            with pe.Fori(1, NJ) as j:
                args = dict(per=3 * SD, rep=j, pair_per=1)
                slots(("cg", 0), 0, 4, xT_hi, xT_lo, last=SD, **args)
                read_out(("bg", 0), 1, j - 1)
                block_transposes(("z", 0), bg_tok, 2, j - 1)
                slots(("cg", 0), 4, SD, xT_hi, xT_lo, **args)
                slots(("cu", 0), 0, SD, xT_hi, xT_lo, **args)
                slots(("bg", 0), 0, 4, xT_hi, xT_lo, last=SD, **args)
                read_out(("cu", 0), 1, j)
                block_transposes(("c", 0), mixed, 2, j)
                slots(("bg", 0), 4, SD, xT_hi, xT_lo, **args)
            for nb in range(NJ):
                job = ("sc_out", nb)
                if nb == 0:
                    pe.wait_ge(lo_ready, LOW[("z", NJ - 2, TT - 1)] + 1)
                slots(job, 0, 4, zT_hi, zT_lo, last=SD)
                if nb == 0:
                    read_out(("bg", NJ - 1))
                    block_transposes(("z", NJ - 1), bg_tok)
                    slots(job, 4, 6, zT_hi, zT_lo, last=SD)
                    pe.wait_ge(lo_ready, LOW[("z", NJ - 1, TT - 1)] + 1)
                    slots(job, 6, SD, zT_hi, zT_lo)
                else:
                    read_out(("sc_out", nb - 1))
                    x_transposes(3, nb - 1)
                    slots(job, 4, SD, zT_hi, zT_lo)

            ffn(1, 3, ("sc_out", NJ - 1), None)

        @block.scalar
        def _(act):
            steps = [0]

            def link(ins):
                steps[0] += 1
                ins.then_inc(act_step, 1)
                act.wait_ge(act_step, steps[0])

            def highs(s_from, s_to, per=0, rep=0):
                for s in range(s_from, min(s_to, SLOTS)):
                    r = s % RING
                    act.wait_ge(w_loaded[r], 16 * (s // RING + 1) + (16 * per // RING) * rep)
                    if s >= RING:
                        act.wait_ge(w_used, s - RING + 1 + per * rep)
                    nc.scalar.activation(w_hi[:, r, :, :], w_raw[:, r, :, :], ACT.Copy).then_inc(w_hi_ready, 1)

            def job_done(job, per=0, rep=0, slots=SD):
                s0, pair, _ = JOB[job]
                act.wait_ge(w_used, s0 + slots + per * rep)
                return pair

            def high_of_scaled(name, dest, k, t, per=0, rep=0, bank_per=0, scaled_t=None):
                _, b, uses = GROUP[name]
                act.wait_ge(t_read[b], uses + 1 + bank_per * rep)
                nc.scalar.activation(dest[:, k, tok(t)], scaled[:, t, :, :], ACT.Copy).then_inc(hi_ready, 1)

            def x_highs(norm, b):
                for t in range(TT):
                    high_of_scaled(("x", norm, b, t), xT_hi, slice(BK * b, BK * (b + 1)), t)

            def high_of_group(name, dest, k, t, per=0, rep=0):
                n, b, _ = GROUP[name]
                act.wait_ge(t_ready, n + 1 + per * rep)
                nc.scalar.activation(dest[:, k, tok(t)], bank4(b), ACT.Copy).then_inc(hi_ready, 1)

            def copy_group(name, dest):
                n, b, _ = GROUP[name]
                act.wait_ge(t_ready, n + 1)
                src = tbank[b][:, :]
                if len(dest.shape) == 3:
                    src = src.rearrange("p (k n) -> p k n", n=dest.shape[2])
                nc.scalar.activation(dest, src, ACT.Copy).then_inc(t_read[b], 1)

            def x_squares(b):
                for t in range(TT):
                    link(nc.scalar.activation(junk[:, :], xs[:, t, blk(b)], ACT.Square,
                                              accum_out=sumsq[:, t, b:b + 1]))
                if b == NJ - 1:
                    nc.scalar.activation(junk[:, :], xs[:, 0, blk(b)], ACT.Copy).then_inc(sumsq_ready, 1)

            def norm_root(norm):
                act.wait_ge(meansq_ready, norm + 1)
                nc.scalar.activation(root[:, :], meansq[:, :], ACT.Sqrt).then_inc(root_ready, 1)

            def read_narrow(job, func, dest):
                pair = job_done(job, slots=SN)
                for t in range(TT):
                    ins = nc.scalar.activation(dest[:, t, :], pairs[pair][t][:, 0:HB], func, scale=rstd[:, t:t + 1])
                ins.then_inc(pair_read[pair], 1)

            def read_pair(job, func, dest, per=0, rep=0):
                pair = job_done(job, per, rep)
                for t in range(TT):
                    ins = nc.scalar.activation(dest[:, t, :], pairs[pair][t][:, :], func,
                                               scale=rstd[:, t:t + 1])
                ins.then_inc(pair_read[pair], 1)

            act.dma_start(tables[:, :], tables_in).then_inc(tables_loaded, 16)
            act.dma_start(cols[:, :], cols_in).then_inc(cols_loaded, 16)
            highs(0, 1)
            for b in range(NJ):
                x_highs(0, b)
                highs(max(2 * b, 1), 2 * b + 2)
                x_squares(b)
            norm_root(0)

            def read_by_other(job):
                _, pair, uses = JOB[job]
                act.wait_ge(pair_read[pair], uses + 1)

            def tap_products(a, b):
                for n in range(a, min(b, len(pool_taps))):
                    c, k = pool_taps[n]
                    u, w = uT[:, c, k:k + SEQ], col(DWW + c * TAPS + k)
                    if k == 0:
                        nc.scalar.activation(cv[:, c, :], u, ACT.Identity, bias=col(DWB + c),
                                             scale=w).then_inc(product_ready, 1)
                        continue
                    if starts_sum(c, k):
                        nc.scalar.activation(cv[:, c, :], u, ACT.Copy, scale=w).then_inc(product_ready, 1)
                        continue
                    if n >= PRODUCTS and pool_adds(n - PRODUCTS):
                        act.wait_ge(pool_tap_done, pool_adds(n - PRODUCTS))
                    nc.scalar.activation(products[:, n % PRODUCTS, :], u, ACT.Copy, scale=w).then_inc(product_ready, 1)

            def highs_and_taps(s_from, s_to):
                for s in range(s_from, s_to):
                    highs(s, s + 1)
                    tap_products(products_by(s - 1), products_by(s))

            def root_of(n):
                act.wait_ge(qk_ms_ready, n + 1)
                nc.scalar.activation(qk_r[n][:, :, :], qk_ms[n][:, :, :], ACT.Sqrt).then_inc(qk_root_ready, 1)

            def query_squares(g):
                part = q_tok[:, :, g * NB:(g + 1) * NB]
                _, pair, uses = JOB[f"q{g}"]
                act.wait_ge(pair_read[pair], uses + 1)
                nc.scalar.activation(q_sq, part, ACT.Square).then_inc(q_sq_ready, 1)

            def exps(hh):
                t = hh % 2
                keys = P if t == 0 else SEQ
                act.wait_ge(top_ready, hh + 1)
                for j in range(GQ):
                    s = scores[t][:, j, 0:keys]
                    nc.scalar.activation(s, s, ACT.Exp, bias=neg_top[:, t, j:j + 1], accum_out=den[:, t, j:j + 1])
                nc.scalar.activation(sink_e[:, t, :], sink_d[:, t, :], ACT.Exp).then_inc(p_ready, 1)

            def prob_copies(hh, r0, r1):
                for r in range(r0, r1):
                    n = P_BEFORE[hh] + r
                    if n >= 2:
                        act.wait_ge(pv_done, n - 1)
                    copy_group(("p", hh, r), probs[:, n % 2, :])

            def heads_highs(g):
                for t in range(TT):
                    high_of_group(("o", g, t), mT_hi, slice(KC + 4 * g, KC + 4 * g + 4), t)

            def query_copies(g):
                for t in range(TT):
                    copy_group(("qT", g, t), qT[:, 4 * g:4 * g + 4, tok(t)])

            highs(8, 11)
            act.wait_ge(rstd_ready, 1)
            read_pair("g0", ACT.Sigmoid, gated)
            kv0, q00, q10, z0 = (JOB[n][0] for n in ("kv", "q0", "q1", ("g1", 0)))
            ao0, co0 = JOB[("attn_out", 0, 0)][0], JOB[("conv_out", 0)][0]

            def u1_copy(h):
                c = BK + h * (BK // 2)
                copy_group(("u1", h), uT[:, c:c + BK // 2, PAD:PAD + SEQ])
                _, b, uses = GROUP[("u1", h)]
                act.wait_ge(t_read[b], uses + 1)

            highs(11, kv0 + 5)
            act.wait_ge(pad_ready, 1)
            for t in range(TT):
                copy_group(("u", 0, t), uT[:, 0:BK, PAD + t * P:PAD + (t + 1) * P])
            for t in range(TT):
                _, b, uses = GROUP[("u", 0, t)]
                act.wait_ge(t_read[b], uses + 1)
            highs_and_taps(kv0 + 5, q00 + 3)
            read_narrow("kv", ACT.Copy, kv_tok)
            highs_and_taps(q00 + 3, q00 + 5)
            root_of(0)
            highs_and_taps(q00 + 5, q10 + 1)
            copy_group("kT", kT[:, :, :].rearrange("p g n -> p (g n)"))
            highs_and_taps(q10 + 1, q10 + 3)
            read_pair("q0", ACT.Copy, q_tok[:, :, 0:NB])
            query_squares(0)
            highs_and_taps(q10 + 3, q10 + 5)
            root_of(1)
            highs_and_taps(q10 + 5, q10 + 8)
            query_copies(0)
            highs_and_taps(q10 + 8, z0 + 3)
            exps(0)
            read_pair("q1", ACT.Copy, q_tok[:, :, NB:2 * NB])
            query_squares(1)
            highs_and_taps(z0 + 3, z0 + 5)
            exps(1)
            prob_copies(0, 0, 2)
            highs_and_taps(z0 + 5, z0 + 6)
            root_of(2)
            highs_and_taps(z0 + 6, z0 + 7)
            read_by_other("a0")
            read_narrow(("g1", 0), ACT.Sigmoid, gated[:, :, 0:HB])
            highs_and_taps(z0 + 7, z0 + 8)
            prob_copies(1, 0, 2)
            highs_and_taps(z0 + 8, z0 + 9)
            prob_copies(1, 2, 4)
            highs_and_taps(z0 + 9, z0 + 10)
            query_copies(1)
            highs_and_taps(z0 + 10, z0 + 12)
            heads_highs(0)
            highs_and_taps(z0 + 12, z0 + 13)
            u1_copy(0)
            exps(2)
            highs_and_taps(z0 + 13, z0 + 15)
            exps(3)
            prob_copies(2, 0, 2)
            highs_and_taps(z0 + 15, z0 + 17)
            read_narrow(("g1", 1), ACT.Sigmoid, gated[:, :, HB:NB])
            highs_and_taps(z0 + 17, z0 + 18)
            prob_copies(3, 0, 2)
            highs_and_taps(z0 + 18, ao0 + 3)
            prob_copies(3, 2, 4)
            highs_and_taps(ao0 + 3, ao0 + 4)
            u1_copy(1)
            highs_and_taps(ao0 + 4, ao0 + 6)
            heads_highs(1)
            highs_and_taps(ao0 + 6, ao0 + 17)

            s0 = co0
            act.wait_ge(meansq_ready, 1)
            nc.scalar.activation(idle[:, :], meansq[:, :], ACT.Sqrt).then_inc(act_step, 1)
            for q in range(KC // 2):
                act.wait_ge(cv_centered, q + 1)
                nc.scalar.activation(ln_sq[:, 2 * q:2 * q + 2, :], cv[:, 2 * q:2 * q + 2, :],
                                     ACT.Square).then_inc(ln_sq_ready, 1)
            highs(ao0 + 17, ao0 + 19)
            act.wait_ge(ln_v_ready, 1)
            nc.scalar.activation(ln_r[:, :], ln_v[:, :], ACT.Sqrt).then_inc(ln_root_ready, 1)
            steps[0] += 1
            act.wait_ge(act_step, steps[0])
            link(nc.scalar.activation(idle[:, :], meansq[:, :], ACT.Silu))
            highs(ao0 + 19, ao0 + 20)
            for q in range(KC // 2):
                act.wait_ge(ln_scaled, q + 1)
                for c in range(2 * q, 2 * q + 2):
                    ins = nc.scalar.activation(cv[:, c, :], cv[:, c, :], ACT.Silu,
                                               bias=col(LNB + c), scale=col(LNG + c))
                ins.then_inc(silu_done, 1)
                act.wait_ge(silu_done, q + 1)
                nc.scalar.activation(mT_hi[:, 2 * q:2 * q + 2, :], cv[:, 2 * q:2 * q + 2, :],
                                     ACT.Copy).then_inc(hi_ready, 1)
            at = s0 + 4
            for nb in range(1, NJ):
                after = s0 + SH * nb + 2
                highs(at, after + 3)
                at = after + 3
                x_highs(1, nb - 1)
                x_squares(nb - 1)

            def first_block(s0, at, norm):
                highs(at, s0 + 7)
                x_highs(norm, NJ - 1)
                x_squares(NJ - 1)
                norm_root(norm)
                highs(s0 + 7, s0 + SD + 3)
                act.wait_ge(rstd_ready, norm + 1)

            def ffn(layer, norm, at, norm_after):
                s0 = JOB[("gate", layer, 0)][0]
                first_block(s0, at, norm)
                read_pair(("gate", layer, 0), ACT.Silu, gated)
                highs(s0 + SD + 3, s0 + 2 * SD + 4)
                with act.Fori(1, NF) as i:
                    highs(s0 + 4, s0 + 7, 2 * SD, i)
                    for t in range(TT):
                        high_of_group(("y", layer, 0, t), yT_hi, ds(BK * (i - 1), BK), t, TT, i - 1)
                    highs(s0 + 7, s0 + SD + 3, 2 * SD, i)
                    act.wait_ge(pair_read[1], JOB[("up", layer, 0)][2] + i)
                    read_pair(("gate", layer, 0), ACT.Silu, gated, 2 * SD, i)
                    highs(s0 + SD + 3, s0 + 2 * SD + 4, 2 * SD, i)
                at = s0 + 2 * SD * NF + 4
                for nb in range(NJ):
                    after = JOB[("down", layer, nb)][0] + 4
                    highs(at, after + 3)
                    at = after + 3
                    if nb == 0:
                        for t in range(TT):
                            high_of_group(("y", layer, NF - 1, t), yT_hi, slice(KF - BK, KF), t)
                    elif norm_after is not None:
                        x_highs(norm_after, nb - 1)
                        x_squares(nb - 1)
                return at

            at = ffn(0, 1, at, 2)

            s0 = JOB[("cg", 0)][0]

            def mixer_block(rep, from_c):
                per = 3 * SD
                if from_c:
                    act.wait_ge(pair_read[1], JOB[("cu", 0)][2] + rep)
                read_pair(("cg", 0), ACT.Copy, gated, per, rep)
                highs(s0 + SD + 3, s0 + 2 * SD + 7, per, rep)
                if from_c:
                    act.wait_ge(c3_done, 3 * BK * rep)
                for t in range(TT):
                    n, b, _ = GROUP[("c", 0, t)]
                    act.wait_ge(t_ready, n + 1 + 2 * TT * rep)
                    nc.scalar.activation(cT[:, :, 2 + t * P:2 + (t + 1) * P], bank4(b),
                                         ACT.Copy).then_inc(t_read[b], 1)
                highs(s0 + 2 * SD + 7, s0 + 3 * SD + 3, per, rep)
                pair = JOB[("bg", 0)][1]
                act.wait_ge(w_used, s0 + 3 * SD + per * rep)
                for t in range(TT):
                    ins = nc.scalar.activation(bg_tok[:, t, :], pairs[pair][t][:, :], ACT.Copy,
                                               scale=rstd[:, t:t + 1])
                ins.then_inc(pair_read[pair], 1)
                highs(s0 + 3 * SD + 3, s0 + 3 * SD + 4, per, rep)

            first_block(s0, at, 2)
            mixer_block(0, False)
            with act.Fori(1, NJ) as j:
                highs(s0 + 4, s0 + 7, 3 * SD, j)
                for t in range(TT):
                    high_of_scaled(("z", 0, t), zT_hi, ds(BK * (j - 1), BK), t, rep=j - 1, bank_per=2)
                highs(s0 + 7, s0 + SD + 3, 3 * SD, j)
                mixer_block(j, True)
            at = s0 + 3 * SD * NJ + 4
            for nb in range(NJ):
                after = JOB[("sc_out", nb)][0] + 4
                highs(at, after + 3)
                at = after + 3
                if nb == 0:
                    for t in range(TT):
                        high_of_scaled(("z", NJ - 1, t), zT_hi, slice(KD - BK, KD), t)
                else:
                    x_highs(3, nb - 1)
                    x_squares(nb - 1)
            at = ffn(1, 3, at, None)
            highs(at, SLOTS)

        @block.vector
        def _(dve):
            steps = [0]

            def link(ins):
                steps[0] += 1
                ins.then_inc(dve_step, 1)
                dve.wait_ge(dve_step, steps[0])

            def lows(s_from, s_to, per=0, rep=0):
                for s in range(s_from + s_from % 2, min(s_to, SLOTS), 2):
                    r = s % RING
                    dve.wait_ge(w_hi_ready, s + 1 + per * rep)
                    nc.vector.tensor_tensor(w_lo[:, r, :, :], w_raw[:, r, :, :],
                                            w_hi[:, r, :, :].bitcast(F32), ALU.subtract).then_inc(w_lo_even, 1)

            def gain(norm, b):
                base = (MIXG if norm % 2 == 0 else FFNG) + (norm // 2) * KD
                return col(base + BK * b, BK).unsqueeze(2).to_broadcast([P, BK, P])

            def x_split(norm, b):
                for t in range(TT):
                    n, bank, _ = GROUP[("x", norm, b, t)]
                    dve.wait_ge(t_ready, n + 1)
                    if LOW[("x", norm, b, t)] >= TT:
                        dve.wait_ge(lo_ready, LOW[("x", norm, b, t)] - TT + 1)
                    nc.vector.tensor_tensor(scaled[:, t, :, :], bank4(bank), gain(norm, b),
                                            ALU.mult).then_inc(t_read[bank], 1)
                for t in range(TT):
                    k = slice(BK * b, BK * (b + 1))
                    dve.wait_ge(hi_ready, HIGH[("x", norm, b, t)] + 1)
                    nc.vector.tensor_tensor(xT_lo[:, k, tok(t)], scaled[:, t, :, :],
                                            xT_hi[:, k, tok(t)].bitcast(F32), ALU.subtract).then_inc(lo_ready, 1)

            def low_of_group(name, hi, lo, k, t, per=0, rep=0, bank_per=0):
                _, b, _ = GROUP[name]
                dve.wait_ge(hi_ready, HIGH[name] + 1 + per * rep)
                nc.vector.tensor_tensor(lo[:, k, tok(t)], bank4(b), hi[:, k, tok(t)].bitcast(F32),
                                        ALU.subtract).then_inc(t_read[b], 1)

            def newton_root(value, r, tmp):
                link(nc.vector.reciprocal(r, r))
                link(nc.vector.tensor_tensor(tmp, r, r, ALU.mult))
                link(nc.vector.scalar_tensor_tensor(tmp, tmp, -0.5, value, ALU.mult, ALU.mult))

            def newton_step(dest, r, tmp):
                return nc.vector.scalar_tensor_tensor(dest, tmp, 1.5, r, ALU.add, ALU.mult)

            def norm_stats(norm):
                dve.wait_ge(sumsq_ready, norm + 1)
                link(nc.vector.reduce_sum(meansq[:, :], sumsq[:, :, :], AX_X))
                nc.vector.tensor_scalar(meansq[:, :], meansq[:, :], 1.0 / D, RMS_EPS, ALU.mult,
                                        ALU.add).then_inc(meansq_ready, 1)
                dve.wait_ge(root_ready, norm + 1)
                newton_root(meansq[:, :], root[:, :], newton[:, :])
                newton_step(rstd[:, :], root[:, :], newton[:, :]).then_inc(rstd_ready, 1)
                dve.wait_ge(rstd_ready, norm + 1)

            def multiply_pair(job, per=0, rep=0, bank_per=0):
                s0, pair, _ = JOB[job]
                dve.wait_ge(w_used, s0 + SD + per * rep)
                for t in range(TT):
                    ins = nc.vector.scalar_tensor_tensor(mixed[:, t, :], pairs[pair][t][:, :], rstd[:, t:t + 1],
                                                         gated[:, t, :], ALU.mult, ALU.mult)
                ins.then_inc(pair_read[pair], 1)

            def multiply_narrow(h):
                s0, pair, _ = JOB[("a1", h)]
                dve.wait_ge(w_used, s0 + SN)
                c = slice(h * HB, (h + 1) * HB)
                for t in range(TT):
                    ins = nc.vector.scalar_tensor_tensor(mixed[:, t, c], pairs[pair][t][:, 0:HB], rstd[:, t:t + 1],
                                                         gated[:, t, c], ALU.mult, ALU.mult)
                ins.then_inc(pair_read[pair], 1)

            def add_pair(job, nb, slots):
                s0, pair, _ = JOB[job]
                dve.wait_ge(w_used, s0 + slots)
                for t in range(TT):
                    ins = nc.vector.tensor_tensor(xs[:, t, blk(nb)], pairs[pair][t][:, :], xs[:, t, blk(nb)], ALU.add)
                ins.then_inc(pair_read[pair], 1)

            before = {step: n for n, step in enumerate(dve_taps)}

            def conv_taps(a, b):
                b = min(b, len(dve_taps))
                for n in range(a, b):
                    c, k = dve_taps[n]
                    place = acc_place[c]
                    acc = conv_acc[:, place * SEQ:(place + 1) * SEQ]
                    if k == TAPS:
                        dve.wait_ge(tap_done, before[(c, SHARE - 1)] + 1)
                        dve.wait_ge(pool_tap_done, pool_adds(len(pool_taps) - 1))
                        nc.vector.tensor_tensor(cv[:, c, :], acc, cv[:, c, :], ALU.add).then_inc(tap_done, 1)
                        continue
                    w = col(DWW + c * TAPS + k)
                    u = uT[:, c, k:k + SEQ]
                    if k == 0:
                        if n >= 2:
                            dve.wait_ge(tap_done, n)
                        nc.vector.tensor_scalar(acc, u, w, col(DWB + c), ALU.mult, ALU.add).then_inc(tap_done, 1)
                    else:
                        dve.wait_ge(tap_done, before[(c, k - 1)] + 1)
                        dest = cv[:, c, :] if k == TAPS - 1 else acc
                        nc.vector.scalar_tensor_tensor(dest, u, w, acc, ALU.mult, ALU.add).then_inc(tap_done, 1)
                return b

            link(nc.vector.memset(uT[:, :, 0:PAD], 0.0))
            nc.vector.memset(junk[:, 0:2], 0.0).then_inc(pad_ready, 1)
            dve.wait_ge(cols_loaded, 16)
            lows(0, 1)
            for b in range(NJ):
                x_split(0, b)
                lows(max(2 * b, 1), 2 * b + 1)
            norm_stats(0)

            def read_by_other(job):
                _, pair, uses = JOB[job]
                dve.wait_ge(pair_read[pair], uses + 1)

            def heads_of(x):
                return x.rearrange("p (h d) -> p h d", d=HD)

            def inverse_roots(n):
                ms, r, tmp = (x[n][:, :, :] for x in (qk_ms, qk_r, qk_t))
                dve.wait_ge(qk_root_ready, n + 1)
                newton_root(ms, r, tmp)
                link(newton_step(r, r, tmp))

            def mean_squares(n):
                ms = qk_ms[n][:, :, :]
                nc.vector.tensor_scalar(ms, ms, 1.0 / HD, RMS_EPS, ALU.mult, ALU.add).then_inc(qk_ms_ready, 1)

            keys = kv_tok[:, :, 0:KVW].rearrange("p t (h d) -> p t h d", d=HD)

            def key_sums():
                read_by_other("kv")
                sq = k_twice[:, :, :, 0, :]
                link(nc.vector.tensor_tensor(sq, keys, keys, ALU.mult))
                link(nc.vector.reduce_sum(qk_ms[0][:, :, :], sq, AX_X))
                link(nc.vector.tensor_scalar(k_gain[:, :], col(KG, HD), HD ** -0.5, None, ALU.mult))
                link(nc.vector.tensor_tensor(k_gain[:, :], k_gain[:, :], col(QG, HD), ALU.mult))
                mean_squares(0)

            def key_norms():
                inverse_roots(0)
                for t in range(TT):
                    ins = nc.vector.tensor_tensor(keys[:, t, :, :], keys[:, t, :, :],
                                                  qk_r[0][:, t, :].unsqueeze(2).to_broadcast([P, HKV, HD]), ALU.mult)
                link(ins)
                for t in range(TT):
                    for w in range(2):
                        ins = nc.vector.tensor_tensor(k_twice[:, t, :, w, :], keys[:, t, :, :],
                                                      k_gain[:, :].unsqueeze(1).to_broadcast([P, HKV, HD]), ALU.mult)
                ins.then_inc(qk_normed, 1)

            def query_sums(g):
                dve.wait_ge(q_sq_ready, g + 1)
                for t in range(TT):
                    ins = nc.vector.reduce_sum(qk_ms[1 + g][:, t, :], heads_of(q_sq[:, t, :]), AX_X)
                link(ins)
                mean_squares(1 + g)

            def query_norms(g):
                inverse_roots(1 + g)
                for t in range(TT):
                    q3 = heads_of(q_tok[:, t, g * NB:(g + 1) * NB])
                    ins = nc.vector.tensor_tensor(q3, q3, qk_r[1 + g][:, t, :].unsqueeze(2).to_broadcast([P, GQ, HD]),
                                                  ALU.mult)
                ins.then_inc(qk_normed, 1)

            def score_rows(hh):
                g, t = hh // 2, hh % 2
                keys = P if t == 0 else SEQ
                if hh >= 2:
                    dve.wait_ge(t_ready, GROUP[("p", hh - 2, P_GROUPS[hh - 2] - 1)][0] + 1)
                for r in range(4):
                    n, b, _ = GROUP[("sc", hh, r)]
                    dve.wait_ge(t_ready, n + 1)
                    for m in range(2):
                        j = 2 * (2 * (r // 2) + m) + r % 2
                        slope = 2.0 ** (-8.0 * (g * GQ + j + 1) / HQ)
                        ins = nc.vector.scalar_tensor_tensor(scores[t][:, j, 0:keys], dist[t], -slope,
                                                             tbank[b][:, m * SEQ:m * SEQ + keys], ALU.mult, ALU.add)
                    ins.then_inc(t_read[b], 1)
                for r in range(2, 4):
                    _, b, uses = GROUP[("sc", hh, r)]
                    dve.wait_ge(t_read[b], uses + 1)
                sink = col(SINK + g * GQ, GQ)
                link(nc.vector.reduce_max(top[:, t, :], scores[t][:, :, 0:keys], AX_X))
                link(nc.vector.tensor_tensor(top[:, t, :], top[:, t, :], sink, ALU.max))
                link(nc.vector.tensor_scalar(neg_top[:, t, :], top[:, t, :], -1.0, None, ALU.mult))
                nc.vector.tensor_tensor(sink_d[:, t, :], sink, neg_top[:, t, :], ALU.add).then_inc(top_ready, 1)

            def heads_out(hh):
                g, t = hh // 2, hh % 2
                dve.wait_ge(p_ready, hh + 1)
                link(nc.vector.tensor_tensor(rden[:, t, :], den[:, t, :], sink_e[:, t, :], ALU.add))
                link(nc.vector.reciprocal(rden[:, t, :], rden[:, t, :]))
                dve.wait_ge(pv_done, P_BEFORE[hh] + P_GROUPS[hh])
                nc.vector.tensor_tensor(heads_of(q_tok[:, t, g * NB:(g + 1) * NB]), heads_of(heads_acc[:, :]),
                                        rden[:, t, :].unsqueeze(2).to_broadcast([P, GQ, HD]),
                                        ALU.mult).then_inc(o_ready, 1)

            def heads_lows(g):
                for t in range(TT):
                    low_of_group(("o", g, t), mT_hi, mT_lo, slice(KC + 4 * g, KC + 4 * g + 4), t)

            def lows_and_taps(s_from, s_to, taps, each, end):
                for s in range(s_from + s_from % 2, s_to, 2):
                    lows(s, s + 1)
                    taps = conv_taps(taps, min(taps + each, end))
                return taps

            kv0, q00, q10, z0 = (JOB[n][0] for n in ("kv", "q0", "q1", ("g1", 0)))
            ao0 = JOB[("attn_out", 0, 0)][0]

            def u_copied(*names):
                for name in names:
                    _, b, uses = GROUP[name]
                    dve.wait_ge(t_read[b], uses + 1)

            lows(8, kv0 + 4)
            read_by_other("g0")
            multiply_pair("a0")
            lows(kv0 + 4, kv0 + 6)
            u_copied(("u", 0, 0), ("u", 0, 1))
            taps = lows_and_taps(kv0 + 6, q00 + 4, 0, 4, U0_TAPS)
            key_sums()
            taps = lows_and_taps(q00 + 4, q00 + 6, taps, 6, U0_TAPS)
            key_norms()
            taps = lows_and_taps(q00 + 6, q10 + 4, taps, 7, U0_TAPS)
            query_sums(0)
            taps = lows_and_taps(q10 + 4, q10 + 6, taps, 2, U0_TAPS)
            query_norms(0)
            taps = lows_and_taps(q10 + 6, q10 + 10, taps, 6, U0_TAPS)
            score_rows(0)
            taps = lows_and_taps(q10 + 10, q10 + 12, taps, 3, U0_TAPS)
            score_rows(1)
            query_sums(1)
            taps = lows_and_taps(z0 + 4, z0 + 8, taps, 4, U0_TAPS)
            heads_out(0)
            query_norms(1)
            taps = lows_and_taps(z0 + 8, z0 + 11, taps, 4, U0_TAPS)
            heads_out(1)
            read_by_other(("g1", 0))
            multiply_narrow(0)
            taps = lows_and_taps(z0 + 11, z0 + 12, taps, 4, U0_TAPS)
            score_rows(2)
            taps = lows_and_taps(z0 + 12, z0 + 13, taps, 4, U0_TAPS)
            heads_lows(0)
            score_rows(3)
            conv_taps(taps, U0_TAPS)
            u_copied(("u1", 0))
            taps = lows_and_taps(z0 + 13, z0 + 17, U0_TAPS, 8, U1_TAPS)
            heads_out(2)
            taps = lows_and_taps(z0 + 17, ao0 + 3, taps, 8, U1_TAPS)
            multiply_narrow(1)
            taps = lows_and_taps(ao0 + 3, ao0 + 5, taps, 7, U1_TAPS)
            heads_out(3)
            conv_taps(taps, U1_TAPS)
            u_copied(("u1", 1))
            taps = lows_and_taps(ao0 + 5, ao0 + 7, U1_TAPS, 0, ALL_TAPS)
            heads_lows(1)
            taps = conv_taps(taps, taps + 10)
            taps = lows_and_taps(ao0 + 7, ao0 + 10, taps, 10, ALL_TAPS)
            add_pair(("attn_out", 1, 0), 0, 2)
            taps = lows_and_taps(ao0 + 10, ao0 + 12, taps, 10, ALL_TAPS)
            add_pair(("attn_out", 1, 1), 1, 2)
            taps = lows_and_taps(ao0 + 12, ao0 + 16, taps, 11, ALL_TAPS)
            add_pair(("attn_out", 1, 2), 2, 2)
            conv_taps(taps, ALL_TAPS)
            lows(ao0 + 16, ao0 + 18)

            n, b, _ = GROUP["mean"]
            dve.wait_ge(tap_done, len(dve_taps))
            dve.wait_ge(pool_tap_done, pool_adds(len(pool_taps) - 1))
            dve.wait_ge(t_ready, n + 1)
            for q in range(KC // 2):
                part = cv[:, 2 * q:2 * q + 2, :]
                nc.vector.tensor_tensor(part, part, tbank[b][:, 0:SEQ].unsqueeze(1).to_broadcast([P, 2, SEQ]),
                                        ALU.subtract).then_inc(cv_centered, 1)
            lows(ao0 + 18, ao0 + 20)
            dve.wait_ge(cv_centered, KC // 2)
            nc.vector.memset(junk[:, 0:2], 0.0).then_inc(t_read[b], 1)
            n, b2, _ = GROUP["var"]
            dve.wait_ge(t_ready, n + 1)
            nc.vector.tensor_scalar(ln_v[:, :], tbank[b2][:, 0:SEQ], LN_EPS, None, ALU.add).then_inc(t_read[b2], 1)
            dve.wait_ge(t_read[b2], GROUP["var"][2] + 1)
            nc.vector.memset(junk[:, 2:4], 0.0).then_inc(ln_v_ready, 1)
            dve.wait_ge(ln_root_ready, 1)
            newton_root(ln_v[:, :], ln_r[:, :], ln_t[:, :])
            link(newton_step(ln_r[:, :], ln_r[:, :], ln_t[:, :]))
            for q in range(KC // 2):
                part = cv[:, 2 * q:2 * q + 2, :]
                nc.vector.tensor_tensor(part, part, ln_r[:, :].unsqueeze(1).to_broadcast([P, 2, SEQ]),
                                        ALU.mult).then_inc(ln_scaled, 1)
            add_pair(("attn_out", 1, 3), 3, 2)
            for q in range(KC // 2):
                dve.wait_ge(hi_ready, HIGH[("ln", q)] + 1)
                nc.vector.tensor_tensor(mT_lo[:, 2 * q:2 * q + 2, :], cv[:, 2 * q:2 * q + 2, :],
                                        mT_hi[:, 2 * q:2 * q + 2, :].bitcast(F32), ALU.subtract).then_inc(lo_ready, 1)

            s0 = JOB[("conv_out", 0)][0]
            at = s0 + 4
            for nb in range(NJ):
                done = s0 + SH * (nb + 1)
                lows(at, done + 3)
                add_pair(("conv_out", nb), nb, SH)
                at = done + 3
                if nb < NJ - 1:
                    lows(at, done + 5)
                    at = done + 5
                    x_split(1, nb)

            def first_block(s0, at, norm):
                lows(at, s0 + 7)
                x_split(norm, NJ - 1)
                norm_stats(norm)
                return s0 + 7

            def ffn(layer, norm, at, norm_after):
                s0 = JOB[("gate", layer, 0)][0]
                at = first_block(s0, at, norm)
                lows(at, s0 + 2 * SD + 3)
                dve.wait_ge(pair_read[0], JOB[("gate", layer, 0)][2] + 1)
                multiply_pair(("up", layer, 0))
                with dve.Fori(1, NF) as i:
                    lows(s0 + 4, s0 + 7, 2 * SD, i)
                    for t in range(TT):
                        low_of_group(("y", layer, 0, t), yT_hi, yT_lo, ds(BK * (i - 1), BK), t, TT, i - 1)
                    lows(s0 + 8, s0 + 2 * SD + 3, 2 * SD, i)
                    dve.wait_ge(pair_read[0], JOB[("gate", layer, 0)][2] + 1 + i)
                    multiply_pair(("up", layer, 0), 2 * SD, i)
                at = s0 + 2 * SD * NF + 4
                for nb in range(NJ):
                    d0 = JOB[("down", layer, nb)][0]
                    lows(at, d0 + 7)
                    at = d0 + 8
                    if nb == 0:
                        for t in range(TT):
                            low_of_group(("y", layer, NF - 1, t), yT_hi, yT_lo, slice(KF - BK, KF), t)
                    elif norm_after is not None:
                        x_split(norm_after, nb - 1)
                    lows(at, d0 + SF + 3)
                    at = d0 + SF + 3
                    add_pair(("down", layer, nb), nb, SF)
                return at

            at = ffn(0, 1, at, 2)

            s0 = JOB[("cg", 0)][0]
            at = first_block(s0, at, 2)
            nc.vector.memset(cT[:, :, 0:2], 0.0)

            def gate_block(j, rep, k):
                for t in range(TT):
                    n, b, _ = GROUP[("z", j, t)]
                    dve.wait_ge(t_ready, n + 1 + 2 * TT * rep)
                    nc.vector.tensor_tensor(scaled[:, t, :, :], bank4(b), zc[:, :, tok(t)],
                                            ALU.mult).then_inc(t_read[b], 1)
                for t in range(TT):
                    dve.wait_ge(hi_ready, HIGH[("z", j, t)] + 1 + TT * rep)
                    nc.vector.tensor_tensor(zT_lo[:, k, tok(t)], scaled[:, t, :, :],
                                            zT_hi[:, k, tok(t)].bitcast(F32), ALU.subtract).then_inc(lo_ready, 1)

            def mixer_block(rep):
                per = 3 * SD
                dve.wait_ge(pair_read[0], JOB[("cg", 0)][2] + 1 + rep)
                multiply_pair(("cu", 0), per, rep)
                lows(s0 + 2 * SD + 4, s0 + 2 * SD + 7, per, rep)
                for t in range(TT):
                    _, b, uses = GROUP[("c", 0, t)]
                    dve.wait_ge(t_read[b], uses + 1 + 2 * rep)
                for tap in range(3):
                    for k in range(BK):
                        w = cols[:, ds(SCW + k * 3 + tap + 3 * BK * rep, 1)]
                        src = cT[:, k, tap:tap + SEQ]
                        if tap:
                            dve.wait_ge(c3_done, BK * (tap - 1) + k + 1 + 3 * BK * rep)
                            ins = nc.vector.scalar_tensor_tensor(zc[:, k, :], src, w, zc[:, k, :], ALU.mult, ALU.add)
                        else:
                            ins = nc.vector.tensor_scalar(zc[:, k, :], src, w, None, ALU.mult)
                        ins.then_inc(c3_done, 1)
                lows(s0 + 2 * SD + 8, s0 + 3 * SD + 4, per, rep)

            lows(at, s0 + 2 * SD + 3)
            mixer_block(0)
            with dve.Fori(1, NJ) as j:
                lows(s0 + 4, s0 + 7, 3 * SD, j)
                dve.wait_ge(c3_done, 3 * BK * j)
                gate_block(0, j - 1, ds(BK * (j - 1), BK))
                lows(s0 + 8, s0 + 2 * SD + 3, 3 * SD, j)
                mixer_block(j)
            at = s0 + 3 * SD * NJ + 4
            for nb in range(NJ):
                o0 = JOB[("sc_out", nb)][0]
                lows(at, o0 + 7)
                at = o0 + 8
                if nb == 0:
                    dve.wait_ge(c3_done, 3 * BK * NJ)
                    gate_block(NJ - 1, 0, slice(KD - BK, KD))
                else:
                    x_split(3, nb - 1)
                lows(at, o0 + SD + 3)
                at = o0 + SD + 3
                add_pair(("sc_out", nb), nb, SD)
            ffn(1, 3, at, None)


def _columns(np, v):
    def feature_major(a):
        a = np.asarray(a)
        lead, feats = a.shape[:-1], a.shape[-1]
        return a.reshape(-1, feats // 128, 128)

    def plain(a):
        a = feature_major(a)
        return a.transpose(2, 0, 1).reshape(128, -1)

    def taps(a):
        a = feature_major(a)
        return a.transpose(2, 1, 0).reshape(128, -1)

    def shared(a):
        return np.broadcast_to(np.asarray(a).reshape(1, -1), (128, np.asarray(a).size))

    return np.ascontiguousarray(np.concatenate([
        plain(v["mix_norm_g"]), plain(v["ffn_norm_g"]), taps(v["conv_dw_w"][0]), plain(v["conv_dw_b"]),
        plain(v["conv_ln_g"]), plain(v["conv_ln_b"]), taps(v["sc_conv_w"][0]),
        shared(v["q_norm_g"]), shared(v["k_norm_g"]), shared(v["attn_sinks"])], axis=1))


def _tables(np):
    chunk, far = 64, 1e33
    parts = [np.eye(128)]
    for q0, keys in ((0, 128), (128, 256)):
        q, k = np.arange(q0, q0 + 128)[:, None], np.arange(keys)[None, :]
        seen = (k // chunk == q // chunk) | (k // chunk == q // chunk - 1)
        parts.append(np.where(seen, np.abs(q - k), far))
    return np.concatenate(parts, axis=1).astype(np.float32)


def kernel(**inputs):
    import numpy as np
    import concourse.bacc as bacc
    from concourse import mybir as mb
    from concourse.bass_utils import run_bass_kernel_spmd

    v = {name: np.asarray(a) for name, a in inputs.items()}
    arrays = {
        "x": v["x"][0], "w_in": v["hy_w_in"][0], "w_out": v["hy_w_out"][0], "sc_in": v["sc_w_in"][0],
        "sc_out": v["sc_w_out"][0], "w_gate": v["ffn_w_gate"], "w_up": v["ffn_w_up"],
        "w_down": v["ffn_w_down"], "cols": _columns(np, v), "tables": _tables(np),
    }
    arrays = {f"in_{name}": np.ascontiguousarray(a) for name, a in arrays.items()}
    nc = bacc.Bacc("TRN2", target_bir_lowering=False, num_devices=1)
    args = [nc.dram_tensor(name, a.shape, mb.dt.from_np(a.dtype), kind="ExternalInput").ap()
            for name, a in arrays.items()]
    shape = v["x"].shape
    out = nc.dram_tensor("out_y", shape[1:], mb.dt.float32, kind="ExternalOutput").ap()
    encoder_kernel(nc, *args, out)
    result = run_bass_kernel_spmd(nc, [arrays], core_ids=[0])
    return result.results[0]["out_y"].reshape(shape)
```
